# Optimizing a Trainium2 kernel written in Bass

```python
import jax
import jax.numpy as jnp
from jax import lax
import numpy as np

D_MODEL = 1024
BATCH = 1
SEQ = 1024
DEPTH = 1
DEC_BATCH = 1
DEC_SEQ = 64
PAST_LEN = 256

CHUNK = 64
HEAD_DIM = 64
N_FOX_HEADS = 8
N_SWA_HEADS = 8
N_SWA_KV = 2
SWA_GROUP = N_SWA_HEADS // N_SWA_KV
WINDOW = 128
WIN_CHUNKS = WINDOW // CHUNK
Q_BLOCK = 128
FOX_W = N_FOX_HEADS * HEAD_DIM
SWA_QW = N_SWA_HEADS * HEAD_DIM
SWA_KVW = N_SWA_KV * HEAD_DIM
MIX_W = FOX_W + SWA_QW
PROJ_W = 3 * FOX_W + N_FOX_HEADS + SWA_QW + 2 * SWA_KVW
N_GROUPS = 4
EXPERTS_PER_GROUP = 8
N_EXPERTS = N_GROUPS * EXPERTS_PER_GROUP
TOP_K = 2
D_EXPERT = 128
FORGET_BIAS = 4.0
EPS = 1e-6
SCALE = HEAD_DIM ** -0.5
F32 = jnp.float32

kernel_name = 'hybrid_fox_swa_hmoe_stream_step'

def rmsnorm(x, g):
    xf = x.astype(F32)
    y = xf * lax.rsqrt(jnp.mean(xf * xf, axis=-1, keepdims=True) + EPS)
    return y.astype(x.dtype) * g

def alibi_slopes(n):
    return jnp.asarray(2.0 ** (-8.0 * (np.arange(n, dtype=np.float32) + 1.0) / n), dtype=F32)

def project(x, g_norm, w_in, b_forget):
    b, s = x.shape[0], x.shape[1]
    h = rmsnorm(x, g_norm)
    p = jnp.einsum('bsd,dp->bsp', h, w_in)
    cuts = np.cumsum([FOX_W, FOX_W, FOX_W, N_FOX_HEADS, SWA_QW, SWA_KVW]).tolist()
    q_a, k_a, v_a, f_a, q_b, k_b, v_b = jnp.split(p, cuts, axis=-1)
    logf = jax.nn.log_sigmoid(f_a.astype(F32) + b_forget.astype(F32))
    return (q_a.reshape(b, s, N_FOX_HEADS, HEAD_DIM),
            k_a.reshape(b, s, N_FOX_HEADS, HEAD_DIM),
            v_a.reshape(b, s, N_FOX_HEADS, HEAD_DIM),
            logf,
            q_b.reshape(b, s, N_SWA_HEADS, HEAD_DIM),
            k_b.reshape(b, s, N_SWA_KV, HEAD_DIM),
            v_b.reshape(b, s, N_SWA_KV, HEAD_DIM))

def fox_prompt(q, k, v, logf):
    b, s, h, dh = q.shape
    nb = s // Q_BLOCK
    c_k = jnp.cumsum(logf, axis=1).transpose(0, 2, 1)
    qb = q.reshape(b, nb, Q_BLOCK, h, dh).transpose(1, 0, 2, 3, 4)
    cb = c_k.reshape(b, h, nb, Q_BLOCK).transpose(2, 0, 1, 3)
    kpos = jnp.arange(s)

    def block(args):
        qi, ci, i = args
        qpos = i * Q_BLOCK + jnp.arange(Q_BLOCK)
        sc = (jnp.einsum('bqhd,bkhd->bhqk', qi, k, preferred_element_type=F32) * SCALE
              + ci[..., None] - c_k[:, :, None, :])
        sc = jnp.where(kpos[None, :] <= qpos[:, None], sc, -jnp.inf)
        pr = jax.nn.softmax(sc, axis=-1)
        return jnp.einsum('bhqk,bkhd->bqhd', pr.astype(v.dtype), v)

    o = lax.map(block, (qb, cb, jnp.arange(nb)))
    return o.transpose(1, 0, 2, 3, 4).reshape(b, s, h, dh)

def fox_sample(q, k_new, v_new, logf_new, cache_k, cache_v, cache_logf):
    t = q.shape[1]
    p_len = cache_k.shape[1]
    k = jnp.concatenate([cache_k, k_new], axis=1)
    v = jnp.concatenate([cache_v, v_new], axis=1)
    c_k = jnp.cumsum(jnp.concatenate([cache_logf.astype(F32), logf_new], axis=1), axis=1).transpose(0, 2, 1)
    c_q = c_k[:, :, p_len:]
    sc = (jnp.einsum('bqhd,bkhd->bhqk', q, k, preferred_element_type=F32) * SCALE
          + c_q[..., None] - c_k[:, :, None, :])
    mask = jnp.arange(p_len + t)[None, :] <= (p_len + jnp.arange(t))[:, None]
    sc = jnp.where(mask, sc, -jnp.inf)
    pr = jax.nn.softmax(sc, axis=-1)
    return jnp.einsum('bhqk,bkhd->bqhd', pr.astype(v.dtype), v)

def sink_attention(q, k, v, bias, sinks):
    sc = jnp.einsum('...qhgd,...shd->...hgqs', q, k, preferred_element_type=F32) * SCALE + bias
    sink = sinks.astype(F32).reshape(N_SWA_KV, SWA_GROUP)[:, :, None]
    m = jnp.maximum(jnp.max(sc, axis=-1), sink)
    e = jnp.exp(sc - m[..., None])
    pr = e / (jnp.sum(e, axis=-1, keepdims=True) + jnp.exp(sink - m)[..., None])
    return jnp.einsum('...hgqs,...shd->...qhgd', pr.astype(v.dtype), v)

def swa_prompt(q, k, v, sinks):
    b, s = q.shape[0], q.shape[1]
    nc = s // CHUNK
    span = (WIN_CHUNKS + 1) * CHUNK
    qc = q.reshape(b, nc, CHUNK, N_SWA_KV, SWA_GROUP, HEAD_DIM)

    def windows(x):
        xc = x.reshape(b, nc, CHUNK, N_SWA_KV, HEAD_DIM)
        xp = jnp.pad(xc, ((0, 0), (WIN_CHUNKS, 0), (0, 0), (0, 0), (0, 0)))
        return jnp.concatenate([xp[:, j:j + nc] for j in range(WIN_CHUNKS + 1)], axis=2)

    kw, vw = windows(k), windows(v)
    qi = jnp.arange(CHUNK)
    kj = jnp.arange(span)
    dist = jnp.abs(qi[:, None] - (kj[None, :] - WIN_CHUNKS * CHUNK)).astype(F32)
    alibi = -alibi_slopes(N_SWA_HEADS).reshape(N_SWA_KV, SWA_GROUP, 1, 1) * dist
    valid = (jnp.arange(nc)[:, None] + kj[None, :] // CHUNK) >= WIN_CHUNKS
    bias = jnp.where(valid[:, None, None, None, :], alibi, -jnp.inf)
    o = sink_attention(qc, kw, vw, bias, sinks)
    return o.reshape(b, s, N_SWA_HEADS, HEAD_DIM)

def swa_sample(q, k_new, v_new, cache_k, cache_v, sinks):
    b, t = q.shape[0], q.shape[1]
    w = cache_k.shape[1]
    k = jnp.concatenate([cache_k, k_new], axis=1)
    v = jnp.concatenate([cache_v, v_new], axis=1)
    kpos = jnp.concatenate([jnp.arange(w) - w, jnp.arange(t)])
    dist = jnp.abs(jnp.arange(t)[:, None] - kpos[None, :]).astype(F32)
    bias = -alibi_slopes(N_SWA_HEADS).reshape(N_SWA_KV, SWA_GROUP, 1, 1) * dist
    o = sink_attention(q.reshape(b, t, N_SWA_KV, SWA_GROUP, HEAD_DIM), k, v, bias, sinks)
    return o.reshape(b, t, N_SWA_HEADS, HEAD_DIM)

def merge_heads(x, o_a, o_b, g_fox_out, g_swa_out, w_out):
    b, s = x.shape[0], x.shape[1]
    oa = rmsnorm(o_a.reshape(b, s, FOX_W), g_fox_out)
    ob = rmsnorm(o_b.reshape(b, s, SWA_QW), g_swa_out)
    return x + jnp.einsum('bsm,md->bsd', jnp.concatenate([oa, ob], axis=-1), w_out)

def hier_moe(h, w_rg, b_rg, w_re, b_re, w_gate, w_up, w_down):
    def per_row(hr):
        n = hr.shape[0]
        pg = jax.nn.softmax(jnp.einsum('sd,dg->sg', hr, w_rg, preferred_element_type=F32) + b_rg.astype(F32), axis=-1)
        g_idx = jnp.argmax(pg, axis=-1)
        p_grp = jnp.take_along_axis(pg, g_idx[:, None], axis=-1)
        le = (jnp.einsum('sd,de->se', hr, w_re, preferred_element_type=F32) + b_re.astype(F32)).reshape(n, N_GROUPS, EXPERTS_PER_GROUP)
        le = jnp.take_along_axis(le, g_idx[:, None, None], axis=1)[:, 0]
        w_top, i_top = lax.top_k(jax.nn.softmax(le, axis=-1), TOP_K)
        w_top = w_top / jnp.sum(w_top, axis=-1, keepdims=True) * p_grp
        e_idx = g_idx[:, None] * EXPERTS_PER_GROUP + i_top
        gate = jnp.sum(jax.nn.one_hot(e_idx, N_EXPERTS, dtype=F32) * w_top[..., None], axis=1)
        a = jnp.einsum('sd,edf->sef', hr, w_gate)
        u = jnp.einsum('sd,edf->sef', hr, w_up)
        hid = jax.nn.silu(a) * u * gate[..., None].astype(hr.dtype)
        return jnp.einsum('sef,efd->sd', hid, w_down)
    return lax.map(per_row, h)

def setup_inputs(seed: int = 0) -> dict:
    key = jax.random.key(seed)
    ks = jax.random.split(key, 24)
    nrm = jax.random.normal
    L = DEPTH
    return {
        'x_prompt': nrm(ks[0], (BATCH, SEQ, D_MODEL), F32),
        'x_sample': nrm(ks[1], (DEC_BATCH, DEC_SEQ, D_MODEL), F32),
        'cache_fox_k': nrm(ks[2], (L, DEC_BATCH, PAST_LEN, N_FOX_HEADS, HEAD_DIM), F32),
        'cache_fox_v': nrm(ks[3], (L, DEC_BATCH, PAST_LEN, N_FOX_HEADS, HEAD_DIM), F32),
        'cache_fox_logf': jax.nn.log_sigmoid(FORGET_BIAS + nrm(ks[4], (L, DEC_BATCH, PAST_LEN, N_FOX_HEADS), F32)),
        'cache_swa_k': nrm(ks[5], (L, DEC_BATCH, WINDOW, N_SWA_KV, HEAD_DIM), F32),
        'cache_swa_v': nrm(ks[6], (L, DEC_BATCH, WINDOW, N_SWA_KV, HEAD_DIM), F32),
        'g_mix_norm': 1.0 + 0.02 * nrm(ks[7], (L, D_MODEL), F32),
        'w_in': nrm(ks[8], (L, D_MODEL, PROJ_W), F32) * D_MODEL ** -0.5,
        'b_forget': FORGET_BIAS + 0.1 * nrm(ks[9], (L, N_FOX_HEADS), F32),
        'swa_sinks': 0.5 * nrm(ks[10], (L, N_SWA_HEADS), F32),
        'g_fox_out': 1.0 + 0.02 * nrm(ks[11], (L, FOX_W), F32),
        'g_swa_out': 1.0 + 0.02 * nrm(ks[12], (L, SWA_QW), F32),
        'w_out': nrm(ks[13], (L, MIX_W, D_MODEL), F32) * MIX_W ** -0.5,
        'g_ffn_norm': 1.0 + 0.02 * nrm(ks[14], (L, D_MODEL), F32),
        'w_router_group': nrm(ks[15], (L, D_MODEL, N_GROUPS), F32) * D_MODEL ** -0.5,
        'b_router_group': 0.01 * nrm(ks[16], (L, N_GROUPS), F32),
        'w_router_expert': nrm(ks[17], (L, D_MODEL, N_EXPERTS), F32) * D_MODEL ** -0.5,
        'b_router_expert': 0.01 * nrm(ks[18], (L, N_EXPERTS), F32),
        'w_gate': nrm(ks[19], (L, N_EXPERTS, D_MODEL, D_EXPERT), F32) * D_MODEL ** -0.5,
        'w_up': nrm(ks[20], (L, N_EXPERTS, D_MODEL, D_EXPERT), F32) * D_MODEL ** -0.5,
        'w_down': nrm(ks[21], (L, N_EXPERTS, D_EXPERT, D_MODEL), F32) * D_EXPERT ** -0.5,
        'g_final': 1.0 + 0.02 * nrm(ks[22], (D_MODEL,), F32),
    }

def reference(x_prompt, x_sample, cache_fox_k, cache_fox_v, cache_fox_logf, cache_swa_k, cache_swa_v,
              g_mix_norm, w_in, b_forget, swa_sinks, g_fox_out, g_swa_out, w_out, g_ffn_norm,
              w_router_group, b_router_group, w_router_expert, b_router_expert,
              w_gate, w_up, w_down, g_final):
    xp, xs = x_prompt, x_sample
    fk_p, fv_p, fl_p, sk_p, sv_p = [], [], [], [], []
    fk_s, fv_s, fl_s, sk_s, sv_s = [], [], [], [], []
    for l in range(DEPTH):
        moe_w = (w_router_group[l], b_router_group[l], w_router_expert[l], b_router_expert[l],
                 w_gate[l], w_up[l], w_down[l])
        q_a, k_a, v_a, lf, q_b, k_b, v_b = project(xp, g_mix_norm[l], w_in[l], b_forget[l])
        o_a = fox_prompt(q_a, k_a, v_a, lf)
        o_b = swa_prompt(q_b, k_b, v_b, swa_sinks[l])
        xp = merge_heads(xp, o_a, o_b, g_fox_out[l], g_swa_out[l], w_out[l])
        xp = xp + hier_moe(rmsnorm(xp, g_ffn_norm[l]), *moe_w)
        fk_p.append(k_a)
        fv_p.append(v_a)
        fl_p.append(lf)
        sk_p.append(k_b[:, -WINDOW:])
        sv_p.append(v_b[:, -WINDOW:])
        q_a, k_a, v_a, lf, q_b, k_b, v_b = project(xs, g_mix_norm[l], w_in[l], b_forget[l])
        o_a = fox_sample(q_a, k_a, v_a, lf, cache_fox_k[l], cache_fox_v[l], cache_fox_logf[l])
        o_b = swa_sample(q_b, k_b, v_b, cache_swa_k[l], cache_swa_v[l], swa_sinks[l])
        xs = merge_heads(xs, o_a, o_b, g_fox_out[l], g_swa_out[l], w_out[l])
        xs = xs + hier_moe(rmsnorm(xs, g_ffn_norm[l]), *moe_w)
        fk_s.append(k_a)
        fv_s.append(v_a)
        fl_s.append(lf)
        sk_s.append(k_b)
        sv_s.append(v_b)
    y_prompt = rmsnorm(xp, g_final)
    y_sample = rmsnorm(xs, g_final)
    fox_k_prompt = jnp.stack(fk_p, axis=0)
    fox_v_prompt = jnp.stack(fv_p, axis=0)
    fox_logf_prompt = jnp.stack(fl_p, axis=0)
    swa_k_prompt = jnp.stack(sk_p, axis=0)
    swa_v_prompt = jnp.stack(sv_p, axis=0)
    fox_k_sample = jnp.stack(fk_s, axis=0)
    fox_v_sample = jnp.stack(fv_s, axis=0)
    fox_logf_sample = jnp.stack(fl_s, axis=0)
    swa_k_sample = jnp.stack(sk_s, axis=0)
    swa_v_sample = jnp.stack(sv_s, axis=0)
    return (y_prompt, y_sample, fox_k_prompt, fox_v_prompt, fox_logf_prompt, swa_k_prompt, swa_v_prompt,
            fox_k_sample, fox_v_sample, fox_logf_sample, swa_k_sample, swa_v_sample)


_drawn_inputs = setup_inputs


def setup_inputs(seed=0):
    import zlib

    import numpy as np

    out = dict(_drawn_inputs(seed))
    spreads = {}
    factors = {'g_fox_out': 2.974,
     'b_router_group': 24.112,
     'b_router_expert': 5.239,
     'g_final': 7.943,
     'g_swa_out': 6.109,
     'g_ffn_norm': 4.204}
    for name, (base, spread) in spreads.items():
        noise = np.random.default_rng([zlib.crc32(name.encode()), seed]).standard_normal(out[name].shape)
        drawn = base * np.exp(spread * noise) if base else spread * noise
        out[name] = jnp.asarray(drawn.astype(out[name].dtype))
    for name, factor in factors.items():
        out[name] = (out[name] * factor).astype(out[name].dtype)
    return out
```

```python
from contextlib import ExitStack

import concourse.bass as bass
import numpy as np
from concourse import mybir

F32 = mybir.dt.float32
BF16 = mybir.dt.bfloat16
I32 = mybir.dt.int32
ALU = mybir.AluOpType
ACT = mybir.ActivationFunctionType
AX = mybir.AxisListType

P = 128
D = 1024
C = D // P
SEQ, DEC, PAST, WIN = 1024, 64, 256, 128
NP_T = SEQ // P
NT = NP_T + 1
SAMPLE = NP_T
NK = NT + PAST // P
DH = 64
NH = 8
QKV = 3 * NH * DH
SWA = NH * DH + 2 * 2 * DH
PROJ = QKV + NH + SWA
GRP, EPG = 4, 8
NE = GRP * EPG
FE = 128
NOVER = 2 * NT * P // P - 2
NTILES = NE + NOVER
TOK = NT * P
SCALE = DH ** -0.5
EPS = 1e-6
BIG = 1.0e30
SKIP = 1 << 20
WSLOT = 3 * D
NSLOT = 4


def build(nc, t):
    ctx = ExitStack()
    with ctx:
        def sb(name, shape, dt=F32):
            return ctx.enter_context(nc.sbuf_tensor(name, shape, dt))

        def sem(name):
            return ctx.enter_context(nc.semaphore(name))

        ds = bass.ds

        big = sb("big", [P, C * PROJ])
        w_in = big[:, :].rearrange("p (c n) -> p c n", c=C)
        o_all = big[:, 0:NT * D].rearrange("p (t n) -> p t n", t=NT)
        free0 = NT * D

        def cut(region, at, *shape):
            n = int(np.prod(shape))
            ap = region[:, at:at + n]
            if len(shape) == 2:
                ap = ap.rearrange("p (a b) -> p a b", b=shape[1])
            return ap

        kT = [cut(big, free0 + u * NK * P, NK * P) for u in range(2)]
        qT = [cut(big, free0 + 2 * NK * P + u * NT * P, NT * P) for u in range(2)]
        at = free0 + 2 * NK * P + 2 * NT * P
        prob = [cut(big, at + u * SEQ, SEQ) for u in range(2)]
        probT = [cut(big, at + (2 + u) * SEQ, SEQ) for u in range(2)]
        skT = [cut(big, free0 + v * (NT + 1) * P, (NT + 1) * P) for v in range(2)]
        at = free0 + 2 * (NT + 1) * P
        sqT = [cut(big, at + u * NT * P, NT * P) for u in range(2)]
        at += 2 * NT * P
        sprob = [cut(big, at + u * 4 * P, 2, 2 * P) for u in range(2)]
        sprobT = [cut(big, at + (2 + u) * 4 * P, 4 * P) for u in range(2)]
        xr = [cut(big, free0 + u * D, D) for u in range(2)]
        on = [cut(big, free0 + (2 + u) * D, D) for u in range(2)]
        oT = [cut(big, free0 + (4 + u) * D, C, P) for u in range(2)]
        hh = [cut(big, free0 + (6 + u) * D, D) for u in range(2)]
        hhT = cut(big, free0 + 8 * D, C, P)
        at = free0
        rt = {}
        for name in ("lem", "eq", "oh1", "oh2", "run", "rank", "pos", "tmp", "q"):
            rt[name] = cut(big, at, NT, NE)
            at += NT * NE
        qi = cut(big, at, NT * NE).bitcast(I32)
        at += NT * NE
        for name in ("lg", "ohg", "eqg"):
            rt[name] = cut(big, at, NT, GRP)
            at += NT * GRP
        small = {}
        for name in ("m0", "m1", "m2", "i0", "i1", "i2", "den", "pg", "e21", "w1", "w2", "p1", "p2"):
            small[name] = cut(big, at, NT)
            at += NT
        nov = cut(big, at, 7, NE)
        at += 7 * NE
        ovi = cut(big, at, 2 * NE).bitcast(I32)
        at += 2 * NE
        ovc = cut(big, at, NOVER, NE)
        at += NOVER * NE
        ovf = cut(big, at, NOVER)
        at += NOVER
        ex = {}
        for name in ("e", "s", "r", "a", "hid", "hidT"):
            ex[name] = [cut(big, at + u * FE, FE) for u in range(2)]
            at += 2 * FE
        logit_t = cut(big, at, NT, GRP + NE)
        at += NT * (GRP + NE)
        maskb = cut(big, at, NT * NE // 2).bitcast(BF16)
        at += NT * NE // 2
        runb = cut(big, at, NT * NE // 2).bitcast(BF16)
        at += NT * NE // 2
        idx = cut(big, at, 8).bitcast(I32)
        at += 8
        ids = cut(big, at, 2 * NTILES).bitcast(I32)
        at += 2 * NTILES
        assert at <= C * PROJ - 2 * D
        ya = [cut(big, free0 + 3 * D + u * D, D) for u in range(2)]
        yb = [cut(big, free0 + 5 * D + u * D, D) for u in range(2)]
        fin = [cut(big, free0 + 7 * D + u * D, D) for u in range(2)]

        fox = sb("fox", [P, NT * QKV])
        fox_t = fox[:, :].rearrange("p (t n) -> p t n", t=NT)
        w_out = cut(fox, 0, C, D)
        swa = sb("swa", [P, NT * SWA])
        swa_t = swa[:, :].rearrange("p (t n) -> p t n", t=NT)
        slot3 = sb("slot3", [P, WSLOT])
        wslot = [cut(fox, C * D, WSLOT), cut(swa, 0, WSLOT), cut(swa, WSLOT, WSLOT), slot3[:, :]]
        assert C * D + WSLOT <= NT * QKV and 2 * WSLOT <= NT * SWA
        work = sb("work", [P, 6 * D])
        x = [cut(work, u * D, D) for u in range(2)]
        xn = [cut(work, (2 + u) * D, D) for u in range(2)]
        xT = [cut(work, (4 + u) * D, C, P) for u in range(2)]
        at = 0
        ck = cut(work, at, 2, (NH + 1) * DH)
        at += 2 * (NH + 1) * DH
        cv = cut(work, at, 2, NH * DH)
        at += 2 * NH * DH
        kst = cut(work, at, NK, DH + 1)
        at += NK * (DH + 1)
        qst = cut(work, at, NT, DH + 1)
        at += NT * (DH + 1)
        skv = cut(work, at, 2 * 2 * DH)
        at += 2 * 2 * DH
        sqst = cut(work, at, NT, P)
        at += NT * P
        lz = cut(work, at, 3 * NT * NH)
        at += 3 * NT * NH
        lsum = cut(work, at, NK * NH)
        lsum_t = cut(work, at, NK, NH)
        at += NK * NH
        assert at <= 6 * D
        hg = [cut(work, u * D, D) for u in range(2)] + [cut(big, C * PROJ - (2 - u) * D, D) for u in range(2)]
        hgT = [cut(work, (2 + u) * D, C, P) for u in range(2)]
        yo = [cut(work, (4 + u) * D, D) for u in range(2)]

        cf = sb("cf", [P, 3 * P])
        ident, upto, ones = cf[:, 0:P], cf[:, P:2 * P], cf[:, 2 * P:3 * P]
        cb = sb("cb", [P, 4 * P + 2 * NH * P], BF16)
        identb, causal, before, onesb = (cb[:, n * P:(n + 1) * P] for n in range(4))
        alibi = cb[:, 4 * P:4 * P + 2 * NH * P]
        ci = sb("ci", [P, NT * 4], I32)
        cr = sb("cr", [P, NE + NT])
        g0 = sb("g0", [P, D])
        g1 = sb("g1", [P, D])
        bf = sb("bf", [P, NH])
        sink = sb("sink", [P, NH])
        nsink = sb("nsink", [P, NH])
        sraw = sb("sraw", [P, NH])
        br = sb("br", [P, GRP + NE])
        wr = sb("wr", [P, C * (GRP + NE)])
        wr_t = wr[:, :].rearrange("p (c e) -> p c e", c=C)
        lf = sb("lf", [P, NK * NH])
        lf_t = lf[:, :].rearrange("p (t h) -> p t h", t=NK)
        negc = sb("negc", [P, NK * (NH + 1)])
        negc_t = negc[:, :].rearrange("p (t h) -> p t h", t=NK)
        st = sb("st", [P, 16])
        eps = sb("eps", [P, 2])
        nm = sb("nm", [P, 16])
        rs = sb("rs", [P, 16])
        rc = sb("rc", [P, 8])
        wgt = sb("wgt", [P, 2 * NT])
        dest = sb("dest", [P, 2 * NT], I32)
        over = sb("over", [1, NOVER + 1], I32)

        ps = [ctx.enter_context(nc.psum_tensor(f"ps{b}", [P, 1024], F32)) for b in range(4)]
        bank = [ps[b // 2][:, 512 * (b % 2):512 * (b % 2) + 512] for b in range(8)]

        h_dram = nc.dram_tensor("h_rows", (TOK, D), F32, kind="Internal").ap()
        y_dram = nc.dram_tensor("y_rows", (2 * TOK, D), F32, kind="Internal").ap()
        id_dram = nc.dram_tensor("id_rows", (P * NTILES, 2), I32, kind="Internal").ap()

        names = """const_in gain_in small_in wr_in cache_in kv_out w_out_in g_late_in eps_set
            square_done rms_done rstd_done xn_done xT_done xT_copied proj_done evac_v evac_s
            lf_v lf_s c_mm c_ready lf_out
            pad_set aug_set kv_staged st_T st_copied_s st_copied_v qk_done nmax_done exp_done pT_a pT_b cp_a cp_b pv_done o_done recip
            s_aug s_staged s_kT s_kcp s_qT_T s_qT_cp s_qk s_nm s_nmc s_exp s_sexp s_pT s_cpv s_cps s_pv s_rc s_od
            o_stat o_rms o_rstd on_done oT_done oT_copied om_done x2_done h_stat h_rms h_rstd h_done h_out_a h_out_b hT_done hT_copied r_done
            r_step r_exp r_mask r_mm r_id id_init id_out id_in
            pool_went idx_set dst_set g_done gT_done gT_cs gT_cv gu_done e_done ev_step hid_done hidT_done hidT_cp dn_done y_cs y_cv hg_set
            v_idx v_g v_w v_gT v_gTc v_gu v_e v_s v_hid v_hT v_hTc v_dn v_y v_out experts_done
            f_acc f_stat f_rms f_rstd f_fin f_out_a f_out_b""".split()
        s = {n: sem(n) for n in names}
        win_in = [sem(f"win_in{n}") for n in range(5)]
        x_in = [sem(f"x_in{u}") for u in range(2)]
        xr_in = [sem(f"xr_in{u}") for u in range(2)]
        w_in_slot = [sem(f"w_in_slot{k}") for k in range(NSLOT)]
        g_in = [sem(f"g_in{u}") for u in range(4)]
        y_out = [sem(f"y_out{u}") for u in range(2)]
        y_in = [sem(f"y_in{u}") for u in range(2)]

        x_rows = t["x_prompt"].rearrange("a s d -> (a s) d")
        xs_rows = t["x_sample"].rearrange("a s d -> (a s) d")
        w_in_dram = t["w_in"].rearrange("l (p c) n -> p (l c) n", c=C)
        COLS = [0, 512, 1024, 1536, 2048, PROJ]
        SW0 = 512 - NH

        def row(ap, n):
            return ap.rearrange("(a n) -> a n", a=1).broadcast_to([P, n])

        STEPS = [(u, i) for u in range(2) for i in range(NT)]
        NS = len(STEPS)
        nblk = [i + 1 for i in range(NP_T)] + [1 + PAST // P]
        TWO = [i for i in range(NT) if nblk[i] > 4]
        SG = [("q", 0, 4), ("q", 4, 8), ("q", 8, 9), ("k", 0, 4), ("k", 4, 8), ("k", 8, 11)]
        SG_AT = {2: 0, 3: 1, 4: 2, 5: 3, 6: 4, 7: 5}
        SSG = [(0, 4), (4, 8), (8, 9)]
        SSG_AT = {3: 0, 5: 1, 7: 2}

        def keytile(i, b):
            return b if i < SAMPLE else [NT, NT + 1, SAMPLE][b]

        def skeytile(i, b):
            return i - 1 + b if i < SAMPLE else [NT, SAMPLE][b]

        block = ctx.enter_context(nc.Block())

        @block.sync
        def _(sp):
            sp.dma_start(x[0], x_rows[0:P, :]).then_inc(x_in[0], 16)
            sp.dma_start(g0[:, :], row(t["g_mix_norm"].rearrange("l d -> (l d)"), D)).then_inc(s["gain_in"], 16)
            sp.dma_start(cf[:, :], t["const_f"]).then_inc(s["const_in"], 16)
            sp.dma_start(w_in[:, :, COLS[0]:COLS[1]], w_in_dram[:, :, COLS[0]:COLS[1]]).then_inc(win_in[0], 16)
            sp.dma_start(x[1], x_rows[P:2 * P, :]).then_inc(x_in[1], 16)
            for n in range(1, 5):
                sp.dma_start(w_in[:, :, COLS[n]:COLS[n + 1]], w_in_dram[:, :, COLS[n]:COLS[n + 1]]).then_inc(win_in[n], 16)
            small_loads = [
                (cb[:, :], t["const_b"]), (ci[:, :], t["const_i"]), (cr[:, :], t["const_r"]),
                (bf[:, :], row(t["b_forget"].rearrange("l d -> (l d)"), NH)),
                (sraw[:, :], row(t["swa_sinks"].rearrange("l d -> (l d)"), NH)),
                (br[:, 0:GRP], row(t["b_router_group"].rearrange("l d -> (l d)"), GRP)),
                (br[:, GRP:GRP + NE], row(t["b_router_expert"].rearrange("l d -> (l d)"), NE)),
                (wr_t[:, :, 0:GRP], t["w_router_group"].rearrange("l (p c) n -> p (l c) n", c=C)),
                (wr_t[:, :, GRP:GRP + NE], t["w_router_expert"].rearrange("l (p c) n -> p (l c) n", c=C)),
                (lf_t[:, NT:NK, :], t["cache_fox_logf"].rearrange("l b (t p) h -> p (l b t) h", p=P)),
                (g1[:, 0:512], row(t["g_fox_out"].rearrange("l d -> (l d)"), 512)),
                (g1[:, 512:D], row(t["g_swa_out"].rearrange("l d -> (l d)"), 512)),
                (slot3[:, 0:D].rearrange("p (c f) -> p c f", c=C), t["w_gate"][0, NSLOT - 1].rearrange("(p c) f -> p c f", c=C)),
                (slot3[:, D:2 * D].rearrange("p (c f) -> p c f", c=C), t["w_up"][0, NSLOT - 1].rearrange("(p c) f -> p c f", c=C)),
                (slot3[:, 2 * D:3 * D], t["w_down"][0, NSLOT - 1]),
            ]
            for dst, src in small_loads:
                sp.dma_start(dst, src).then_inc(s["small_in"], 16)
            with sp.Fori(1, NP_T // 2) as j:
                for u in range(2):
                    sp.wait_ge(s["xn_done"], j * 2 + (u - 1))
                    sp.dma_start(x[u], x_rows[ds(j * 2 * P + u * P, P), :]).then_inc(x_in[u], 16)
            sp.wait_ge(s["xn_done"], NT - 2)
            sp.dma_start(x[0][0:DEC, :], xs_rows).then_inc(x_in[0], 16)
            sp.wait_ge(s["evac_v"], 3 * (NT + 1))
            sp.wait_ge(s["evac_s"], 2 * (NT + 1))
            sp.dma_start(ck[:, :, 0:NH * DH], t["cache_fox_k"].rearrange("l b (t p) h d -> p (l b t) (h d)", p=P)).then_inc(s["cache_in"], 16)
            sp.dma_start(cv[:, :, :], t["cache_fox_v"].rearrange("l b (t p) h d -> p (l b t) (h d)", p=P)).then_inc(s["cache_in"], 16)
            sp.dma_start(skv[:, 0:2 * DH], t["cache_swa_k"].rearrange("l b p h d -> p (l b h d)")).then_inc(s["cache_in"], 16)
            sp.dma_start(skv[:, 2 * DH:4 * DH], t["cache_swa_v"].rearrange("l b p h d -> p (l b h d)")).then_inc(s["cache_in"], 16)
            sp.dma_start(g0[:, :], row(t["g_ffn_norm"].rearrange("l d -> (l d)"), D)).then_inc(s["g_late_in"], 16)
            for n, name in ((1, "fox_k"), (2, "fox_v")):
                cols = slice(n * 512, (n + 1) * 512)
                sp.dma_start(t[name + "_prompt"].rearrange("l b (t p) h d -> p (l b t) (h d)", p=P),
                             fox_t[:, 0:NP_T, cols]).then_inc(s["kv_out"], 16)
                sp.dma_start(t[name + "_sample"].rearrange("l b s h d -> (l b s) (h d)"),
                             fox_t[0:DEC, SAMPLE, cols]).then_inc(s["kv_out"], 16)
            for n, name in ((4, "swa_k"), (5, "swa_v")):
                cols = slice(n * P, (n + 1) * P)
                sp.dma_start(t[name + "_prompt"].rearrange("l b s h d -> (l b s) (h d)"),
                             swa_t[:, NP_T - 1, cols]).then_inc(s["kv_out"], 16)
                sp.dma_start(t[name + "_sample"].rearrange("l b s h d -> (l b s) (h d)"),
                             swa_t[0:DEC, SAMPLE, cols]).then_inc(s["kv_out"], 16)
            sp.wait_ge(s["lf_v"], 3)
            sp.dma_start(t["fox_logf_prompt"].rearrange("l b (t p) h -> p (l b t) h", p=P),
                         lf_t[:, 0:NP_T, :]).then_inc(s["kv_out"], 16)
            sp.dma_start(t["fox_logf_sample"].rearrange("l b s h -> (l b s) h"),
                         lf_t[0:DEC, SAMPLE, :]).then_inc(s["kv_out"], 16)
            sp.wait_ge(s["kv_out"], 16 * 10)
            sp.wait_ge(s["pv_done"], 4 * NS)
            sp.wait_ge(s["kv_staged"], NH + 1)
            sp.dma_start(w_out, t["w_out"].rearrange("l (c p) n -> p (l c) n", p=P)).then_inc(s["w_out_in"], 16)

            def expert(k, gate, up, down):
                sp.dma_start(wslot[k][:, 0:D].rearrange("p (c f) -> p c f", c=C), gate).then_inc(w_in_slot[k], 16)
                sp.dma_start(wslot[k][:, D:2 * D].rearrange("p (c f) -> p c f", c=C), up).then_inc(w_in_slot[k], 16)
                sp.dma_start(wslot[k][:, 2 * D:3 * D], down).then_inc(w_in_slot[k], 16)

            wg = t["w_gate"].rearrange("l e (p c) f -> (l e) p c f", c=C)
            wu = t["w_up"].rearrange("l e (p c) f -> (l e) p c f", c=C)
            wd = t["w_down"].rearrange("l e f d -> (l e) f d")
            expert(0, wg[0], wu[0], wd[0])
            sp.wait_ge(s["s_pv"], 2 * NS)
            for k in (1, 2):
                expert(k, wg[k], wu[k], wd[k])
            def load_xr(i, u, rows):
                src = x_rows[ds(i * P, P), :] if rows == P else xs_rows
                sp.dma_start(xr[u][0:rows, :], src).then_inc(xr_in[u], 16)

            for u in range(2):
                load_xr(u, u, P)

            def send_h(i, u):
                sp.wait_ge(s["h_done"], i + 1)
                sp.dma_start(h_dram[ds(i * P, P), :], hh[u]).then_inc(s["h_out_b" if u else "h_out_a"], 16)

            with sp.Fori(0, NP_T // 2 - 1) as j:
                for u in range(2):
                    sp.wait_ge(s["x2_done"], (j * 2 + (u + 1)) * 2)
                    load_xr(j * 2 + (u + 2), u, P)
                    send_h(j * 2 + u, u)
            sp.wait_ge(s["x2_done"], (NT - 2) * 2)
            load_xr(NT - 1, 0, DEC)
            for i in range(NT - 3, NT):
                send_h(i, i % 2)
            sp.wait_ge(s["on_done"], 2 * NT)
            sp.dma_start(g1[:, :], row(t["g_final"], D)).then_inc(s["g_late_in"], 16)
            sp.wait_ge(s["r_id"], 1)
            sp.dma_start(id_dram.rearrange("(p t) w -> p (t w)", p=P), ids[:, :]).then_inc(s["id_init"], 16)
            sp.wait_ge(s["id_out"], 16 * 2 * NT)
            sp.dma_start(ids[:, :], id_dram.rearrange("(p t) w -> p (t w)", p=P)).then_inc(s["id_in"], 16)
            with sp.Fori(1, NE // NSLOT) as j:
                for k in range(NSLOT):
                    sp.wait_ge(s["dn_done"], j * NSLOT + (k + 1 - NSLOT))
                    e = j * NSLOT + k
                    expert(k, wg[ds(e, 1)].rearrange("e p c f -> p (e c) f"), wu[ds(e, 1)].rearrange("e p c f -> p (e c) f"),
                           wd[ds(e, 1)].rearrange("e f d -> (e f) d"))
            sp.wait_ge(s["dn_done"], NE)
            sp.wait_ge(s["id_in"], 16)
            n_over = sp.value_load(over[0:1, 0:1], min_val=0, max_val=NOVER)
            with sp.Fori(0, NOVER) as k:
                with sp.If(k < n_over):
                    e = sp.value_load(over[0:1, ds(k + 1, 1)], min_val=0, max_val=NE - 1)
                    sp.wait_ge(s["v_dn"], k + 1)
                    for n, w in ((0, wg), (1, wu)):
                        sp.dma_start(wslot[0][:, n * D:(n + 1) * D].rearrange("p (c f) -> p c f", c=C),
                                     w[ds(e, 1)].rearrange("e p c f -> p (e c) f")).then_inc(s["v_w"], 16)
                    sp.dma_start(wslot[0][:, 2 * D:3 * D], wd[ds(e, 1)].rearrange("e f d -> (e f) d")).then_inc(s["v_w"], 16)
            sp.wait_ge(s["experts_done"], 1)

            def load_y(i, u, rows):
                sp.dma_start(ya[u][0:rows, :], y_dram[ds(i * P, rows), :]).then_inc(y_in[u], 16)
                sp.dma_start(yb[u][0:rows, :], y_dram[ds(i * P + TOK, rows), :]).then_inc(y_in[u], 16)

            def store(i, u):
                sp.wait_ge(s["f_fin"], i + 1)
                sp.dma_start(t["y_prompt"].rearrange("a s d -> (a s) d")[ds(i * P, P), :], fin[u]).then_inc(s["f_out_b" if u else "f_out_a"], 16)

            for u in range(2):
                load_y(u, u, P)
            with sp.Fori(0, NP_T // 2 - 1) as j:
                for u in range(2):
                    sp.wait_ge(s["f_acc"], (j * 2 + (u + 1)) * 2)
                    load_y(j * 2 + (u + 2), u, P)
                    store(j * 2 + u, u)
            sp.wait_ge(s["f_acc"], (NT - 2) * 2)
            load_y(NT - 1, 0, DEC)
            for i in (NP_T - 2, NP_T - 1):
                store(i, i % 2)
            sp.wait_ge(s["f_fin"], NT)
            sp.dma_start(t["y_sample"].rearrange("a s d -> (a s) d"), fin[0][0:DEC, :]).then_inc(s["f_out_a"], 16)
            sp.wait_ge(s["f_out_a"], 16 * 5)
            sp.wait_ge(s["f_out_b"], 16 * 4)

        @block.gpsimd
        def _(pool):
            pool.wait_ge(s["cache_in"], 64)
            pool.memset(qst[:, :, DH:DH + 1], 1.0 / SCALE).then_inc(s["pad_set"], 1)
            pool.memset(ck[:, :, NH * DH:], 0.0).then_inc(s["pad_set"], 1)
            pool.wait_ge(s["pad_set"], 2)
            pool.wait_ge(s["c_ready"], 1)

            def stage(h, done, first=False):
                if not first:
                    pool.wait_ge(s["st_T"], done)
                pool.tensor_copy(qst[:, :, 0:DH], fox_t[:, :, ds(h * DH, DH)])
                pool.tensor_copy(kst[:, 0:NT, 0:DH], fox_t[:, :, ds(h * DH + NH * DH, DH)])
                pool.tensor_copy(kst[:, NT:NK, 0:DH], ck[:, :, ds(h * DH, DH)])
                pool.tensor_copy(kst[:, :, DH:DH + 1], negc_t[:, :, ds(h, 1)]).then_inc(s["kv_staged"], 1)

            stage(0, 0, True)
            with pool.Fori(0, NH) as h:
                stage(h + 1, h * 6 + 6)

            def s_stage(g, done, first=False):
                if not first:
                    pool.wait_ge(s["s_qT_T"], done)
                pool.tensor_copy(sqst[:, :, 0:DH], swa_t[:, :, ds(g * DH, DH)])
                pool.tensor_copy(sqst[:, :, DH:P], swa_t[:, :, ds(g * DH + 4 * DH, DH)]).then_inc(s["s_staged"], 1)

            s_stage(0, 0, True)
            with pool.Fori(0, 4) as g:
                s_stage(g + 1, g * 3 + 3)
            pool.wait_ge(s["r_mm"], 2)
            pool.memset(ids[:, :], SKIP).then_inc(s["r_id"], 1)
            pool.wait_ge(s["id_init"], 16)
            pool.wait_ge(s["r_mask"], 2)
            for i in range(NT):
                for c in range(2):
                    n = 2 * i + c
                    pool.indirect_dma_start(
                        out=id_dram, out_offset=bass.IndirectOffsetOnAxis(ap=dest[:, n:n + 1], axis=0),
                        in_=ci[:, 2 * n:2 * n + 2], in_offset=None,
                        bounds_check=P * NTILES - 1, oob_is_err=False).then_inc(s["id_out"], 16)
            pool.wait_ge(s["s_staged"], 5)
            pool.wait_ge(s["pv_done"], 4 * NS)
            pool.wait_ge(s["s_pv"], 2 * NS)
            pool.wait_ge(s["s_qT_T"], 15)
            for k in range(4):
                pool.memset(hg[k], 0.0).then_inc(s["hg_set"], 1)
            pool.wait_ge(s["hg_set"], 4)
            pool.wait_ge(s["id_in"], 16)
            for i in range(2):
                pool.wait_ge(s["h_out_a"], 16 * 5)
                pool.wait_ge(s["h_out_b"], 16 * 4)

            def gather(tt, k):
                pool.tensor_copy(idx[:, k:k + 1], ids[:, ds(tt * 2, 1)]).then_inc(s["idx_set"], 1)
                pool.wait_ge(s["idx_set"], tt + 1)
                pool.sem_inc(s["pool_went"], 1)
                pool.indirect_dma_start(
                    out=hg[k], out_offset=None, in_=h_dram,
                    in_offset=bass.IndirectOffsetOnAxis(ap=idx[:, k:k + 1], axis=0),
                    bounds_check=TOK - 1, oob_is_err=False).then_inc(g_in[k], 16)

            def scatter(tt, k):
                u = k % 2
                if not (isinstance(tt, int) and tt < 2):
                    pool.wait_ge(y_out[u], (tt - u) * 8)
                pool.tensor_copy(idx[:, 4 + u:5 + u], ids[:, ds(tt * 2 + 1, 1)]).then_inc(s["dst_set"], 1)
                pool.wait_ge(s["dst_set"], tt + 1)
                pool.wait_ge(s["y_cs"], tt + 1)
                pool.wait_ge(s["y_cv"], tt + 1)
                pool.sem_inc(s["pool_went"], 1)
                pool.indirect_dma_start(
                    out=y_dram, out_offset=bass.IndirectOffsetOnAxis(ap=idx[:, 4 + u:5 + u], axis=0),
                    in_=yo[u], in_offset=None,
                    bounds_check=2 * TOK - 1, oob_is_err=False).then_inc(y_out[u], 16)

            def rows_step(tt, k, more=True):
                if more:
                    pool.wait_ge(s["gT_done"], tt * 2 + 4)
                    gather(tt + 5, (k + 1) % 4)
                scatter(tt, k)

            for tt in range(4):
                gather(tt, tt)
            pool.wait_ge(s["gT_done"], 2)
            gather(4, 0)
            for tt in range(4):
                rows_step(tt, tt)
            with pool.Fori(1, NE // 4 - 2) as j:
                for k in range(4):
                    rows_step(j * 4 + k, k)
            for tt in range(NE - 8, NE):
                rows_step(tt, tt % 4, tt + 5 < NE)
            pool.wait_ge(y_out[0], 16 * NE // 2)
            pool.wait_ge(y_out[1], 16 * NE // 2)
            n_over = pool.value_load(over[0:1, 0:1], min_val=0, max_val=NOVER)
            with pool.Fori(0, NOVER) as k:
                with pool.If(k < n_over):
                    pool.tensor_copy(idx[:, 0:2], ids[:, ds(k * 2 + 2 * NE, 2)]).then_inc(s["v_idx"], 1)
                    pool.wait_ge(s["v_idx"], k + 1)
                    pool.sem_inc(s["pool_went"], 1)
                    pool.indirect_dma_start(
                        out=hg[0], out_offset=None, in_=h_dram,
                        in_offset=bass.IndirectOffsetOnAxis(ap=idx[:, 0:1], axis=0),
                        bounds_check=TOK - 1, oob_is_err=False).then_inc(s["v_g"], 16)
                    pool.wait_ge(s["v_y"], k * 2 + 2)
                    pool.sem_inc(s["pool_went"], 1)
                    pool.indirect_dma_start(
                        out=y_dram, out_offset=bass.IndirectOffsetOnAxis(ap=idx[:, 1:2], axis=0),
                        in_=yo[0], in_offset=None,
                        bounds_check=2 * TOK - 1, oob_is_err=False).then_inc(s["v_out"], 16)
                    pool.wait_ge(s["v_out"], k * 16 + 16)
            pool.sem_inc(s["experts_done"], 1)

        @block.scalar
        def _(act):
            act.sem_inc(s["evac_s"], 2)
            act.sem_inc(s["cp_b"], 1)
            act.sem_inc(s["exp_done"], 2)
            act.wait_ge(s["eps_set"], 1)

            def norm(i, j, u):
                act.wait_ge(x_in[u], j * 16 + 16)
                if not (isinstance(i, int) and i < 2):
                    act.wait_ge(s["xT_done"], i * 2 - 2)
                act.activation(xn[u], x[u], ACT.Square, accum_out=st[:, u:u + 1]).then_inc(s["square_done"], 1)
                act.wait_ge(s["square_done"], i + 1)
                act.activation(st[:, 2 + u:3 + u], st[:, u:u + 1], ACT.Sqrt, bias=eps[:, 0:1], scale=1.0 / D).then_inc(s["rms_done"], 1)

            def copy_xT(i, u):
                if not (isinstance(i, int) and i < 2):
                    act.wait_ge(s["proj_done"], i * 5 - 5)
                for b in range(2):
                    act.wait_ge(s["xT_done"], i * 2 + (b + 1))
                    act.activation(xT[u][:, 4 * b:4 * b + 4, :], bank[b].rearrange("p (c k) -> p c k", c=4), ACT.Copy).then_inc(s["xT_copied"], 1)

            def evac(i, u):
                act.wait_ge(s["proj_done"], i * 5 + 2)
                act.activation(fox_t[:, ds(i, 1), 512:1024].rearrange("p a n -> p (a n)"), bank[3], ACT.Copy).then_inc(s["evac_s"], 1)
                act.wait_ge(s["proj_done"], i * 5 + 4)
                act.activation(lf_t[:, ds(i, 1), :].rearrange("p a n -> p (a n)"), bank[5][:, 0:NH], ACT.Copy)
                act.activation(swa_t[:, ds(i, 1), 0:SW0].rearrange("p a n -> p (a n)"), bank[5][:, NH:512], ACT.Copy).then_inc(s["evac_s"], 1)

            norm(0, 0, 0)
            copy_xT(0, 0)
            norm(1, 0, 1)
            def step(i, j, u):
                copy_xT(i + 1, 1 - u)
                norm(i + 2, j + 1, u)
                evac(i, u)

            for i in (0, 1):
                step(i, 0, i)
            with act.Fori(1, 3) as j:
                for u in range(2):
                    step(j * 2 + u, j, u)
            step(6, 3, 0)
            copy_xT(8, 0)
            evac(7, 1)
            evac(8, 0)

            n = NT * NH
            act.wait_ge(s["lf_v"], 2)
            act.activation(lz[:, n:2 * n], lz[:, 2 * n:3 * n], ACT.Exp, scale=-1.0).then_inc(s["lf_s"], 1)
            act.wait_ge(s["lf_s"], 1)
            act.activation(lz[:, 2 * n:3 * n], lz[:, n:2 * n], ACT.Ln, bias=eps[:, 1:2]).then_inc(s["lf_s"], 1)

            def stage_q(h6, u, gi):
                _, a, b = SG[gi]
                act.wait_ge(s["st_T"], h6 + (gi + 1))
                act.activation(qT[u][0:DH + 1, a * P:b * P], bank[7][0:DH + 1, 0:(b - a) * P], ACT.Copy, scale=SCALE).then_inc(s["st_copied_s"], 1)

            act.wait_ge(s["aug_set"], 4)
            for gi in range(3):
                stage_q(0, 0, gi)

            def fexp(it, k):
                u, i = STEPS[k]
                n = nblk[i] * P
                act.wait_ge(s["nmax_done"], it * NS + (k + 1))
                if k >= 1:
                    act.wait_ge(s["pT_a"], it * NS + max(k - 1, 1))
                act.activation(prob[k % 2][:, 0:n], ps[k % 2][:, 0:n], ACT.Exp, bias=nm[:, k % 2:k % 2 + 1],
                               accum_out=rs[:, k % 4:k % 4 + 1]).then_inc(s["exp_done"], 1)

            def copy_b(it, k):
                u, i = STEPS[k]
                n = nblk[i] * P
                if n > 512:
                    seen = sum(nblk[STEPS[m][1]] > 4 for m in range(k + 1))
                    act.wait_ge(s["pT_b"], it * 2 * len(TWO) + seen)
                    act.wait_ge(s["pv_done"], it * NS + (k - 1))
                    act.activation(probT[k % 2][:, 512:n], bank[5][:, 0:n - 512], ACT.Copy).then_inc(s["cp_b"], 1)

            with act.Fori(0, NH // 2) as it:
                fexp(it, 0)
                for k in range(NS):
                    u, i = STEPS[k]
                    if k + 1 < NS:
                        fexp(it, k + 1)
                    if i in SG_AT and SG_AT[i] < 3:
                        stage_q(it * 12 + 6 * (u + 1), 1 - u, SG_AT[i])
                    copy_b(it, k)

            def stage_sq(g3, u, gi):
                a, b = SSG[gi]
                act.wait_ge(s["s_qT_T"], g3 + (gi + 1))
                act.activation(sqT[u][:, a * P:b * P], bank[7][:, 0:(b - a) * P], ACT.Copy, scale=SCALE).then_inc(s["s_qT_cp"], 1)

            for gi in range(3):
                stage_sq(0, 0, gi)

            def sexp(it, k):
                u, i = STEPS[k]
                lo = P if i == 0 else 0
                act.wait_ge(s["s_nm"], it * NS + (k + 1))
                if k >= 1:
                    act.wait_ge(s["s_pT"], it * NS + max(k - 1, 1))
                for v in range(2):
                    act.activation(sprob[k % 2][:, v, lo:2 * P], ps[k % 2][:, v * 256 + lo:v * 256 + 256], ACT.Exp,
                                   bias=nm[:, 4 + 2 * (k % 2) + v:5 + 2 * (k % 2) + v],
                                   accum_out=rs[:, 4 + 2 * (k % 3) + v:5 + 2 * (k % 3) + v]).then_inc(s["s_exp"], 1)
                act.activation(rs[:, 10 + 2 * (k % 3):12 + 2 * (k % 3)], nm[:, 8 + 2 * (k % 2):10 + 2 * (k % 2)], ACT.Exp).then_inc(s["s_sexp"], 1)

            def scopy(it, k):
                if k % 2:
                    n = 2 * P if STEPS[k][1] == 0 else 4 * P
                    act.wait_ge(s["s_pT"], it * NS + (k + 1))
                    if k > 1:
                        act.wait_ge(s["s_pv"], it * NS + (k - 1))
                    act.activation(sprobT[1][:, 0:n], bank[5][:, 0:n], ACT.Copy).then_inc(s["s_cps"], 1)

            with act.Fori(0, 2) as it:
                sexp(it, 0)
                for k in range(NS):
                    u, i = STEPS[k]
                    if k + 1 < NS:
                        sexp(it, k + 1)
                    if i in SSG_AT:
                        stage_sq(it * 6 + 3 * (u + 1), 1 - u, SSG_AT[i])
                    scopy(it, k)

            act.wait_ge(s["s_od"], 2 * NS + 1)

            def norm_o(i, u):
                if not (isinstance(i, int) and i < 2):
                    act.wait_ge(s["oT_done"], i * 2 - 2)
                for v in range(2):
                    act.activation(on[u][:, 512 * v:512 * v + 512], o_all[:, ds(i, 1), 512 * v:512 * v + 512].rearrange("p a n -> p (a n)"),
                                   ACT.Square, accum_out=st[:, 2 * u + v:2 * u + v + 1]).then_inc(s["o_stat"], 1)
                act.wait_ge(s["o_stat"], i * 2 + 2)
                act.activation(st[:, 4 + 2 * u:6 + 2 * u], st[:, 2 * u:2 * u + 2], ACT.Sqrt, bias=eps[:, 0:1], scale=2.0 / D).then_inc(s["o_rms"], 1)

            def copy_oT(i, u):
                if not (isinstance(i, int) and i < 2):
                    act.wait_ge(s["om_done"], i - 1)
                for b in range(2):
                    act.wait_ge(s["oT_done"], i * 2 + (b + 1))
                    act.activation(oT[u][:, 4 * b:4 * b + 4, :], bank[b].rearrange("p (c k) -> p c k", c=4), ACT.Copy).then_inc(s["oT_copied"], 1)

            def norm_h(i, u):
                act.wait_ge(s["x2_done"], i * 2 + 2)
                if not (isinstance(i, int) and i < 2):
                    act.wait_ge(s["hT_done"], i * 2 - 2)
                    act.wait_ge(s["h_out_b" if u else "h_out_a"], (i - u) * 8)
                act.activation(hh[u], o_all[:, ds(i, 1), :].rearrange("p a n -> p (a n)"), ACT.Square,
                               accum_out=st[:, 12:13]).then_inc(s["h_stat"], 1)
                act.wait_ge(s["h_stat"], i + 1)
                act.activation(st[:, 13:14], st[:, 12:13], ACT.Sqrt, bias=eps[:, 0:1], scale=1.0 / D).then_inc(s["h_rms"], 1)

            def copy_hT(i):
                if not (isinstance(i, int) and i < 1):
                    act.wait_ge(s["r_done"], i)
                for b in range(2):
                    act.wait_ge(s["hT_done"], i * 2 + (b + 1))
                    act.activation(hhT[:, 4 * b:4 * b + 4, :], bank[4 + b].rearrange("p (c k) -> p c k", c=4), ACT.Copy).then_inc(s["hT_copied"], 1)

            norm_o(0, 0)
            copy_oT(0, 0)
            norm_o(1, 1)

            def ostep(i, u, last=2):
                if last >= 2:
                    norm_o(i + 2, u)
                if last >= 1:
                    copy_oT(i + 1, 1 - u)
                norm_h(i, u)

            ostep(0, 0)
            ostep(1, 1)
            copy_hT(0)
            with act.Fori(1, 3) as j:
                for u in range(2):
                    ostep(j * 2 + u, u)
                    copy_hT(j * 2 + (u - 1))
            ostep(6, 0)
            copy_hT(5)
            ostep(7, 1, 1)
            copy_hT(6)
            ostep(8, 0, 0)
            copy_hT(7)
            copy_hT(8)

            act.wait_ge(s["r_exp"], 1)
            act.activation(rt["eqg"], rt["lg"], ACT.Exp).then_inc(s["r_exp"], 1)
            act.wait_ge(s["r_exp"], 3)
            act.activation(small["e21"], small["m2"], ACT.Exp).then_inc(s["r_exp"], 1)

            def copy_gT(tt, u):
                act.wait_ge(s["gT_done"], tt * 2 + 1)
                if not (isinstance(tt, int) and tt < 2):
                    act.wait_ge(s["gu_done"], tt - 1)
                act.activation(hgT[u][:, 0:4, :], bank[0].rearrange("p (c k) -> p c k", c=4), ACT.Copy).then_inc(s["gT_cs"], 1)

            def gate_exp(tt, u):
                act.wait_ge(s["gu_done"], tt + 1)
                if not (isinstance(tt, int) and tt < 2):
                    act.wait_ge(s["ev_step"], tt * 3 - 5)
                act.activation(ex["e"][u], bank[2 + u][:, 0:FE], ACT.Exp, scale=-1.0).then_inc(s["e_done"], 1)

            def copy_hid(tt, u):
                act.wait_ge(s["hidT_done"], tt + 1)
                if not (isinstance(tt, int) and tt < 2):
                    act.wait_ge(s["dn_done"], tt - 1)
                act.activation(ex["hidT"][u], bank[6][:, 0:P], ACT.Copy).then_inc(s["hidT_cp"], 1)

            def copy_y(tt, u):
                act.wait_ge(s["dn_done"], tt + 1)
                if not (isinstance(tt, int) and tt < 2):
                    act.wait_ge(y_out[u], (tt - u) * 8)
                act.activation(yo[u][:, 0:512], bank[4], ACT.Copy).then_inc(s["y_cs"], 1)

            def estep(tt, u, last=2):
                if last >= 1:
                    gate_exp(tt + 1, 1 - u)
                copy_hid(tt, u)
                if last >= 2:
                    copy_gT(tt + 2, u)
                copy_y(tt, u)

            copy_gT(0, 0)
            copy_gT(1, 1)
            gate_exp(0, 0)
            estep(0, 0)
            estep(1, 1)
            with act.Fori(1, NE // 2 - 1) as j:
                for u in range(2):
                    estep(j * 2 + u, u)
            estep(NE - 2, 0, 1)
            estep(NE - 1, 1, 0)

            n_over = act.value_load(over[0:1, 0:1], min_val=0, max_val=NOVER)
            with act.Fori(0, NOVER) as k:
                with act.If(k < n_over):
                    act.wait_ge(s["v_gT"], k * 2 + 1)
                    act.activation(hgT[0][:, 0:4, :], bank[0].rearrange("p (c k) -> p c k", c=4), ACT.Copy).then_inc(s["v_gTc"], 1)
                    act.wait_ge(s["v_gu"], k + 1)
                    act.activation(ex["e"][0], bank[2][:, 0:FE], ACT.Exp, scale=-1.0).then_inc(s["v_e"], 1)
                    act.wait_ge(s["v_hT"], k + 1)
                    act.activation(ex["hidT"][0], bank[6][:, 0:P], ACT.Copy).then_inc(s["v_hTc"], 1)
                    act.wait_ge(s["v_dn"], k + 2)
                    act.activation(yo[0][:, 0:512], bank[4], ACT.Copy).then_inc(s["v_y"], 1)
            act.wait_ge(s["experts_done"], 1)

            def norm_f(i, u, rows):
                act.wait_ge(s["f_acc"], i * 2 + 2)
                if not (isinstance(i, int) and i < 2):
                    act.wait_ge(s["f_out_b" if u else "f_out_a"], (i - u) * 8)
                act.activation(fin[u][0:rows, :], o_all[0:rows, ds(i, 1), :].rearrange("p a n -> p (a n)"), ACT.Square,
                               accum_out=st[0:rows, u:u + 1]).then_inc(s["f_stat"], 1)
                act.wait_ge(s["f_stat"], i + 1)
                act.activation(st[0:rows, 2 + u:3 + u], st[0:rows, u:u + 1], ACT.Sqrt, bias=eps[0:rows, 0:1], scale=1.0 / D).then_inc(s["f_rms"], 1)

            norm_f(0, 0, P)
            norm_f(1, 1, P)
            with act.Fori(1, NP_T // 2) as j:
                for u in range(2):
                    norm_f(j * 2 + u, u, P)
            norm_f(8, 0, DEC)

        @block.vector
        def _(dve):
            dve.memset(eps[:, 0:1], EPS)
            dve.memset(negc[:, :], 0.0)
            dve.memset(eps[:, 1:2], 1.0).then_inc(s["eps_set"], 1)
            dve.sem_inc(s["evac_v"], 3)
            dve.sem_inc(s["o_done"], 1)
            dve.sem_inc(s["s_od"], 1)

            def scale_x(i, u):
                dve.wait_ge(s["rms_done"], i + 1)
                dve.reciprocal(st[:, 4 + u:5 + u], st[:, 2 + u:3 + u]).then_inc(s["rstd_done"], 1)
                dve.wait_ge(s["rstd_done"], i + 1)
                dve.scalar_tensor_tensor(out=xn[u], in0=x[u], scalar=st[:, 4 + u:5 + u], in1=g0[:, :],
                                         op0=ALU.mult, op1=ALU.mult).then_inc(s["xn_done"], 1)

            def evac(i):
                dve.wait_ge(s["proj_done"], i * 5 + 1)
                dve.tensor_copy(fox_t[:, ds(i, 1), 0:512].rearrange("p a n -> p (a n)"), bank[2]).then_inc(s["evac_v"], 1)
                dve.wait_ge(s["proj_done"], i * 5 + 3)
                dve.tensor_copy(fox_t[:, ds(i, 1), 1024:1536].rearrange("p a n -> p (a n)"), bank[4]).then_inc(s["evac_v"], 1)
                dve.wait_ge(s["proj_done"], i * 5 + 5)
                dve.tensor_copy(swa_t[:, ds(i, 1), SW0:SWA].rearrange("p a n -> p (a n)"), bank[6][:, 0:SWA - SW0]).then_inc(s["evac_v"], 1)

            dve.wait_ge(s["gain_in"], 16)
            scale_x(0, 0)
            scale_x(1, 1)
            with dve.Fori(0, 3) as j:
                for u in range(2):
                    scale_x(j * 2 + (u + 2), u)
                    evac(j * 2 + u)
            scale_x(8, 0)
            for i in (6, 7, 8):
                evac(i)

            n = NT * NH
            dve.wait_ge(s["small_in"], 16 * 15)
            dve.wait_ge(s["evac_v"], 3 * (NT + 1))
            dve.wait_ge(s["evac_s"], 2 * (NT + 1))
            z, mn = lz[:, 0:n], lz[:, n:2 * n]
            dve.tensor_tensor(z.rearrange("p (t h) -> p t h", h=NH), lf_t[:, 0:NT, :],
                              bf[:, None, :].to_broadcast([P, NT, NH]), ALU.add).then_inc(s["lf_v"], 1)
            dve.wait_ge(s["lf_v"], 1)
            dve.scalar_tensor_tensor(out=lz[:, 2 * n:3 * n], in0=z, scalar=-1.0, in1=z, op0=ALU.mult, op1=ALU.max).then_inc(s["lf_v"], 1)
            dve.wait_ge(s["lf_s"], 2)
            dve.scalar_tensor_tensor(out=lf[:, 0:n], in0=z, scalar=0.0, in1=lz[:, 2 * n:3 * n],
                                     op0=ALU.min, op1=ALU.subtract).then_inc(s["lf_v"], 1)
            dve.wait_ge(s["lf_v"], 3)
            dve.memset(lsum[:, :], 0.0).then_inc(s["lf_v"], 1)
            dve.wait_ge(s["lf_v"], 4)
            dve.tensor_copy(lsum_t[:, NT + 1, :], lf_t[:, NT, :])
            dve.tensor_tensor(lsum_t[:, SAMPLE, :], lf_t[:, NT, :], lf_t[:, NT + 1, :], ALU.add)
            for i in range(1, NP_T):
                dve.tensor_tensor(lsum_t[:, i, :], lsum_t[:, i - 1, :], lf_t[:, i - 1, :], ALU.add).then_inc(s["lf_v"], 1)
                dve.wait_ge(s["lf_v"], 4 + i)
            dve.wait_ge(s["c_mm"], 1)
            dve.tensor_scalar(negc_t[:, :, 0:NH], bank[0][:, 0:NK * NH].rearrange("p (t h) -> p t h", h=NH),
                              -1.0, None, ALU.mult).then_inc(s["c_ready"], 1)
            for u in range(2):
                dve.memset(qT[u][DH:P, :], 0.0).then_inc(s["aug_set"], 1)
                dve.memset(kT[u][DH:P, :], 0.0).then_inc(s["aug_set"], 1)
            dve.wait_ge(s["aug_set"], 4)

            def stage_k(h6, u, gi):
                _, a, b = SG[gi]
                dve.wait_ge(s["st_T"], h6 + (gi + 1))
                dve.tensor_copy(kT[u][0:DH + 1, a * P:b * P], bank[7][0:DH + 1, 0:(b - a) * P]).then_inc(s["st_copied_v"], 1)

            for gi in range(3, 6):
                stage_k(0, 0, gi)

            def fmax(it, k):
                n = nblk[STEPS[k][1]] * P
                dve.wait_ge(s["qk_done"], it * NS + (k + 1))
                dve.tensor_reduce(nm[:, k % 2:k % 2 + 1], ps[k % 2][:, 0:n], AX.X, ALU.max, negate=True).then_inc(s["nmax_done"], 1)

            def copy_a(it, k):
                n = min(nblk[STEPS[k][1]] * P, 512)
                dve.wait_ge(s["pT_a"], it * NS + (k + 1))
                dve.tensor_copy(probT[k % 2][:, 0:n], bank[4][:, 0:n]).then_inc(s["cp_a"], 1)

            def fnorm(it, k):
                u, i = STEPS[k]
                dve.reciprocal(rc[:, k % 2:k % 2 + 1], rs[:, k % 4:k % 4 + 1]).then_inc(s["recip"], 1)
                dve.wait_ge(s["recip"], it * NS + (k + 1))
                dve.wait_ge(s["pv_done"], it * NS + (k + 1))
                dve.tensor_scalar(o_all[:, i, ds(it * 2 * DH + u * DH, DH)], bank[6][:, (k % 2) * DH:(k % 2) * DH + DH],
                                  rc[:, k % 2:k % 2 + 1], None, ALU.mult).then_inc(s["o_done"], 1)

            with dve.Fori(0, NH // 2) as it:
                fmax(it, 0)
                for k in range(NS):
                    u, i = STEPS[k]
                    if k + 1 < NS:
                        fmax(it, k + 1)
                    if i in SG_AT and SG_AT[i] >= 3:
                        stage_k(it * 12 + 6 * (u + 1), 1 - u, SG_AT[i])
                    copy_a(it, k)
                    if k >= 1:
                        fnorm(it, k - 1)
                fnorm(it, NS - 1)

            pairs = sraw[:, :].rearrange("p (v g) -> p g v", v=2)
            dve.tensor_copy(sink[:, :].rearrange("p (g v) -> p g v", v=2), pairs)
            dve.tensor_scalar(nsink[:, :].rearrange("p (g v) -> p g v", v=2), pairs, -1.0, None, ALU.mult).then_inc(s["s_aug"], 1)
            dve.wait_ge(s["s_aug"], 1)
            dve.memset(skT[0][DH:P, :], 0.0).then_inc(s["s_aug"], 1)
            dve.memset(skT[1][0:DH, :], 0.0).then_inc(s["s_aug"], 1)
            for gi, (a, b) in enumerate([(0, 4), (4, 8), (8, 10)]):
                dve.wait_ge(s["s_kT"], gi + 1)
                dve.tensor_copy(skT[0][0:DH, a * P:b * P], bank[4 + gi % 2][0:DH, 0:(b - a) * P])
                dve.tensor_copy(skT[1][DH:P, a * P:b * P], bank[4 + gi % 2][DH:P, 0:(b - a) * P]).then_inc(s["s_kcp"], 1)

            def smax(it, k):
                u, i = STEPS[k]
                lo = P if i == 0 else 0
                a, q = 4 + 2 * (k % 2), 8 + 2 * (k % 2)
                n = it * NS * 2 + 2 * k
                dve.wait_ge(s["s_qk"], it * NS + (k + 1))
                if k >= 2:
                    dve.wait_ge(s["s_sexp"], it * NS + (k - 1))
                dve.tensor_reduce(nm[:, 12:14], ps[k % 2][:, 0:512].rearrange("p (v n) -> p v n", v=2)[:, :, lo:256],
                                  AX.X, ALU.max, negate=True).then_inc(s["s_nmc"], 1)
                dve.wait_ge(s["s_nmc"], n + 1)
                g2 = it * 4 + 2 * u
                dve.tensor_tensor(nm[:, a:a + 2], nm[:, 12:14], nsink[:, ds(g2, 2)], ALU.min).then_inc(s["s_nmc"], 1)
                dve.wait_ge(s["s_nmc"], n + 2)
                dve.tensor_tensor(nm[:, q:q + 2], nm[:, a:a + 2], sink[:, ds(g2, 2)], ALU.add).then_inc(s["s_nm"], 1)

            def scopy(it, k):
                if k % 2 == 0:
                    n = 2 * P if STEPS[k][1] == 0 else 4 * P
                    dve.wait_ge(s["s_pT"], it * NS + (k + 1))
                    dve.tensor_copy(sprobT[0][:, 0:n], bank[4][:, 0:n]).then_inc(s["s_cpv"], 1)

            def snorm(it, k):
                u, i = STEPS[k]
                a, q = 4 + 2 * (k % 3), 10 + 2 * (k % 3)
                n = it * NS * 2 + 2 * k
                dve.wait_ge(s["s_sexp"], it * NS + (k + 1))
                dve.tensor_tensor(rc[:, 2:4], rs[:, a:a + 2], rs[:, q:q + 2], ALU.add).then_inc(s["s_rc"], 1)
                dve.wait_ge(s["s_rc"], n + 1)
                dve.reciprocal(rc[:, 4:6], rc[:, 2:4]).then_inc(s["s_rc"], 1)
                dve.wait_ge(s["s_rc"], n + 2)
                dve.wait_ge(s["s_pv"], it * NS + (k + 1))
                o = o_all[:, i, :].rearrange("p (b g d) -> p b g d", g=4, d=DH)[:, 2:4, ds(it * 2 + u, 1), :]
                dve.tensor_tensor(o.rearrange("p b g d -> p b (g d)"),
                                  bank[6][:, (k % 2) * P:(k % 2) * P + P].rearrange("p (v d) -> p v d", v=2),
                                  rc[:, 4:6, None].to_broadcast([P, 2, DH]), ALU.mult).then_inc(s["s_od"], 1)

            with dve.Fori(0, 2) as it:
                smax(it, 0)
                for k in range(NS):
                    if k + 1 < NS:
                        smax(it, k + 1)
                    scopy(it, k)
                    if k >= 1:
                        snorm(it, k - 1)
                snorm(it, NS - 1)

            dve.wait_ge(s["s_od"], 2 * NS + 1)

            def scale_o(i, u):
                dve.wait_ge(s["o_rms"], i + 1)
                dve.reciprocal(st[:, 8 + 2 * u:10 + 2 * u], st[:, 4 + 2 * u:6 + 2 * u]).then_inc(s["o_rstd"], 1)
                dve.wait_ge(s["o_rstd"], i + 1)
                for v in range(2):
                    cols = slice(512 * v, 512 * v + 512)
                    dve.scalar_tensor_tensor(out=on[u][:, cols], in0=o_all[:, ds(i, 1), cols].rearrange("p a n -> p (a n)"),
                                             scalar=st[:, 8 + 2 * u + v:9 + 2 * u + v], in1=g1[:, cols],
                                             op0=ALU.mult, op1=ALU.mult).then_inc(s["on_done"], 1)

            def add_x(i, j, u):
                dve.wait_ge(xr_in[u], j * 16 + 16)
                dve.wait_ge(s["om_done"], i + 1)
                dve.wait_ge(s["on_done"], i * 2 + 2)
                for v in range(2):
                    cols = slice(512 * v, 512 * v + 512)
                    dve.tensor_tensor(o_all[:, ds(i, 1), cols].rearrange("p a n -> p (a n)"), bank[2 + v], xr[u][:, cols],
                                      ALU.add).then_inc(s["x2_done"], 1)

            def scale_h(i, u):
                dve.wait_ge(s["h_rms"], i + 1)
                dve.reciprocal(st[:, 14:15], st[:, 13:14]).then_inc(s["h_rstd"], 1)
                dve.wait_ge(s["h_rstd"], i + 1)
                dve.scalar_tensor_tensor(out=hh[u], in0=o_all[:, ds(i, 1), :].rearrange("p a n -> p (a n)"),
                                         scalar=st[:, 14:15], in1=g0[:, :], op0=ALU.mult, op1=ALU.mult).then_inc(s["h_done"], 1)

            scale_o(0, 0)
            scale_o(1, 1)
            dve.wait_ge(s["g_late_in"], 16)
            with dve.Fori(0, 3) as j:
                for u in range(2):
                    scale_o(j * 2 + (u + 2), u)
                    add_x(j * 2 + u, j, u)
                    scale_h(j * 2 + u, u)
            scale_o(8, 0)
            for i in (6, 7, 8):
                add_x(i, i // 2, i % 2)
                scale_h(i, i % 2)

            cnt = [0]

            def link(ins):
                cnt[0] += 1
                ins.then_inc(s["r_step"], 1)
                dve.wait_ge(s["r_step"], cnt[0])

            dve.wait_ge(s["r_done"], NT)
            dve.wait_ge(s["h_out_a"], 16 * 5)
            dve.wait_ge(s["h_out_b"], 16 * 4)
            link(dve.tensor_tensor(logit_t, bank[6][:, 0:NT * (GRP + NE)].rearrange("p (t e) -> p t e", t=NT),
                                   br[:, None, :].to_broadcast([P, NT, GRP + NE]), ALU.add))
            iota = cr[:, 0:NE]
            lg, le = logit_t[:, :, 0:GRP], logit_t[:, :, GRP:GRP + NE]

            def first_max(val, n, m, idx_, eq, oh):
                link(dve.tensor_reduce(m, val, AX.X, ALU.max))
                link(dve.tensor_tensor(eq, val, m[:, :, None].to_broadcast([P, NT, n]), ALU.is_equal))
                link(dve.scalar_tensor_tensor(out=eq, in0=eq, scalar=-64.0, in1=iota[:, None, 0:n].to_broadcast([P, NT, n]),
                                              op0=ALU.mult, op1=ALU.add))
                link(dve.tensor_reduce(idx_, eq, AX.X, ALU.min))
                link(dve.tensor_tensor(oh, eq, idx_[:, :, None].to_broadcast([P, NT, n]), ALU.is_equal))

            first_max(lg, GRP, small["m0"], small["i0"], rt["eqg"], rt["ohg"])
            dve.tensor_tensor(rt["lg"], lg, small["m0"][:, :, None].to_broadcast([P, NT, GRP]), ALU.subtract).then_inc(s["r_exp"], 1)
            link(dve.tensor_scalar(rt["ohg"], rt["ohg"], BIG, -BIG, ALU.mult, ALU.add))
            link(dve.tensor_tensor(rt["lem"].rearrange("p t (g e) -> p t g e", g=GRP), le.rearrange("p t (g e) -> p t g e", g=GRP),
                                   rt["ohg"][:, :, :, None].to_broadcast([P, NT, GRP, EPG]), ALU.add))
            first_max(rt["lem"], NE, small["m1"], small["i1"], rt["eq"], rt["oh1"])
            link(dve.scalar_tensor_tensor(out=rt["lem"], in0=rt["oh1"], scalar=-2 * BIG, in1=rt["lem"], op0=ALU.mult, op1=ALU.add))
            first_max(rt["lem"], NE, small["m2"], small["i2"], rt["eq"], rt["oh2"])
            valid = cr[:, NE:NE + NT]
            link(dve.tensor_tensor(rt["tmp"], rt["oh1"], rt["oh2"], ALU.add))
            link(dve.tensor_tensor(maskb[:, :].rearrange("p (t e) -> p t e", t=NT), rt["tmp"],
                                   valid[:, :, None].to_broadcast([P, NT, NE]), ALU.mult))
            runb_t = runb[:, :].rearrange("p (t e) -> p t e", t=NT)
            maskb_t = maskb[:, :].rearrange("p (t e) -> p t e", t=NT)
            link(dve.memset(runb[:, :], 0.0))
            for i in range(1, NT):
                link(dve.tensor_tensor(runb_t[:, i, :], runb_t[:, i - 1, :], maskb_t[:, i - 1, :], ALU.add))
            dve.sem_inc(s["r_mask"], 1)
            link(dve.tensor_tensor(small["m2"], small["m2"], small["m1"], ALU.subtract))
            dve.wait_ge(s["r_exp"], 2)
            link(dve.tensor_reduce(small["den"], rt["eqg"], AX.X, ALU.add))
            dve.sem_inc(s["r_exp"], 1)
            dve.wait_ge(s["r_exp"], 4)
            link(dve.tensor_scalar(small["pg"], small["e21"], 1.0, None, ALU.add))
            link(dve.tensor_tensor(small["den"], small["den"], small["pg"], ALU.mult))
            link(dve.reciprocal(wgt[:, 0:NT], small["den"]))
            link(dve.tensor_tensor(wgt[:, NT:2 * NT], wgt[:, 0:NT], small["e21"], ALU.mult))
            dve.wait_ge(s["r_mm"], 2)
            link(dve.tensor_copy(rt["rank"].rearrange("p t e -> p (t e)"), bank[0][:, 0:NT * NE]))
            cntp = bank[1][:, 0:NE]
            link(dve.tensor_scalar(nov[:, 0, :], cntp, -1.0, 0.0, ALU.add, ALU.max))
            link(dve.tensor_copy(ovi[:, 0:NE], nov[:, 0, :]))
            link(dve.tensor_scalar(ovi[:, NE:2 * NE], ovi[:, 0:NE], 7, None, ALU.logical_shift_right))
            link(dve.tensor_copy(nov[:, 1, :], ovi[:, NE:2 * NE]))
            cur = 1
            for b in range(5):
                sh = 1 << b
                nxt = 2 + b % 2
                link(dve.tensor_copy(nov[:, nxt, :], nov[:, cur, :]))
                link(dve.tensor_tensor(nov[:, nxt, sh:NE], nov[:, cur, sh:NE], nov[:, cur, 0:NE - sh], ALU.add))
                cur = nxt
            incl = nov[:, cur, :]
            link(dve.tensor_tensor(nov[:, 4, :], incl, nov[:, 1, :], ALU.subtract))
            link(dve.scalar_tensor_tensor(out=nov[:, 5, :], in0=nov[:, 4, :], scalar=float(NE - 1), in1=iota,
                                          op0=ALU.add, op1=ALU.subtract))
            link(dve.tensor_copy(qi, rt["rank"].rearrange("p t e -> p (t e)")))
            link(dve.tensor_scalar(qi, qi, 7, None, ALU.logical_shift_right))
            link(dve.tensor_copy(rt["q"].rearrange("p t e -> p (t e)"), qi))
            link(dve.tensor_scalar(rt["tmp"], rt["rank"], float(NTILES), None, ALU.mult))
            link(dve.scalar_tensor_tensor(out=rt["tmp"], in0=rt["q"], scalar=float(1 - P * NTILES), in1=rt["tmp"],
                                          op0=ALU.mult, op1=ALU.add))
            link(dve.tensor_tensor(rt["pos"], rt["tmp"], iota[:, None, :].to_broadcast([P, NT, NE]), ALU.add))
            link(dve.tensor_scalar(rt["q"], rt["q"], 1.0, None, ALU.min))
            link(dve.tensor_tensor(rt["tmp"], rt["q"], nov[:, 5, None, :].to_broadcast([P, NT, NE]), ALU.mult))
            link(dve.tensor_tensor(rt["pos"], rt["pos"], rt["tmp"], ALU.add))
            link(dve.tensor_scalar(small["m0"], valid, float(-SKIP), float(SKIP), ALU.mult, ALU.add))
            for c, oh in enumerate(("oh1", "oh2")):
                link(dve.tensor_tensor(rt[oh], rt[oh], rt["pos"], ALU.mult))
                link(dve.tensor_reduce(small["p1"], rt[oh], AX.X, ALU.add))
                link(dve.tensor_tensor(dest[:, :].rearrange("p (t c) -> p t c", c=2)[:, :, c], small["p1"], small["m0"], ALU.add))
            dve.sem_inc(s["r_mask"], 1)
            link(dve.tensor_tensor(ovc, incl[:, None, :].to_broadcast([P, NOVER, NE]),
                                   iota[:, 0:NOVER, None].to_broadcast([P, NOVER, NE]), ALU.is_le))
            link(dve.tensor_reduce(ovf, ovc, AX.X, ALU.add))
            link(dve.tensor_scalar(ovf, ovf, float(NE - 1), None, ALU.min))
            link(dve.tensor_copy(over[0:1, 1:NOVER + 1], ovf[0:1, :]))
            link(dve.tensor_copy(over[0:1, 0:1], incl[0:1, NE - 1:NE]))
            dve.sem_inc(s["r_mask"], 1)

            def copy_gT(tt, u):
                dve.wait_ge(s["gT_done"], tt * 2 + 2)
                if not (isinstance(tt, int) and tt < 2):
                    dve.wait_ge(s["gu_done"], tt - 1)
                dve.tensor_copy(hgT[u][:, 4:8, :], bank[1].rearrange("p (c k) -> p c k", c=4)).then_inc(s["gT_cv"], 1)

            def gate(tt, u):
                dve.wait_ge(s["e_done"], tt + 1)
                dve.tensor_scalar(ex["s"][u], ex["e"][u], 1.0, None, ALU.add).then_inc(s["ev_step"], 1)
                dve.wait_ge(s["ev_step"], tt * 3 + 1)
                dve.reciprocal(ex["r"][u], ex["s"][u]).then_inc(s["ev_step"], 1)
                dve.wait_ge(s["ev_step"], tt * 3 + 2)
                dve.tensor_tensor(ex["a"][u], ex["r"][u], bank[2 + u][:, 0:FE], ALU.mult).then_inc(s["ev_step"], 1)
                dve.wait_ge(s["ev_step"], tt * 3 + 3)
                dve.tensor_tensor(ex["hid"][u], ex["a"][u], bank[2 + u][:, FE:2 * FE], ALU.mult).then_inc(s["hid_done"], 1)

            def copy_y(tt, u):
                dve.wait_ge(s["dn_done"], tt + 1)
                if not (isinstance(tt, int) and tt < 2):
                    dve.wait_ge(y_out[u], (tt - u) * 8)
                dve.tensor_copy(yo[u][:, 512:D], bank[5]).then_inc(s["y_cv"], 1)

            copy_gT(0, 0)
            copy_gT(1, 1)
            gate(0, 0)

            def estep(tt, u, last=2):
                if last >= 1:
                    gate(tt + 1, 1 - u)
                if last >= 2:
                    copy_gT(tt + 2, u)
                copy_y(tt, u)

            estep(0, 0)
            estep(1, 1)
            with dve.Fori(1, NE // 2 - 1) as j:
                for u in range(2):
                    estep(j * 2 + u, u)
            estep(NE - 2, 0, 1)
            estep(NE - 1, 1, 0)

            n_over = dve.value_load(over[0:1, 0:1], min_val=0, max_val=NOVER)
            with dve.Fori(0, NOVER) as k:
                with dve.If(k < n_over):
                    dve.wait_ge(s["v_gT"], k * 2 + 2)
                    dve.tensor_copy(hgT[0][:, 4:8, :], bank[1].rearrange("p (c k) -> p c k", c=4)).then_inc(s["v_gTc"], 1)
                    dve.wait_ge(s["v_e"], k + 1)
                    dve.tensor_scalar(ex["s"][0], ex["e"][0], 1.0, None, ALU.add).then_inc(s["v_s"], 1)
                    dve.wait_ge(s["v_s"], k * 3 + 1)
                    dve.reciprocal(ex["r"][0], ex["s"][0]).then_inc(s["v_s"], 1)
                    dve.wait_ge(s["v_s"], k * 3 + 2)
                    dve.tensor_tensor(ex["a"][0], ex["r"][0], bank[2][:, 0:FE], ALU.mult).then_inc(s["v_s"], 1)
                    dve.wait_ge(s["v_s"], k * 3 + 3)
                    dve.tensor_tensor(ex["hid"][0], ex["a"][0], bank[2][:, FE:2 * FE], ALU.mult).then_inc(s["v_hid"], 1)
                    dve.wait_ge(s["v_dn"], k + 2)
                    dve.tensor_copy(yo[0][:, 512:D], bank[5]).then_inc(s["v_y"], 1)

            def add_y(i, j, u, rows):
                dve.wait_ge(y_in[u], j * 32 + 32)
                o = o_all[0:rows, ds(i, 1), :].rearrange("p a n -> p (a n)")
                dve.scalar_tensor_tensor(out=o, in0=ya[u][0:rows, :], scalar=wgt[0:rows, ds(i, 1)], in1=o,
                                         op0=ALU.mult, op1=ALU.add).then_inc(s["f_acc"], 1)
                dve.wait_ge(s["f_acc"], i * 2 + 1)
                dve.scalar_tensor_tensor(out=o, in0=yb[u][0:rows, :], scalar=wgt[0:rows, ds(i + NT, 1)], in1=o,
                                         op0=ALU.mult, op1=ALU.add).then_inc(s["f_acc"], 1)

            def scale_f(i, u, rows):
                dve.wait_ge(s["f_rms"], i + 1)
                dve.reciprocal(st[0:rows, 4 + u:5 + u], st[0:rows, 2 + u:3 + u]).then_inc(s["f_rstd"], 1)
                dve.wait_ge(s["f_rstd"], i + 1)
                dve.scalar_tensor_tensor(out=fin[u][0:rows, :], in0=o_all[0:rows, ds(i, 1), :].rearrange("p a n -> p (a n)"),
                                         scalar=st[0:rows, 4 + u:5 + u], in1=g1[0:rows, :],
                                         op0=ALU.mult, op1=ALU.mult).then_inc(s["f_fin"], 1)

            dve.wait_ge(s["g_late_in"], 32)
            add_y(0, 0, 0, P)
            with dve.Fori(0, NP_T // 2 - 1) as j:
                add_y(j * 2 + 1, j, 1, P)
                scale_f(j * 2, 0, P)
                add_y(j * 2 + 2, j + 1, 0, P)
                scale_f(j * 2 + 1, 1, P)
            add_y(7, 3, 1, P)
            scale_f(6, 0, P)
            add_y(8, 4, 0, DEC)
            scale_f(7, 1, P)
            scale_f(8, 0, DEC)

        @block.tensor
        def _(pe):
            pe.wait_ge(s["const_in"], 16)

            def transpose_x(i, u):
                pe.wait_ge(s["xn_done"], i + 1)
                if not (isinstance(i, int) and i < 1):
                    pe.wait_ge(s["xT_copied"], i * 2)
                src = xn[u].rearrange("p (k c) -> p c k", c=C)
                for c in range(C):
                    mm = pe.transpose(bank[c // 4][:, (c % 4) * P:(c % 4) * P + P], src[:, c, :], ident)
                    if c % 4 == 3:
                        mm.then_inc(s["xT_done"], 1)

            def project(i, u, first=False):
                pe.wait_ge(s["xT_copied"], i * 2 + 2)
                for n in range(5):
                    if first:
                        pe.wait_ge(win_in[n], 16)
                    if n % 2 == 0:
                        pe.wait_ge(s["evac_v"], i * 3 + (n // 2 + 1))
                    else:
                        pe.wait_ge(s["evac_s"], i * 2 + (n // 2 + 1))
                    w = COLS[n + 1] - COLS[n]
                    for c in range(C):
                        mm = pe.matmul(bank[2 + n][:, 0:w], xT[u][:, c, :], w_in[:, c, COLS[n]:COLS[n + 1]],
                                       start=(c == 0), stop=(c == C - 1))
                    mm.then_inc(s["proj_done"], 1)

            transpose_x(0, 0)
            transpose_x(1, 1)
            project(0, 0, True)
            with pe.Fori(0, 3) as j:
                transpose_x(j * 2 + 2, 0)
                project(j * 2 + 1, 1)
                transpose_x(j * 2 + 3, 1)
                project(j * 2 + 2, 0)
            transpose_x(8, 0)
            project(7, 1)
            project(8, 0)

            pe.wait_ge(s["lf_v"], 4 + NP_T - 1)
            pe.matmul(bank[0][:, 0:NK * NH], upto, lf[:, :], start=True, stop=False)
            pe.matmul(bank[0][:, 0:NK * NH], ones, lsum[:, :], start=False, stop=True).then_inc(s["c_mm"], 1)

            def stage(h1, h6, c3, gi):
                kind, a, b = SG[gi]
                if gi == 0:
                    pe.wait_ge(s["kv_staged"], h1)
                if gi == 0:
                    if not (isinstance(c3, int) and c3 == 0):
                        pe.wait_ge(s["st_copied_v"], c3)
                elif gi <= 3:
                    pe.wait_ge(s["st_copied_s"], c3 + gi)
                else:
                    pe.wait_ge(s["st_copied_v"], c3 + (gi - 3))
                src = qst if kind == "q" else kst
                for m in range(a, b):
                    mm = pe.transpose(bank[7][0:DH + 1, (m - a) * P:(m - a + 1) * P], src[:, m, :], ident)
                mm.then_inc(s["st_T"], 1)

            for gi in range(6):
                stage(1, 0, 0, gi)

            def fqk(it, k):
                u, i = STEPS[k]
                if i == 0:
                    pe.wait_ge(s["st_copied_s"], it * 6 + 3 * (u + 1))
                    pe.wait_ge(s["st_copied_v"], it * 6 + 3 * (u + 1))
                pe.wait_ge(s["exp_done"], it * NS + (k + 1))
                n = nblk[i] * P
                q = qT[u][:, i * P:(i + 1) * P]
                if i < SAMPLE:
                    spans = [(0, 0, min(n, 512))] + ([(512, 512, n - 512)] if n > 512 else [])
                    dg = i * P
                else:
                    spans = [(0, NT * P, PAST), (PAST, SAMPLE * P, P)]
                    dg = PAST
                for at_, k0, w in spans:
                    pe.matmul(ps[k % 2][:, at_:at_ + w], q, kT[u][:, k0:k0 + w], start=(at_ % 512 == 0), stop=False,
                              skip_group_check=True)
                pe.matmul(ps[k % 2][:, dg:dg + P], identb, causal, start=False, stop=True,
                          skip_group_check=True).then_inc(s["qk_done"], 1)

            def ftrans(it, k):
                u, i = STEPS[k]
                nb = nblk[i]
                pe.wait_ge(s["exp_done"], it * NS + (k + 3))
                if k >= 1:
                    pe.wait_ge(s["cp_a"], it * NS + k)
                for b in range(nb):
                    if b == 4:
                        seen = sum(nblk[STEPS[m][1]] > 4 for m in range(k))
                        pe.wait_ge(s["cp_b"], it * 2 * len(TWO) + (seen + 1))
                    mm = pe.transpose(bank[4 + b // 4][:, (b % 4) * P:(b % 4) * P + P], prob[k % 2][:, b * P:(b + 1) * P], ident)
                    if b == min(nb, 4) - 1:
                        mm.then_inc(s["pT_a"], 1)
                if nb > 4:
                    mm.then_inc(s["pT_b"], 1)

            def fpv(it, k):
                u, i = STEPS[k]
                nb = nblk[i]
                pe.wait_ge(s["cp_a"], it * NS + (k + 1))
                if nb > 4:
                    seen = sum(nblk[STEPS[m][1]] > 4 for m in range(k + 1))
                    pe.wait_ge(s["cp_b"], it * 2 * len(TWO) + (seen + 1))
                pe.wait_ge(s["o_done"], it * NS + (k + 1))
                for b in range(nb):
                    m = keytile(i, b)
                    if m < NT:
                        v = fox_t[:, m, ds(it * 2 * DH + (2 * NH * DH + u * DH), DH)]
                    else:
                        v = cv[:, m - NT, ds(it * 2 * DH + u * DH, DH)]
                    mm = pe.matmul(bank[6][:, (k % 2) * DH:(k % 2) * DH + DH], probT[k % 2][:, b * P:(b + 1) * P], v,
                                   start=(b == 0), stop=(b == nb - 1))
                mm.then_inc(s["pv_done"], 1)

            with pe.Fori(0, NH // 2) as it:
                fqk(it, 0)
                for k in range(NS):
                    u, i = STEPS[k]
                    if k + 1 < NS:
                        fqk(it, k + 1)
                    if i in SG_AT:
                        stage(it * 2 + (u + 2), None, it * 6 + 3 * (u + 1), SG_AT[i])
                    ftrans(it, k)
                    if k >= 1:
                        fpv(it, k - 1)
                fpv(it, NS - 1)

            pe.wait_ge(s["o_done"], 4 * NS + 1)
            for gi, (a, b) in enumerate([(0, 4), (4, 8), (8, 10)]):
                if gi == 2:
                    pe.wait_ge(s["s_kcp"], 1)
                for m in range(a, b):
                    src = swa_t[:, m, NH * DH:NH * DH + 2 * DH] if m < NT else skv[:, 0:2 * DH]
                    mm = pe.transpose(bank[4 + gi % 2][:, (m - a) * P:(m - a + 1) * P], src, ident)
                mm.then_inc(s["s_kT"], 1)

            def s_stage(g1_, c3, gi):
                a, b = SSG[gi]
                if gi == 0:
                    pe.wait_ge(s["s_staged"], g1_)
                if not (isinstance(c3, int) and c3 + gi == 0):
                    pe.wait_ge(s["s_qT_cp"], c3 + gi)
                for m in range(a, b):
                    mm = pe.transpose(bank[7][:, (m - a) * P:(m - a + 1) * P], sqst[:, m, :], ident)
                mm.then_inc(s["s_qT_T"], 1)

            for gi in range(3):
                s_stage(1, 0, gi)
            pe.wait_ge(s["s_kcp"], 3)
            pe.wait_ge(s["s_aug"], 3)

            def sqk(it, k):
                u, i = STEPS[k]
                if i == 0:
                    pe.wait_ge(s["s_qT_cp"], it * 6 + 3 * (u + 1))
                if k >= 2:
                    pe.wait_ge(s["s_exp"], it * NS * 2 + 2 * (k - 1))
                for v in range(2):
                    for b in range(1 if i == 0 else 0, 2):
                        m = skeytile(i, b)
                        pe.matmul(ps[k % 2][:, v * 256 + b * P:v * 256 + (b + 1) * P], sqT[u][:, i * P:(i + 1) * P],
                                  skT[v][:, m * P:(m + 1) * P], start=(v == 0 and b == (1 if i == 0 else 0)), stop=False,
                                  skip_group_check=True)
                lo = P if i == 0 else 0
                bias = alibi[:, ds(it * 4 * 256 + u * 2 * 256, 512)].rearrange("p (v n) -> p v n", v=2)[:, :, lo:256]
                pe.matmul(ps[k % 2][:, 0:512].rearrange("p (v n) -> p v n", v=2)[:, :, lo:256], identb, bias,
                          start=False, stop=True, skip_group_check=True).then_inc(s["s_qk"], 1)

            def strans(it, k):
                u, i = STEPS[k]
                pe.wait_ge(s["s_exp"], it * NS * 2 + 2 * (k + 1))
                if k >= 2:
                    pe.wait_ge(s["s_cps"] if k % 2 else s["s_cpv"], it * (NS // 2) + k // 2)
                n = 0
                for v in range(2):
                    for b in range(1 if i == 0 else 0, 2):
                        mm = pe.transpose(bank[4 + k % 2][:, n * P:(n + 1) * P], sprob[k % 2][:, v, b * P:(b + 1) * P], ident)
                        n += 1
                mm.then_inc(s["s_pT"], 1)

            def spv(it, k):
                u, i = STEPS[k]
                if k % 2 == 0:
                    pe.wait_ge(s["s_cpv"], it * (NS // 2) + (k // 2 + 1))
                else:
                    pe.wait_ge(s["s_cps"], it * (NS // 2) + (k // 2 + 1))
                pe.wait_ge(s["s_od"], it * NS + (k + 1))
                n = 0
                for v in range(2):
                    for b in range(1 if i == 0 else 0, 2):
                        m = skeytile(i, b)
                        val = swa_t[:, m, NH * DH + (2 + v) * DH:NH * DH + (3 + v) * DH] if m < NT else skv[:, (2 + v) * DH:(3 + v) * DH]
                        mm = pe.matmul(bank[6][:, (k % 2) * P + v * DH:(k % 2) * P + (v + 1) * DH],
                                       sprobT[k % 2][:, n * P:(n + 1) * P], val,
                                       start=(b == (1 if i == 0 else 0)), stop=(b == 1))
                        n += 1
                mm.then_inc(s["s_pv"], 1)

            with pe.Fori(0, 2) as it:
                sqk(it, 0)
                for k in range(NS):
                    u, i = STEPS[k]
                    if k + 1 < NS:
                        sqk(it, k + 1)
                    if i in SSG_AT:
                        s_stage(it * 2 + (u + 2), it * 6 + 3 * (u + 1), SSG_AT[i])
                    strans(it, k)
                    if k >= 1:
                        spv(it, k - 1)
                spv(it, NS - 1)

            def transpose_o(i, u):
                pe.wait_ge(s["on_done"], i * 2 + 2)
                if not (isinstance(i, int) and i < 1):
                    pe.wait_ge(s["oT_copied"], i * 2)
                for c in range(C):
                    mm = pe.transpose(bank[c // 4][:, (c % 4) * P:(c % 4) * P + P], on[u][:, c * P:(c + 1) * P], ident)
                    if c % 4 == 3:
                        mm.then_inc(s["oT_done"], 1)

            def out_proj(i, u):
                pe.wait_ge(s["oT_copied"], i * 2 + 2)
                if not (isinstance(i, int) and i < 1):
                    pe.wait_ge(s["x2_done"], i * 2)
                for n in range(2):
                    for c in range(C):
                        mm = pe.matmul(bank[2 + n], oT[u][:, c, :], w_out[:, c, 512 * n:512 * n + 512],
                                       start=(c == 0), stop=(c == C - 1))
                mm.then_inc(s["om_done"], 1)

            def transpose_h(i, u):
                pe.wait_ge(s["h_done"], i + 1)
                if not (isinstance(i, int) and i < 1):
                    pe.wait_ge(s["hT_copied"], i * 2)
                src = hh[u].rearrange("p (k c) -> p c k", c=C)
                for c in range(C):
                    mm = pe.transpose(bank[4 + c // 4][:, (c % 4) * P:(c % 4) * P + P], src[:, c, :], ident)
                    if c % 4 == 3:
                        mm.then_inc(s["hT_done"], 1)

            def router(i):
                pe.wait_ge(s["hT_copied"], i * 2 + 2)
                for c in range(C):
                    mm = pe.matmul(bank[6][:, ds(i * (GRP + NE), GRP + NE)], hhT[:, c, :], wr_t[:, c, :],
                                   start=(c == 0), stop=(c == C - 1))
                mm.then_inc(s["r_done"], 1)

            pe.wait_ge(s["s_od"], 2 * NS + 1)
            transpose_o(0, 0)
            pe.wait_ge(s["w_out_in"], 16)
            transpose_o(1, 1)
            out_proj(0, 0)
            with pe.Fori(0, 3) as j:
                for u in range(2):
                    transpose_o(j * 2 + (u + 2), u)
                    out_proj(j * 2 + (u + 1), 1 - u)
                    transpose_h(j * 2 + u, u)
                    router(j * 2 + u)
            transpose_o(8, 0)
            out_proj(7, 1)
            transpose_h(6, 0)
            router(6)
            out_proj(8, 0)
            transpose_h(7, 1)
            router(7)
            transpose_h(8, 0)
            router(8)

            pe.wait_ge(s["r_mask"], 1)
            pe.matmul(bank[0][:, 0:NT * NE], before, maskb[:, :], start=True, stop=False)
            pe.matmul(bank[0][:, 0:NT * NE], onesb, runb[:, :], start=False, stop=True).then_inc(s["r_mm"], 1)
            pe.matmul(bank[1][:, 0:NE], onesb, runb[:, (NT - 1) * NE:NT * NE], start=True, stop=False)
            pe.matmul(bank[1][:, 0:NE], onesb, maskb[:, (NT - 1) * NE:NT * NE], start=False, stop=True).then_inc(s["r_mm"], 1)

            def transpose_g(u, sig):
                src = hg[u].rearrange("p (k c) -> p c k", c=C)
                for c in range(C):
                    mm = pe.transpose(bank[c // 4][:, (c % 4) * P:(c % 4) * P + P], src[:, c, :], ident)
                    if c % 4 == 3:
                        mm.then_inc(sig, 1)

            def gate_up(u, w, sig):
                wv = w[:, 0:2 * D].rearrange("p (m c f) -> p c m f", m=2, c=C)
                for c in range(C):
                    mm = pe.matmul(bank[2 + u][:, 0:2 * FE].rearrange("p (m f) -> p m f", m=2), hgT[u][:, c, :], wv[:, c, :, :],
                                   start=(c == 0), stop=(c == C - 1))
                mm.then_inc(sig, 1)

            def down(u, w, sig):
                for n in range(2):
                    mm = pe.matmul(bank[4 + n], ex["hidT"][u], w[:, 2 * D + 512 * n:2 * D + 512 * n + 512], start=True, stop=True)
                mm.then_inc(sig, 1)

            def tg(tt, j, k):
                pe.wait_ge(g_in[k], j * 16 + 16)
                if not (isinstance(tt, int) and tt < 1):
                    pe.wait_ge(s["gT_cs"], tt)
                    pe.wait_ge(s["gT_cv"], tt)
                transpose_g(k, s["gT_done"])

            def gu(tt, j, k):
                u = k % 2
                if k == NSLOT - 1:
                    pe.wait_ge(w_in_slot[k], j * 48) if not isinstance(j, int) or j > 0 else pe.wait_ge(s["small_in"], 16 * 15)
                else:
                    pe.wait_ge(w_in_slot[k], j * 48 + 48)
                pe.wait_ge(s["gT_cs"], tt + 1)
                pe.wait_ge(s["gT_cv"], tt + 1)
                if not (isinstance(tt, int) and tt < 2):
                    pe.wait_ge(s["hid_done"], tt - 1)
                gate_up(u, wslot[k], s["gu_done"])

            def hd(tt, k):
                u = k % 2
                pe.wait_ge(s["hid_done"], tt + 1)
                if not (isinstance(tt, int) and tt < 1):
                    pe.wait_ge(s["hidT_cp"], tt)
                pe.transpose(bank[6][:, 0:P], ex["hid"][u], ident).then_inc(s["hidT_done"], 1)

            def dn(tt, k):
                pe.wait_ge(s["hidT_cp"], tt + 1)
                if not (isinstance(tt, int) and tt < 1):
                    pe.wait_ge(s["y_cs"], tt)
                    pe.wait_ge(s["y_cv"], tt)
                down(k % 2, wslot[k], s["dn_done"])

            def estep(tt, j4, k, last=2):
                if last >= 1:
                    gu(tt + 1, j4 + (k + 1) // NSLOT, (k + 1) % NSLOT)
                hd(tt, k)
                if last >= 2:
                    tg(tt + 2, j4 + (k + 2) // 4, (k + 2) % 4)
                dn(tt, k)

            pe.wait_ge(s["r_mask"], 3)
            tg(0, 0, 0)
            tg(1, 0, 1)
            gu(0, 0, 0)
            for tt in range(4):
                estep(tt, 0, tt)
            with pe.Fori(1, NE // NSLOT - 1) as j:
                for k in range(NSLOT):
                    estep(j * NSLOT + k, j, k)
            for tt in range(NE - NSLOT, NE):
                estep(tt, tt // NSLOT, tt % NSLOT, min(2, NE - 1 - tt))

            pe.sem_inc(s["v_dn"], 1)
            n_over = pe.value_load(over[0:1, 0:1], min_val=0, max_val=NOVER)
            with pe.Fori(0, NOVER) as k:
                with pe.If(k < n_over):
                    pe.wait_ge(s["v_g"], k * 16 + 16)
                    transpose_g(0, s["v_gT"])
                    pe.wait_ge(s["v_gTc"], k * 2 + 2)
                    pe.wait_ge(s["v_w"], k * 48 + 48)
                    gate_up(0, wslot[0], s["v_gu"])
                    pe.wait_ge(s["v_hid"], k + 1)
                    pe.transpose(bank[6][:, 0:P], ex["hid"][0], ident).then_inc(s["v_hT"], 1)
                    pe.wait_ge(s["v_hTc"], k + 1)
                    down(0, wslot[0], s["v_dn"])
            pe.wait_ge(s["experts_done"], 1)


_INS = ['x_prompt', 'x_sample', 'cache_fox_k', 'cache_fox_v', 'cache_fox_logf', 'cache_swa_k', 'cache_swa_v',
        'g_mix_norm', 'w_in', 'b_forget', 'swa_sinks', 'g_fox_out', 'g_swa_out', 'w_out', 'g_ffn_norm',
        'w_router_group', 'b_router_group', 'w_router_expert', 'b_router_expert', 'w_gate', 'w_up', 'w_down', 'g_final']
_OUTS = [('y_prompt', (1, SEQ, D)), ('y_sample', (1, DEC, D)),
         ('fox_k_prompt', (1, 1, SEQ, NH, DH)), ('fox_v_prompt', (1, 1, SEQ, NH, DH)), ('fox_logf_prompt', (1, 1, SEQ, NH)),
         ('swa_k_prompt', (1, 1, WIN, 2, DH)), ('swa_v_prompt', (1, 1, WIN, 2, DH)),
         ('fox_k_sample', (1, 1, DEC, NH, DH)), ('fox_v_sample', (1, 1, DEC, NH, DH)), ('fox_logf_sample', (1, 1, DEC, NH)),
         ('swa_k_sample', (1, 1, DEC, 2, DH)), ('swa_v_sample', (1, 1, DEC, 2, DH))]


def constants():
    r = np.arange(P)
    const_f = np.concatenate([np.eye(P), r[:, None] <= r[None, :], np.ones((P, P))], axis=1).astype(np.float32)
    causal = np.where(r[None, :] <= r[:, None], 0.0, -BIG)
    k = np.arange(2 * P)
    dist = np.abs(r[:, None] + P - k[None, :])
    behind = r[:, None] // 64 + 2 - k[None, :] // 64
    seen = (behind >= 0) & (behind <= 2)
    slope = 2.0 ** -(np.arange(NH) + 1.0)
    bias = np.where(seen[:, None, :], -slope[None, :, None] * dist[:, None, :], -BIG)
    bias = bias.reshape(P, 2, 4, 2 * P).transpose(0, 2, 1, 3).reshape(P, 2 * NH * P)
    const_b = np.concatenate([np.eye(P), causal, r[:, None] < r[None, :], np.ones((P, P)), bias], axis=1).astype(mybir.dt.np(BF16))
    tok = np.arange(NT)[None, :, None] * P + r[:, None, None]
    const_i = np.stack([np.broadcast_to(tok, (P, NT, 2)), tok + TOK * np.arange(2)[None, None, :]], axis=-1)
    const_i = const_i.reshape(P, NT * 4).astype(np.int32)
    exists = (np.arange(NT)[None, :] * P + r[:, None]) < SEQ + DEC
    const_r = np.concatenate([np.broadcast_to(np.arange(NE), (P, NE)), exists], axis=1).astype(np.float32)
    return {"const_f": const_f, "const_b": const_b, "const_i": const_i, "const_r": const_r}


def kernel(**inputs):
    import concourse.bacc as _bacc
    from concourse.bass_utils import run_bass_kernel_spmd as _run

    nc = _bacc.Bacc("TRN2", target_bir_lowering=False, num_devices=1)
    arrays, t = {}, {}
    for name, a in [(n, inputs[n]) for n in _INS] + list(constants().items()):
        a = np.ascontiguousarray(a)
        arrays[f"in_{name}"] = a
        t[name] = nc.dram_tensor(f"in_{name}", a.shape, mybir.dt.from_np(a.dtype), kind="ExternalInput").ap()
    for name, shape in _OUTS:
        t[name] = nc.dram_tensor(f"out_{name}", shape, F32, kind="ExternalOutput").ap()
    build(nc, t)
    r = _run(nc, [arrays], core_ids=[0])
    return tuple(r.results[0][f"out_{name}"] for name, _ in _OUTS)
```

```python
from contextlib import ExitStack

import concourse.bass as bass
import numpy as np
from concourse import mybir

F32 = mybir.dt.float32
F32R = mybir.dt.float32r
BF16 = mybir.dt.bfloat16
I32 = mybir.dt.int32
ALU = mybir.AluOpType
ACT = mybir.ActivationFunctionType
AX = mybir.AxisListType

P = 128
D = 1024
C = D // P
SEQ, DEC, PAST, WIN = 1024, 64, 256, 128
NP_T = SEQ // P
NT = NP_T + 1
SAMPLE = NP_T
NK = NT + PAST // P
DH = 64
NH = 8
QKV = 3 * NH * DH
SWA = NH * DH + 2 * 2 * DH
PROJ = QKV + NH + SWA
GRP, EPG = 4, 8
NE = GRP * EPG
FE = 128
NOVER = 2 * NT * P // P - 2
NTILES = NE + NOVER
TOK = NT * P
SCALE = DH ** -0.5
EPS = 1e-6
BIG = 1.0e30
SKIP = 1 << 20
WSLOT = 3 * D
NSLOT = 4
WG = 256
NG = (PROJ - NH) // WG
FOX_G = QKV // WG


def build(nc, t):
    ctx = ExitStack()
    with ctx:
        def sb(name, shape, dt=F32):
            return ctx.enter_context(nc.sbuf_tensor(name, shape, dt))

        def sem(name):
            return ctx.enter_context(nc.semaphore(name))

        ds = bass.ds

        def sb_at(name, shape):
            at_ = -(-nc.sbuf_base // 32) * 32
            return sb(name, shape), at_

        def rounded(name, base, first, *shape):
            n_ = int(np.prod(shape))
            r = nc.alloc_sbuf_tensor_at(name, [P, n_], F32R, offset=base + 4 * first)
            return r[:, :] if len(shape) == 1 else r[:, :].rearrange("p (a b) -> p a b", b=shape[1])

        def cut(region, at, *shape):
            n = int(np.prod(shape))
            ap = region[:, at:at + n]
            if len(shape) == 2:
                ap = ap.rearrange("p (a b) -> p a b", b=shape[1])
            return ap

        big, big_at = sb_at("big", [P, C * PROJ])
        xh = rounded("xh", big_at, 0, NT * C, P)
        xl = rounded("xl", big_at, NT * D, NT * C, P)
        wf_raw, wf_lo = cut(big, 2 * NT * D, C, NH), rounded("wf_lo", big_at, 2 * NT * D, C, NH)
        assert 2 * NT * D + C * NH <= C * PROJ
        o_all = big[:, 0:NT * D].rearrange("p (t n) -> p t n", t=NT)
        free0 = NT * D

        kT = [cut(big, free0 + u * NK * P, NK * P) for u in range(2)]
        qT = [cut(big, free0 + 2 * NK * P + u * NT * P, NT * P) for u in range(2)]
        at = free0 + 2 * NK * P + 2 * NT * P
        prob = [cut(big, at + u * SEQ, SEQ) for u in range(2)]
        probT = [cut(big, at + (2 + u) * SEQ, SEQ) for u in range(2)]
        skT = [cut(big, free0 + v * (NT + 1) * P, (NT + 1) * P) for v in range(2)]
        at = free0 + 2 * (NT + 1) * P
        sqT = [cut(big, at + u * NT * P, NT * P) for u in range(2)]
        at += 2 * NT * P
        sprob = [cut(big, at + u * 4 * P, 2, 2 * P) for u in range(2)]
        sprobT = [cut(big, at + (2 + u) * 4 * P, 4 * P) for u in range(2)]
        xr = [cut(big, free0 + u * D, D) for u in range(2)]
        on = [cut(big, free0 + (2 + u) * D, D) for u in range(2)]
        hh = [cut(big, free0 + (4 + u) * D, D) for u in range(2)]
        hhT = cut(big, free0 + 6 * D, C, P)
        at = free0
        rt = {}
        for name in ("lem", "eq", "oh1", "oh2", "run", "rank", "pos", "tmp", "q"):
            rt[name] = cut(big, at, NT, NE)
            at += NT * NE
        qi = cut(big, at, NT * NE).bitcast(I32)
        at += NT * NE
        for name in ("lg", "ohg", "eqg"):
            rt[name] = cut(big, at, NT, GRP)
            at += NT * GRP
        small = {}
        for name in ("m0", "m1", "m2", "i0", "i1", "i2", "den", "pg", "e21", "w1", "w2", "p1", "p2"):
            small[name] = cut(big, at, NT)
            at += NT
        nov = cut(big, at, 7, NE)
        at += 7 * NE
        ovi = cut(big, at, 2 * NE).bitcast(I32)
        at += 2 * NE
        ovc = cut(big, at, NOVER, NE)
        at += NOVER * NE
        ovf = cut(big, at, NOVER)
        at += NOVER
        ex = {}
        for name in ("e", "s", "r", "a", "hid", "hidT"):
            ex[name] = [cut(big, at + u * FE, FE) for u in range(2)]
            at += 2 * FE
        logit_t = cut(big, at, NT, GRP + NE)
        at += NT * (GRP + NE)
        maskb = cut(big, at, NT * NE // 2).bitcast(BF16)
        at += NT * NE // 2
        runb = cut(big, at, NT * NE // 2).bitcast(BF16)
        at += NT * NE // 2
        idx = cut(big, at, 8).bitcast(I32)
        at += 8
        ids = cut(big, at, 2 * NTILES).bitcast(I32)
        at += 2 * NTILES
        assert at <= C * PROJ - 2 * D
        ya = [cut(big, free0 + 3 * D + u * D, D) for u in range(2)]
        yb = [cut(big, free0 + 5 * D + u * D, D) for u in range(2)]
        fin = [cut(big, free0 + 7 * D + u * D, D) for u in range(2)]

        fox, fox_at = sb_at("fox", [P, NT * QKV + WSLOT])
        fox_t = fox[:, 0:NT * QKV].rearrange("p (t n) -> p t n", t=NT)
        w_out_h = rounded("w_out_h", fox_at, 0, C, D)
        swa = sb("swa", [P, NT * SWA])
        swa_t = swa[:, :].rearrange("p (t n) -> p t n", t=NT)
        w_out_at = NT * QKV + WSLOT - C * D
        w_out_raw = fox[:, w_out_at:w_out_at + C * D]
        w_out_l = rounded("w_out_l", fox_at, w_out_at, C, D)
        wslot = [cut(swa, 0, WSLOT), cut(swa, WSLOT, WSLOT), cut(fox, 0, WSLOT), cut(fox, WSLOT, WSLOT)]
        assert C * D <= w_out_at and 2 * WSLOT <= NT * SWA
        work, work_at = sb_at("work", [P, 6 * D])
        x = [cut(work, u * D, D) for u in range(2)]
        xn = [cut(work, (2 + u) * D, D) for u in range(2)]
        wg_raw = [cut(work, 4 * D, C, WG), cut(work, 0, C, WG)]
        wg_lo = [rounded("wg_lo0", work_at, 4 * D, C, WG), rounded("wg_lo1", work_at, 0, C, WG)]
        wg_hi = [rounded("wg_hi0", fox_at, NT * QKV, C, WG), rounded("wg_hi1", work_at, 2 * D, C, WG)]
        wf_hi = rounded("wf_hi", fox_at, NT * QKV + C * WG, C, NH)
        at = 0
        ck = cut(work, at, 2, (NH + 1) * DH)
        at += 2 * (NH + 1) * DH
        cv = cut(work, at, 2, NH * DH)
        at += 2 * NH * DH
        kst = cut(work, at, NK, DH + 1)
        at += NK * (DH + 1)
        qst = cut(work, at, NT, DH + 1)
        at += NT * (DH + 1)
        skv = cut(work, at, 2 * 2 * DH)
        at += 2 * 2 * DH
        sqst = cut(work, at, NT, P)
        at += NT * P
        lz = cut(work, at, 3 * NT * NH)
        at += 3 * NT * NH
        lsum = cut(work, at, NK * NH)
        lsum_t = cut(work, at, NK, NH)
        at += NK * NH
        assert at <= 6 * D
        hg = [cut(work, u * D, D) for u in range(2)] + [cut(big, C * PROJ - (2 - u) * D, D) for u in range(2)]
        hgT = [cut(work, (2 + u) * D, C, P) for u in range(2)]
        yo = [cut(work, (4 + u) * D, D) for u in range(2)]
        oTh = [rounded(f"oTh{u}", work_at, u * D, C, P) for u in range(2)]
        oTl = [rounded(f"oTl{u}", work_at, (2 + u) * D, C, P) for u in range(2)]

        cf = sb("cf", [P, 3 * P])
        ident, upto, ones = cf[:, 0:P], cf[:, P:2 * P], cf[:, 2 * P:3 * P]
        cb = sb("cb", [P, 4 * P + 2 * NH * P], BF16)
        identb, causal, before, onesb = (cb[:, n * P:(n + 1) * P] for n in range(4))
        alibi = cb[:, 4 * P:4 * P + 2 * NH * P]
        ci = sb("ci", [P, NT * 4], I32)
        cr = sb("cr", [P, NE + NT])
        g0 = sb("g0", [P, D])
        g1 = sb("g1", [P, D])
        bf = sb("bf", [P, NH])
        sink = sb("sink", [P, NH])
        nsink = sb("nsink", [P, NH])
        sraw = sb("sraw", [P, NH])
        br = sb("br", [P, GRP + NE])
        wr = sb("wr", [P, C * (GRP + NE)])
        wr_t = wr[:, :].rearrange("p (c e) -> p c e", c=C)
        lf = sb("lf", [P, NK * NH])
        lf_t = lf[:, :].rearrange("p (t h) -> p t h", t=NK)
        negc = sb("negc", [P, NK * (NH + 1)])
        negc_t = negc[:, :].rearrange("p (t h) -> p t h", t=NK)
        st = sb("st", [P, 16])
        eps = sb("eps", [P, 2])
        nm = sb("nm", [P, 16])
        rs = sb("rs", [P, 16])
        rc = sb("rc", [P, 8])
        wgt = sb("wgt", [P, 2 * NT])
        dest = sb("dest", [P, 2 * NT], I32)
        over = sb("over", [1, NOVER + 1], I32)

        ps = [ctx.enter_context(nc.psum_tensor(f"ps{b}", [P, 1024], F32)) for b in range(4)]
        bank = [ps[b // 2][:, 512 * (b % 2):512 * (b % 2) + 512] for b in range(8)]

        h_dram = nc.dram_tensor("h_rows", (TOK, D), F32, kind="Internal").ap()
        y_dram = nc.dram_tensor("y_rows", (2 * TOK, D), F32, kind="Internal").ap()
        id_dram = nc.dram_tensor("id_rows", (P * NTILES, 2), I32, kind="Internal").ap()

        names = """const_in gain_in small_in wf_in cache_in kv_out w_out_in g_late_in eps_set
            square_done rms_done rstd_done xn_done xT_done xh_done xl_done wg_hi_set wg_lo_set proj_done evac_v evac_s
            lf_v lf_s c_mm c_ready wo_hi_set wo_lo_set
            pad_set aug_set kv_staged st_T st_copied_s st_copied_v qk_done nmax_done exp_done pT_a pT_b cp_a cp_b pv_done o_done recip
            s_aug s_staged s_kT s_kcp s_qT_T s_qT_cp s_qk s_nm s_nmc s_exp s_sexp s_pT s_cpv s_cps s_pv s_rc s_od
            o_stat o_rms o_rstd on_done oT_done oTh_done oTl_done om_done x2_done h_stat h_rms h_rstd h_done h_out_a h_out_b hT_done hT_copied r_done
            r_step r_exp r_mask r_mm r_id id_init id_out id_in
            pool_went idx_set dst_set g_done gT_done gT_cs gT_cv gu_done e_done ev_step hid_done hidT_done hidT_cp dn_done y_cs y_cv hg_set
            v_idx v_g v_w v_gT v_gTc v_gu v_e v_s v_hid v_hT v_hTc v_dn v_y v_out experts_done
            f_acc f_stat f_rms f_rstd f_fin f_out_a f_out_b""".split()
        s = {n: sem(n) for n in names}
        wg_in = [sem(f"wg_in{u}") for u in range(2)]
        x_in = [sem(f"x_in{u}") for u in range(2)]
        xr_in = [sem(f"xr_in{u}") for u in range(2)]
        w_in_slot = [sem(f"w_in_slot{k}") for k in range(NSLOT)]
        g_in = [sem(f"g_in{u}") for u in range(4)]
        y_out = [sem(f"y_out{u}") for u in range(2)]
        y_in = [sem(f"y_in{u}") for u in range(2)]

        x_rows = t["x_prompt"].rearrange("a s d -> (a s) d")
        xs_rows = t["x_sample"].rearrange("a s d -> (a s) d")
        w_in_dram = t["w_in"].rearrange("l (p c) n -> p (l c) n", c=C)

        def wg_cols(g):
            at_ = g * WG + (NH if g >= FOX_G else 0)
            return w_in_dram[:, :, at_:at_ + WG]

        def wg_dest(g, i):
            to, c0 = (fox_t, g * WG) if g < FOX_G else (swa_t, (g - FOX_G) * WG)
            return to[:, i, c0:c0 + WG]

        def row(ap, n):
            return ap.rearrange("(a n) -> a n", a=1).broadcast_to([P, n])

        EVAC_V, EVAC_S = 3 + (NG * NT + 1) // 2, 3 + NG * NT // 2
        STEPS = [(u, i) for u in range(2) for i in range(NT)]
        NS = len(STEPS)
        nblk = [i + 1 for i in range(NP_T)] + [1 + PAST // P]
        TWO = [i for i in range(NT) if nblk[i] > 4]
        SG = [("q", 0, 4), ("q", 4, 8), ("q", 8, 9), ("k", 0, 4), ("k", 4, 8), ("k", 8, 11)]
        SG_AT = {2: 0, 3: 1, 4: 2, 5: 3, 6: 4, 7: 5}
        SSG = [(0, 4), (4, 8), (8, 9)]
        SSG_AT = {3: 0, 5: 1, 7: 2}

        WO_AT = (4, 8, 12, 16)

        def keytile(i, b):
            return b if i < SAMPLE else [NT, NT + 1, SAMPLE][b]

        def skeytile(i, b):
            return i - 1 + b if i < SAMPLE else [NT, SAMPLE][b]

        block = ctx.enter_context(nc.Block())

        @block.sync
        def _(sp):
            sp.dma_start(x[0], x_rows[0:P, :]).then_inc(x_in[0], 16)
            sp.dma_start(g0[:, :], row(t["g_mix_norm"].rearrange("l d -> (l d)"), D)).then_inc(s["gain_in"], 16)
            sp.dma_start(cf[:, :], t["const_f"]).then_inc(s["const_in"], 16)
            sp.dma_start(wg_raw[0], wg_cols(0)).then_inc(wg_in[0], 16)
            sp.dma_start(wf_raw, w_in_dram[:, :, QKV:QKV + NH]).then_inc(s["wf_in"], 16)
            sp.dma_start(x[1], x_rows[P:2 * P, :]).then_inc(x_in[1], 16)
            small_loads = [
                (cb[:, :], t["const_b"]), (ci[:, :], t["const_i"]), (cr[:, :], t["const_r"]),
                (bf[:, :], row(t["b_forget"].rearrange("l d -> (l d)"), NH)),
                (sraw[:, :], row(t["swa_sinks"].rearrange("l d -> (l d)"), NH)),
                (br[:, 0:GRP], row(t["b_router_group"].rearrange("l d -> (l d)"), GRP)),
                (br[:, GRP:GRP + NE], row(t["b_router_expert"].rearrange("l d -> (l d)"), NE)),
                (wr_t[:, :, 0:GRP], t["w_router_group"].rearrange("l (p c) n -> p (l c) n", c=C)),
                (wr_t[:, :, GRP:GRP + NE], t["w_router_expert"].rearrange("l (p c) n -> p (l c) n", c=C)),
                (lf_t[:, NT:NK, :], t["cache_fox_logf"].rearrange("l b (t p) h -> p (l b t) h", p=P)),
                (g1[:, 0:512], row(t["g_fox_out"].rearrange("l d -> (l d)"), 512)),
                (g1[:, 512:D], row(t["g_swa_out"].rearrange("l d -> (l d)"), 512)),
            ]
            for dst, src in small_loads:
                sp.dma_start(dst, src).then_inc(s["small_in"], 16)
            with sp.Fori(1, NP_T // 2) as j:
                for u in range(2):
                    sp.wait_ge(s["xn_done"], j * 2 + (u - 1))
                    sp.dma_start(x[u], x_rows[ds(j * 2 * P + u * P, P), :]).then_inc(x_in[u], 16)
            sp.wait_ge(s["xn_done"], NT - 2)
            sp.dma_start(x[0][0:DEC, :], xs_rows).then_inc(x_in[0], 16)
            sp.wait_ge(s["xn_done"], NT)
            for g in range(1, NG):
                if g >= 2:
                    sp.wait_ge(s["proj_done"], NT * (g - 1))
                sp.dma_start(wg_raw[g % 2], wg_cols(g)).then_inc(wg_in[g % 2], 16)
            sp.wait_ge(s["evac_v"], EVAC_V)
            sp.wait_ge(s["evac_s"], EVAC_S)
            sp.dma_start(ck[:, :, 0:NH * DH], t["cache_fox_k"].rearrange("l b (t p) h d -> p (l b t) (h d)", p=P)).then_inc(s["cache_in"], 16)
            sp.dma_start(cv[:, :, :], t["cache_fox_v"].rearrange("l b (t p) h d -> p (l b t) (h d)", p=P)).then_inc(s["cache_in"], 16)
            sp.dma_start(skv[:, 0:2 * DH], t["cache_swa_k"].rearrange("l b p h d -> p (l b h d)")).then_inc(s["cache_in"], 16)
            sp.dma_start(skv[:, 2 * DH:4 * DH], t["cache_swa_v"].rearrange("l b p h d -> p (l b h d)")).then_inc(s["cache_in"], 16)
            sp.dma_start(g0[:, :], row(t["g_ffn_norm"].rearrange("l d -> (l d)"), D)).then_inc(s["g_late_in"], 16)
            for n, name in ((1, "fox_k"), (2, "fox_v")):
                cols = slice(n * 512, (n + 1) * 512)
                sp.dma_start(t[name + "_prompt"].rearrange("l b (t p) h d -> p (l b t) (h d)", p=P),
                             fox_t[:, 0:NP_T, cols]).then_inc(s["kv_out"], 16)
                sp.dma_start(t[name + "_sample"].rearrange("l b s h d -> (l b s) (h d)"),
                             fox_t[0:DEC, SAMPLE, cols]).then_inc(s["kv_out"], 16)
            for n, name in ((4, "swa_k"), (5, "swa_v")):
                cols = slice(n * P, (n + 1) * P)
                sp.dma_start(t[name + "_prompt"].rearrange("l b s h d -> (l b s) (h d)"),
                             swa_t[:, NP_T - 1, cols]).then_inc(s["kv_out"], 16)
                sp.dma_start(t[name + "_sample"].rearrange("l b s h d -> (l b s) (h d)"),
                             swa_t[0:DEC, SAMPLE, cols]).then_inc(s["kv_out"], 16)
            sp.wait_ge(s["lf_v"], 3)
            sp.dma_start(t["fox_logf_prompt"].rearrange("l b (t p) h -> p (l b t) h", p=P),
                         lf_t[:, 0:NP_T, :]).then_inc(s["kv_out"], 16)
            sp.dma_start(t["fox_logf_sample"].rearrange("l b s h -> (l b s) h"),
                         lf_t[0:DEC, SAMPLE, :]).then_inc(s["kv_out"], 16)
            sp.wait_ge(s["kv_out"], 16 * 10)
            sp.wait_ge(s["pv_done"], 4 * NS)
            sp.wait_ge(s["kv_staged"], NH + 1)
            sp.dma_start(w_out_raw.rearrange("p (c n) -> p c n", c=C), t["w_out"].rearrange("l (c p) n -> p (l c) n", p=P)).then_inc(s["w_out_in"], 16)

            def expert(k, gate, up, down):
                sp.dma_start(wslot[k][:, 0:D].rearrange("p (c f) -> p c f", c=C), gate).then_inc(w_in_slot[k], 16)
                sp.dma_start(wslot[k][:, D:2 * D].rearrange("p (c f) -> p c f", c=C), up).then_inc(w_in_slot[k], 16)
                sp.dma_start(wslot[k][:, 2 * D:3 * D], down).then_inc(w_in_slot[k], 16)

            wg = t["w_gate"].rearrange("l e (p c) f -> (l e) p c f", c=C)
            wu = t["w_up"].rearrange("l e (p c) f -> (l e) p c f", c=C)
            wd = t["w_down"].rearrange("l e f d -> (l e) f d")
            sp.wait_ge(s["s_pv"], 2 * NS)
            for k in (0, 1):
                expert(k, wg[k], wu[k], wd[k])
            def load_xr(i, u, rows):
                src = x_rows[ds(i * P, P), :] if rows == P else xs_rows
                sp.dma_start(xr[u][0:rows, :], src).then_inc(xr_in[u], 16)

            for u in range(2):
                load_xr(u, u, P)

            def send_h(i, u):
                sp.wait_ge(s["h_done"], i + 1)
                sp.dma_start(h_dram[ds(i * P, P), :], hh[u]).then_inc(s["h_out_b" if u else "h_out_a"], 16)

            with sp.Fori(0, NP_T // 2 - 1) as j:
                for u in range(2):
                    sp.wait_ge(s["x2_done"], (j * 2 + (u + 1)) * 2)
                    load_xr(j * 2 + (u + 2), u, P)
                    send_h(j * 2 + u, u)
            sp.wait_ge(s["x2_done"], (NT - 2) * 2)
            load_xr(NT - 1, 0, DEC)
            for i in range(NT - 3, NT):
                send_h(i, i % 2)
            sp.wait_ge(s["on_done"], 2 * NT)
            sp.dma_start(g1[:, :], row(t["g_final"], D)).then_inc(s["g_late_in"], 16)
            sp.wait_ge(s["om_done"], NT)
            for k in (2, 3):
                expert(k, wg[k], wu[k], wd[k])
            sp.wait_ge(s["r_id"], 1)
            sp.dma_start(id_dram.rearrange("(p t) w -> p (t w)", p=P), ids[:, :]).then_inc(s["id_init"], 16)
            sp.wait_ge(s["id_out"], 16 * 2 * NT)
            sp.dma_start(ids[:, :], id_dram.rearrange("(p t) w -> p (t w)", p=P)).then_inc(s["id_in"], 16)
            with sp.Fori(1, NE // NSLOT) as j:
                for k in range(NSLOT):
                    sp.wait_ge(s["dn_done"], j * NSLOT + (k + 1 - NSLOT))
                    e = j * NSLOT + k
                    expert(k, wg[ds(e, 1)].rearrange("e p c f -> p (e c) f"), wu[ds(e, 1)].rearrange("e p c f -> p (e c) f"),
                           wd[ds(e, 1)].rearrange("e f d -> (e f) d"))
            sp.wait_ge(s["dn_done"], NE)
            sp.wait_ge(s["id_in"], 16)
            n_over = sp.value_load(over[0:1, 0:1], min_val=0, max_val=NOVER)
            with sp.Fori(0, NOVER) as k:
                with sp.If(k < n_over):
                    e = sp.value_load(over[0:1, ds(k + 1, 1)], min_val=0, max_val=NE - 1)
                    sp.wait_ge(s["v_dn"], k + 1)
                    for n, w in ((0, wg), (1, wu)):
                        sp.dma_start(wslot[0][:, n * D:(n + 1) * D].rearrange("p (c f) -> p c f", c=C),
                                     w[ds(e, 1)].rearrange("e p c f -> p (e c) f")).then_inc(s["v_w"], 16)
                    sp.dma_start(wslot[0][:, 2 * D:3 * D], wd[ds(e, 1)].rearrange("e f d -> (e f) d")).then_inc(s["v_w"], 16)
            sp.wait_ge(s["experts_done"], 1)

            def load_y(i, u, rows):
                sp.dma_start(ya[u][0:rows, :], y_dram[ds(i * P, rows), :]).then_inc(y_in[u], 16)
                sp.dma_start(yb[u][0:rows, :], y_dram[ds(i * P + TOK, rows), :]).then_inc(y_in[u], 16)

            def store(i, u):
                sp.wait_ge(s["f_fin"], i + 1)
                sp.dma_start(t["y_prompt"].rearrange("a s d -> (a s) d")[ds(i * P, P), :], fin[u]).then_inc(s["f_out_b" if u else "f_out_a"], 16)

            for u in range(2):
                load_y(u, u, P)
            with sp.Fori(0, NP_T // 2 - 1) as j:
                for u in range(2):
                    sp.wait_ge(s["f_acc"], (j * 2 + (u + 1)) * 2)
                    load_y(j * 2 + (u + 2), u, P)
                    store(j * 2 + u, u)
            sp.wait_ge(s["f_acc"], (NT - 2) * 2)
            load_y(NT - 1, 0, DEC)
            for i in (NP_T - 2, NP_T - 1):
                store(i, i % 2)
            sp.wait_ge(s["f_fin"], NT)
            sp.dma_start(t["y_sample"].rearrange("a s d -> (a s) d"), fin[0][0:DEC, :]).then_inc(s["f_out_a"], 16)
            sp.wait_ge(s["f_out_a"], 16 * 5)
            sp.wait_ge(s["f_out_b"], 16 * 4)

        @block.gpsimd
        def _(pool):
            pool.wait_ge(s["cache_in"], 64)
            pool.memset(qst[:, :, DH:DH + 1], 1.0 / SCALE).then_inc(s["pad_set"], 1)
            pool.memset(ck[:, :, NH * DH:], 0.0).then_inc(s["pad_set"], 1)
            pool.wait_ge(s["pad_set"], 2)
            pool.wait_ge(s["c_ready"], 1)

            def stage(h, done, first=False):
                if not first:
                    pool.wait_ge(s["st_T"], done)
                pool.tensor_copy(qst[:, :, 0:DH], fox_t[:, :, ds(h * DH, DH)])
                pool.tensor_copy(kst[:, 0:NT, 0:DH], fox_t[:, :, ds(h * DH + NH * DH, DH)])
                pool.tensor_copy(kst[:, NT:NK, 0:DH], ck[:, :, ds(h * DH, DH)])
                pool.tensor_copy(kst[:, :, DH:DH + 1], negc_t[:, :, ds(h, 1)]).then_inc(s["kv_staged"], 1)

            stage(0, 0, True)
            with pool.Fori(0, NH) as h:
                stage(h + 1, h * 6 + 6)

            def s_stage(g, done, first=False):
                if not first:
                    pool.wait_ge(s["s_qT_T"], done)
                pool.tensor_copy(sqst[:, :, 0:DH], swa_t[:, :, ds(g * DH, DH)])
                pool.tensor_copy(sqst[:, :, DH:P], swa_t[:, :, ds(g * DH + 4 * DH, DH)]).then_inc(s["s_staged"], 1)

            s_stage(0, 0, True)
            with pool.Fori(0, 4) as g:
                s_stage(g + 1, g * 3 + 3)
            pool.wait_ge(s["r_mm"], 2)
            pool.memset(ids[:, :], SKIP).then_inc(s["r_id"], 1)
            pool.wait_ge(s["id_init"], 16)
            pool.wait_ge(s["r_mask"], 2)
            for i in range(NT):
                for c in range(2):
                    n = 2 * i + c
                    pool.indirect_dma_start(
                        out=id_dram, out_offset=bass.IndirectOffsetOnAxis(ap=dest[:, n:n + 1], axis=0),
                        in_=ci[:, 2 * n:2 * n + 2], in_offset=None,
                        bounds_check=P * NTILES - 1, oob_is_err=False).then_inc(s["id_out"], 16)
            pool.wait_ge(s["s_staged"], 5)
            pool.wait_ge(s["pv_done"], 4 * NS)
            pool.wait_ge(s["s_pv"], 2 * NS)
            pool.wait_ge(s["s_qT_T"], 15)
            for k in range(4):
                pool.memset(hg[k], 0.0).then_inc(s["hg_set"], 1)
            pool.wait_ge(s["hg_set"], 4)
            pool.wait_ge(s["id_in"], 16)
            for i in range(2):
                pool.wait_ge(s["h_out_a"], 16 * 5)
                pool.wait_ge(s["h_out_b"], 16 * 4)

            def gather(tt, k):
                pool.tensor_copy(idx[:, k:k + 1], ids[:, ds(tt * 2, 1)]).then_inc(s["idx_set"], 1)
                pool.wait_ge(s["idx_set"], tt + 1)
                pool.sem_inc(s["pool_went"], 1)
                pool.indirect_dma_start(
                    out=hg[k], out_offset=None, in_=h_dram,
                    in_offset=bass.IndirectOffsetOnAxis(ap=idx[:, k:k + 1], axis=0),
                    bounds_check=TOK - 1, oob_is_err=False).then_inc(g_in[k], 16)

            def scatter(tt, k):
                u = k % 2
                if not (isinstance(tt, int) and tt < 2):
                    pool.wait_ge(y_out[u], (tt - u) * 8)
                pool.tensor_copy(idx[:, 4 + u:5 + u], ids[:, ds(tt * 2 + 1, 1)]).then_inc(s["dst_set"], 1)
                pool.wait_ge(s["dst_set"], tt + 1)
                pool.wait_ge(s["y_cs"], tt + 1)
                pool.wait_ge(s["y_cv"], tt + 1)
                pool.sem_inc(s["pool_went"], 1)
                pool.indirect_dma_start(
                    out=y_dram, out_offset=bass.IndirectOffsetOnAxis(ap=idx[:, 4 + u:5 + u], axis=0),
                    in_=yo[u], in_offset=None,
                    bounds_check=2 * TOK - 1, oob_is_err=False).then_inc(y_out[u], 16)

            def rows_step(tt, k, more=True):
                if more:
                    pool.wait_ge(s["gT_done"], tt * 2 + 4)
                    gather(tt + 5, (k + 1) % 4)
                scatter(tt, k)

            for tt in range(4):
                gather(tt, tt)
            pool.wait_ge(s["gT_done"], 2)
            gather(4, 0)
            for tt in range(4):
                rows_step(tt, tt)
            with pool.Fori(1, NE // 4 - 2) as j:
                for k in range(4):
                    rows_step(j * 4 + k, k)
            for tt in range(NE - 8, NE):
                rows_step(tt, tt % 4, tt + 5 < NE)
            pool.wait_ge(y_out[0], 16 * NE // 2)
            pool.wait_ge(y_out[1], 16 * NE // 2)
            n_over = pool.value_load(over[0:1, 0:1], min_val=0, max_val=NOVER)
            with pool.Fori(0, NOVER) as k:
                with pool.If(k < n_over):
                    pool.tensor_copy(idx[:, 0:2], ids[:, ds(k * 2 + 2 * NE, 2)]).then_inc(s["v_idx"], 1)
                    pool.wait_ge(s["v_idx"], k + 1)
                    pool.sem_inc(s["pool_went"], 1)
                    pool.indirect_dma_start(
                        out=hg[0], out_offset=None, in_=h_dram,
                        in_offset=bass.IndirectOffsetOnAxis(ap=idx[:, 0:1], axis=0),
                        bounds_check=TOK - 1, oob_is_err=False).then_inc(s["v_g"], 16)
                    pool.wait_ge(s["v_y"], k * 2 + 2)
                    pool.sem_inc(s["pool_went"], 1)
                    pool.indirect_dma_start(
                        out=y_dram, out_offset=bass.IndirectOffsetOnAxis(ap=idx[:, 1:2], axis=0),
                        in_=yo[0], in_offset=None,
                        bounds_check=2 * TOK - 1, oob_is_err=False).then_inc(s["v_out"], 16)
                    pool.wait_ge(s["v_out"], k * 16 + 16)
            pool.sem_inc(s["experts_done"], 1)

        @block.scalar
        def _(act):
            act.sem_inc(s["evac_s"], 3)
            act.sem_inc(s["cp_b"], 1)
            act.sem_inc(s["exp_done"], 2)
            act.wait_ge(s["eps_set"], 1)

            def norm(i, j, u):
                act.wait_ge(x_in[u], j * 16 + 16)
                if not (isinstance(i, int) and i < 2):
                    act.wait_ge(s["xT_done"], i * 2 - 2)
                act.activation(xn[u], x[u], ACT.Square, accum_out=st[:, u:u + 1]).then_inc(s["square_done"], 1)
                act.wait_ge(s["square_done"], i + 1)
                act.activation(st[:, 2 + u:3 + u], st[:, u:u + 1], ACT.Sqrt, bias=eps[:, 0:1], scale=1.0 / D).then_inc(s["rms_done"], 1)

            def high_x(i):
                for b in range(2):
                    act.wait_ge(s["xT_done"], i * 2 + (b + 1))
                    act.activation(xh[:, ds(i * C + 4 * b, 4), :], bank[b].rearrange("p (c k) -> p c k", c=4), ACT.Copy).then_inc(s["xh_done"], 1)

            def high_w(u, loads):
                act.wait_ge(wg_in[u], loads * 16)
                act.activation(wg_hi[u], wg_raw[u], ACT.Copy).then_inc(s["wg_hi_set"], 1)

            def evac(n, k, dest):
                act.wait_ge(s["proj_done"], n + 1)
                act.activation(dest, bank[2 + k % 6][:, 0:WG], ACT.Copy).then_inc(s["evac_s"], 1)

            def evac_first(i, k):
                act.wait_ge(s["proj_done"], i + 1)
                act.activation(lf_t[:, ds(i, 1), :].rearrange("p a n -> p (a n)"), bank[2 + k % 6][:, WG:WG + NH], ACT.Copy)
                evac(i, k, fox_t[:, ds(i, 1), 0:WG].rearrange("p a n -> p (a n)"))

            norm(0, 0, 0)
            high_x(0)
            high_w(0, 1)
            act.wait_ge(s["wf_in"], 16)
            act.activation(wf_hi, wf_raw, ACT.Copy).then_inc(s["wg_hi_set"], 1)
            norm(1, 0, 1)
            for i in range(6):
                high_x(i + 1)
                norm(i + 2, (i + 2) // 2, i % 2)
                if i % 2:
                    evac_first(i, i)
            high_x(7)
            norm(8, 4, 0)
            high_x(8)
            act.wait_ge(s["xT_done"], 2 * NT)
            high_w(1, 1)
            evac_first(7, 7)

            def group(n0, k0, loads, proj, dest, more=True):
                for i in range(NT):
                    if i == 3 and more:
                        act.wait_ge(s["proj_done"], proj)
                        high_w((k0 + 1) % 2, loads)
                    if (k0 + i) % 2:
                        evac(n0 + i, k0 + i, dest(i))

            with act.Fori(0, 2) as j:
                for g in (1, 2):
                    group(j * 2 * NT + g * NT, g * NT, j + ((g + 1) // 2 + 1), j * 2 * NT + g * NT,
                          lambda i: fox_t[:, i, ds(j * 2 * WG + g * WG, WG)])
            for g in range(5, NG):
                group(g * NT, g * NT, (g + 1) // 2 + 1, g * NT, lambda i: wg_dest(g, i), g + 1 < NG)

            n = NT * NH
            act.wait_ge(s["lf_v"], 2)
            act.activation(lz[:, n:2 * n], lz[:, 2 * n:3 * n], ACT.Exp, scale=-1.0).then_inc(s["lf_s"], 1)
            act.wait_ge(s["lf_s"], 1)
            act.activation(lz[:, 2 * n:3 * n], lz[:, n:2 * n], ACT.Ln, bias=eps[:, 1:2]).then_inc(s["lf_s"], 1)

            def stage_q(h6, u, gi):
                _, a, b = SG[gi]
                act.wait_ge(s["st_T"], h6 + (gi + 1))
                act.activation(qT[u][0:DH + 1, a * P:b * P], bank[7][0:DH + 1, 0:(b - a) * P], ACT.Copy, scale=SCALE).then_inc(s["st_copied_s"], 1)

            act.wait_ge(s["aug_set"], 4)
            for gi in range(3):
                stage_q(0, 0, gi)

            def fexp(it, k):
                u, i = STEPS[k]
                n = nblk[i] * P
                act.wait_ge(s["nmax_done"], it * NS + (k + 1))
                if k >= 1:
                    act.wait_ge(s["pT_a"], it * NS + max(k - 1, 1))
                act.activation(prob[k % 2][:, 0:n], ps[k % 2][:, 0:n], ACT.Exp, bias=nm[:, k % 2:k % 2 + 1],
                               accum_out=rs[:, k % 4:k % 4 + 1]).then_inc(s["exp_done"], 1)

            def copy_b(it, k):
                u, i = STEPS[k]
                n = nblk[i] * P
                if n > 512:
                    seen = sum(nblk[STEPS[m][1]] > 4 for m in range(k + 1))
                    act.wait_ge(s["pT_b"], it * 2 * len(TWO) + seen)
                    act.wait_ge(s["pv_done"], it * NS + (k - 1))
                    act.activation(probT[k % 2][:, 512:n], bank[5][:, 0:n - 512], ACT.Copy).then_inc(s["cp_b"], 1)

            with act.Fori(0, NH // 2) as it:
                fexp(it, 0)
                for k in range(NS):
                    u, i = STEPS[k]
                    if k + 1 < NS:
                        fexp(it, k + 1)
                    if i in SG_AT and SG_AT[i] < 3:
                        stage_q(it * 12 + 6 * (u + 1), 1 - u, SG_AT[i])
                    copy_b(it, k)

            def stage_sq(g3, u, gi):
                a, b = SSG[gi]
                act.wait_ge(s["s_qT_T"], g3 + (gi + 1))
                act.activation(sqT[u][:, a * P:b * P], bank[7][:, 0:(b - a) * P], ACT.Copy, scale=SCALE).then_inc(s["s_qT_cp"], 1)

            for gi in range(3):
                stage_sq(0, 0, gi)

            def sexp(it, k):
                u, i = STEPS[k]
                lo = P if i == 0 else 0
                act.wait_ge(s["s_nm"], it * NS + (k + 1))
                if k >= 1:
                    act.wait_ge(s["s_pT"], it * NS + max(k - 1, 1))
                for v in range(2):
                    act.activation(sprob[k % 2][:, v, lo:2 * P], ps[k % 2][:, v * 256 + lo:v * 256 + 256], ACT.Exp,
                                   bias=nm[:, 4 + 2 * (k % 2) + v:5 + 2 * (k % 2) + v],
                                   accum_out=rs[:, 4 + 2 * (k % 3) + v:5 + 2 * (k % 3) + v]).then_inc(s["s_exp"], 1)
                act.activation(rs[:, 10 + 2 * (k % 3):12 + 2 * (k % 3)], nm[:, 8 + 2 * (k % 2):10 + 2 * (k % 2)], ACT.Exp).then_inc(s["s_sexp"], 1)

            def scopy(it, k):
                if k % 2:
                    n = 2 * P if STEPS[k][1] == 0 else 4 * P
                    act.wait_ge(s["s_pT"], it * NS + (k + 1))
                    if k > 1:
                        act.wait_ge(s["s_pv"], it * NS + (k - 1))
                    act.activation(sprobT[1][:, 0:n], bank[5][:, 0:n], ACT.Copy).then_inc(s["s_cps"], 1)

            with act.Fori(0, 2) as it:
                sexp(it, 0)
                for k in range(NS):
                    u, i = STEPS[k]
                    if k + 1 < NS:
                        sexp(it, k + 1)
                    if i in SSG_AT:
                        stage_sq(it * 6 + 3 * (u + 1), 1 - u, SSG_AT[i])
                    scopy(it, k)
                    if k in WO_AT:
                        act.wait_ge(s["w_out_in"], 16)
                        c = it * (C // 2) + WO_AT.index(k)
                        act.activation(w_out_h[:, ds(c, 1), :].rearrange("p a n -> p (a n)"), fox[:, ds(c * D + w_out_at, D)],
                                       ACT.Copy).then_inc(s["wo_hi_set"], 1)

            act.wait_ge(s["s_od"], 2 * NS + 1)

            def norm_o(i, u):
                if not (isinstance(i, int) and i < 2):
                    act.wait_ge(s["oT_done"], i * 2 - 2)
                for v in range(2):
                    act.activation(on[u][:, 512 * v:512 * v + 512], o_all[:, ds(i, 1), 512 * v:512 * v + 512].rearrange("p a n -> p (a n)"),
                                   ACT.Square, accum_out=st[:, 2 * u + v:2 * u + v + 1]).then_inc(s["o_stat"], 1)
                act.wait_ge(s["o_stat"], i * 2 + 2)
                act.activation(st[:, 4 + 2 * u:6 + 2 * u], st[:, 2 * u:2 * u + 2], ACT.Sqrt, bias=eps[:, 0:1], scale=2.0 / D).then_inc(s["o_rms"], 1)

            def high_o(i, u):
                if not (isinstance(i, int) and i < 2):
                    act.wait_ge(s["om_done"], i - 1)
                for b in range(2):
                    act.wait_ge(s["oT_done"], i * 2 + (b + 1))
                    act.activation(oTh[u][:, 4 * b:4 * b + 4, :], bank[b].rearrange("p (c k) -> p c k", c=4), ACT.Copy).then_inc(s["oTh_done"], 1)

            def norm_h(i, u):
                act.wait_ge(s["x2_done"], i * 2 + 2)
                if not (isinstance(i, int) and i < 2):
                    act.wait_ge(s["hT_done"], i * 2 - 2)
                    act.wait_ge(s["h_out_b" if u else "h_out_a"], (i - u) * 8)
                act.activation(hh[u], o_all[:, ds(i, 1), :].rearrange("p a n -> p (a n)"), ACT.Square,
                               accum_out=st[:, 12:13]).then_inc(s["h_stat"], 1)
                act.wait_ge(s["h_stat"], i + 1)
                act.activation(st[:, 13:14], st[:, 12:13], ACT.Sqrt, bias=eps[:, 0:1], scale=1.0 / D).then_inc(s["h_rms"], 1)

            def copy_hT(i):
                if not (isinstance(i, int) and i < 1):
                    act.wait_ge(s["r_done"], i)
                for b in range(2):
                    act.wait_ge(s["hT_done"], i * 2 + (b + 1))
                    act.activation(hhT[:, 4 * b:4 * b + 4, :], bank[b].rearrange("p (c k) -> p c k", c=4), ACT.Copy).then_inc(s["hT_copied"], 1)

            for i in range(3):
                norm_o(i, i % 2)
                high_o(i, i % 2)

            def ostep(i, u, more=True):
                if more:
                    norm_o(i + 3, 1 - u)
                norm_h(i, u)
                copy_hT(i)
                if more:
                    high_o(i + 3, 1 - u)

            for i in (0, 1):
                ostep(i, i)
            with act.Fori(1, 3) as j:
                for u in range(2):
                    ostep(j * 2 + u, u)
            for i in (6, 7, 8):
                ostep(i, i % 2, False)

            act.wait_ge(s["r_exp"], 1)
            act.activation(rt["eqg"], rt["lg"], ACT.Exp).then_inc(s["r_exp"], 1)
            act.wait_ge(s["r_exp"], 3)
            act.activation(small["e21"], small["m2"], ACT.Exp).then_inc(s["r_exp"], 1)

            def copy_gT(tt, u):
                act.wait_ge(s["gT_done"], tt * 2 + 1)
                if not (isinstance(tt, int) and tt < 2):
                    act.wait_ge(s["gu_done"], tt - 1)
                act.activation(hgT[u][:, 0:4, :], bank[0].rearrange("p (c k) -> p c k", c=4), ACT.Copy).then_inc(s["gT_cs"], 1)

            def gate_exp(tt, u):
                act.wait_ge(s["gu_done"], tt + 1)
                if not (isinstance(tt, int) and tt < 2):
                    act.wait_ge(s["ev_step"], tt * 3 - 5)
                act.activation(ex["e"][u], bank[2 + u][:, 0:FE], ACT.Exp, scale=-1.0).then_inc(s["e_done"], 1)

            def copy_hid(tt, u):
                act.wait_ge(s["hidT_done"], tt + 1)
                if not (isinstance(tt, int) and tt < 2):
                    act.wait_ge(s["dn_done"], tt - 1)
                act.activation(ex["hidT"][u], bank[6][:, 0:P], ACT.Copy).then_inc(s["hidT_cp"], 1)

            def copy_y(tt, u):
                act.wait_ge(s["dn_done"], tt + 1)
                if not (isinstance(tt, int) and tt < 2):
                    act.wait_ge(y_out[u], (tt - u) * 8)
                act.activation(yo[u][:, 0:512], bank[4], ACT.Copy).then_inc(s["y_cs"], 1)

            def estep(tt, u, last=2):
                if last >= 1:
                    gate_exp(tt + 1, 1 - u)
                copy_hid(tt, u)
                if last >= 2:
                    copy_gT(tt + 2, u)
                copy_y(tt, u)

            copy_gT(0, 0)
            copy_gT(1, 1)
            gate_exp(0, 0)
            estep(0, 0)
            estep(1, 1)
            with act.Fori(1, NE // 2 - 1) as j:
                for u in range(2):
                    estep(j * 2 + u, u)
            estep(NE - 2, 0, 1)
            estep(NE - 1, 1, 0)

            n_over = act.value_load(over[0:1, 0:1], min_val=0, max_val=NOVER)
            with act.Fori(0, NOVER) as k:
                with act.If(k < n_over):
                    act.wait_ge(s["v_gT"], k * 2 + 1)
                    act.activation(hgT[0][:, 0:4, :], bank[0].rearrange("p (c k) -> p c k", c=4), ACT.Copy).then_inc(s["v_gTc"], 1)
                    act.wait_ge(s["v_gu"], k + 1)
                    act.activation(ex["e"][0], bank[2][:, 0:FE], ACT.Exp, scale=-1.0).then_inc(s["v_e"], 1)
                    act.wait_ge(s["v_hT"], k + 1)
                    act.activation(ex["hidT"][0], bank[6][:, 0:P], ACT.Copy).then_inc(s["v_hTc"], 1)
                    act.wait_ge(s["v_dn"], k + 2)
                    act.activation(yo[0][:, 0:512], bank[4], ACT.Copy).then_inc(s["v_y"], 1)
            act.wait_ge(s["experts_done"], 1)

            def norm_f(i, u, rows):
                act.wait_ge(s["f_acc"], i * 2 + 2)
                if not (isinstance(i, int) and i < 2):
                    act.wait_ge(s["f_out_b" if u else "f_out_a"], (i - u) * 8)
                act.activation(fin[u][0:rows, :], o_all[0:rows, ds(i, 1), :].rearrange("p a n -> p (a n)"), ACT.Square,
                               accum_out=st[0:rows, u:u + 1]).then_inc(s["f_stat"], 1)
                act.wait_ge(s["f_stat"], i + 1)
                act.activation(st[0:rows, 2 + u:3 + u], st[0:rows, u:u + 1], ACT.Sqrt, bias=eps[0:rows, 0:1], scale=1.0 / D).then_inc(s["f_rms"], 1)

            norm_f(0, 0, P)
            norm_f(1, 1, P)
            with act.Fori(1, NP_T // 2) as j:
                for u in range(2):
                    norm_f(j * 2 + u, u, P)
            norm_f(8, 0, DEC)

        @block.vector
        def _(dve):
            dve.memset(eps[:, 0:1], EPS)
            dve.memset(negc[:, :], 0.0)
            dve.memset(eps[:, 1:2], 1.0).then_inc(s["eps_set"], 1)
            dve.sem_inc(s["evac_v"], 3)
            dve.sem_inc(s["o_done"], 1)
            dve.sem_inc(s["s_od"], 1)

            def scale_x(i, u):
                dve.wait_ge(s["rms_done"], i + 1)
                dve.reciprocal(st[:, 4 + u:5 + u], st[:, 2 + u:3 + u]).then_inc(s["rstd_done"], 1)
                dve.wait_ge(s["rstd_done"], i + 1)
                dve.scalar_tensor_tensor(out=xn[u], in0=x[u], scalar=st[:, 4 + u:5 + u], in1=g0[:, :],
                                         op0=ALU.mult, op1=ALU.mult).then_inc(s["xn_done"], 1)

            def low_x(i):
                for b in range(2):
                    dve.wait_ge(s["xh_done"], i * 2 + (b + 1))
                    dve.tensor_tensor(xl[:, ds(i * C + 4 * b, 4), :], bank[b].rearrange("p (c k) -> p c k", c=4),
                                      xh[:, ds(i * C + 4 * b, 4), :].bitcast(F32), ALU.subtract).then_inc(s["xl_done"], 1)

            def low_w(u, highs):
                dve.wait_ge(s["wg_hi_set"], highs)
                dve.tensor_tensor(wg_lo[u], wg_raw[u], wg_hi[u].bitcast(F32), ALU.subtract).then_inc(s["wg_lo_set"], 1)

            def evac(n, k, dest):
                dve.wait_ge(s["proj_done"], n + 1)
                dve.tensor_copy(dest, bank[2 + k % 6][:, 0:WG]).then_inc(s["evac_v"], 1)

            def evac_first(i, k):
                dve.wait_ge(s["proj_done"], i + 1)
                dve.tensor_copy(lf_t[:, ds(i, 1), :].rearrange("p a n -> p (a n)"), bank[2 + k % 6][:, WG:WG + NH])
                evac(i, k, fox_t[:, ds(i, 1), 0:WG].rearrange("p a n -> p (a n)"))

            dve.wait_ge(s["gain_in"], 16)
            scale_x(0, 0)
            low_x(0)
            low_w(0, 1)
            dve.wait_ge(s["wg_hi_set"], 2)
            dve.tensor_tensor(wf_lo, wf_raw, wf_hi.bitcast(F32), ALU.subtract).then_inc(s["wg_lo_set"], 1)
            scale_x(1, 1)
            for i in range(6):
                low_x(i + 1)
                scale_x(i + 2, i % 2)
                if i % 2 == 0:
                    evac_first(i, i)
            low_x(7)
            scale_x(8, 0)
            low_x(8)
            low_w(1, 3)
            evac_first(6, 6)
            evac_first(8, 8)

            def group(n0, k0, highs, dest, more=True):
                for i in range(NT):
                    if i == 4 and more:
                        low_w((k0 + 1) % 2, highs)
                    if (k0 + i) % 2 == 0:
                        evac(n0 + i, k0 + i, dest(i))

            with dve.Fori(0, 2) as j:
                for g in (1, 2):
                    group(j * 2 * NT + g * NT, g * NT, j * 2 + (g + 3),
                          lambda i: fox_t[:, i, ds(j * 2 * WG + g * WG, WG)])
            for g in range(5, NG):
                group(g * NT, g * NT, g + 3, lambda i: wg_dest(g, i), g + 1 < NG)

            n = NT * NH
            dve.wait_ge(s["small_in"], 16 * 12)
            dve.wait_ge(s["evac_v"], EVAC_V)
            dve.wait_ge(s["evac_s"], EVAC_S)
            z, mn = lz[:, 0:n], lz[:, n:2 * n]
            dve.tensor_tensor(z.rearrange("p (t h) -> p t h", h=NH), lf_t[:, 0:NT, :],
                              bf[:, None, :].to_broadcast([P, NT, NH]), ALU.add).then_inc(s["lf_v"], 1)
            dve.wait_ge(s["lf_v"], 1)
            dve.scalar_tensor_tensor(out=lz[:, 2 * n:3 * n], in0=z, scalar=-1.0, in1=z, op0=ALU.mult, op1=ALU.max).then_inc(s["lf_v"], 1)
            dve.wait_ge(s["lf_s"], 2)
            dve.scalar_tensor_tensor(out=lf[:, 0:n], in0=z, scalar=0.0, in1=lz[:, 2 * n:3 * n],
                                     op0=ALU.min, op1=ALU.subtract).then_inc(s["lf_v"], 1)
            dve.wait_ge(s["lf_v"], 3)
            dve.memset(lsum[:, :], 0.0).then_inc(s["lf_v"], 1)
            dve.wait_ge(s["lf_v"], 4)
            dve.tensor_copy(lsum_t[:, NT + 1, :], lf_t[:, NT, :])
            dve.tensor_tensor(lsum_t[:, SAMPLE, :], lf_t[:, NT, :], lf_t[:, NT + 1, :], ALU.add)
            for i in range(1, NP_T):
                dve.tensor_tensor(lsum_t[:, i, :], lsum_t[:, i - 1, :], lf_t[:, i - 1, :], ALU.add).then_inc(s["lf_v"], 1)
                dve.wait_ge(s["lf_v"], 4 + i)
            dve.wait_ge(s["c_mm"], 1)
            dve.tensor_scalar(negc_t[:, :, 0:NH], bank[0][:, 0:NK * NH].rearrange("p (t h) -> p t h", h=NH),
                              -1.0, None, ALU.mult).then_inc(s["c_ready"], 1)
            for u in range(2):
                dve.memset(qT[u][DH:P, :], 0.0).then_inc(s["aug_set"], 1)
                dve.memset(kT[u][DH:P, :], 0.0).then_inc(s["aug_set"], 1)
            dve.wait_ge(s["aug_set"], 4)

            def stage_k(h6, u, gi):
                _, a, b = SG[gi]
                dve.wait_ge(s["st_T"], h6 + (gi + 1))
                dve.tensor_copy(kT[u][0:DH + 1, a * P:b * P], bank[7][0:DH + 1, 0:(b - a) * P]).then_inc(s["st_copied_v"], 1)

            for gi in range(3, 6):
                stage_k(0, 0, gi)

            def fmax(it, k):
                n = nblk[STEPS[k][1]] * P
                dve.wait_ge(s["qk_done"], it * NS + (k + 1))
                dve.tensor_reduce(nm[:, k % 2:k % 2 + 1], ps[k % 2][:, 0:n], AX.X, ALU.max, negate=True).then_inc(s["nmax_done"], 1)

            def copy_a(it, k):
                n = min(nblk[STEPS[k][1]] * P, 512)
                dve.wait_ge(s["pT_a"], it * NS + (k + 1))
                dve.tensor_copy(probT[k % 2][:, 0:n], bank[4][:, 0:n]).then_inc(s["cp_a"], 1)

            def fnorm(it, k):
                u, i = STEPS[k]
                dve.reciprocal(rc[:, k % 2:k % 2 + 1], rs[:, k % 4:k % 4 + 1]).then_inc(s["recip"], 1)
                dve.wait_ge(s["recip"], it * NS + (k + 1))
                dve.wait_ge(s["pv_done"], it * NS + (k + 1))
                dve.tensor_scalar(o_all[:, i, ds(it * 2 * DH + u * DH, DH)], bank[6][:, (k % 2) * DH:(k % 2) * DH + DH],
                                  rc[:, k % 2:k % 2 + 1], None, ALU.mult).then_inc(s["o_done"], 1)

            with dve.Fori(0, NH // 2) as it:
                fmax(it, 0)
                for k in range(NS):
                    u, i = STEPS[k]
                    if k + 1 < NS:
                        fmax(it, k + 1)
                    if i in SG_AT and SG_AT[i] >= 3:
                        stage_k(it * 12 + 6 * (u + 1), 1 - u, SG_AT[i])
                    copy_a(it, k)
                    if k >= 1:
                        fnorm(it, k - 1)
                fnorm(it, NS - 1)

            pairs = sraw[:, :].rearrange("p (v g) -> p g v", v=2)
            dve.tensor_copy(sink[:, :].rearrange("p (g v) -> p g v", v=2), pairs)
            dve.tensor_scalar(nsink[:, :].rearrange("p (g v) -> p g v", v=2), pairs, -1.0, None, ALU.mult).then_inc(s["s_aug"], 1)
            dve.wait_ge(s["s_aug"], 1)
            dve.memset(skT[0][DH:P, :], 0.0).then_inc(s["s_aug"], 1)
            dve.memset(skT[1][0:DH, :], 0.0).then_inc(s["s_aug"], 1)
            for gi, (a, b) in enumerate([(0, 4), (4, 8), (8, 10)]):
                dve.wait_ge(s["s_kT"], gi + 1)
                dve.tensor_copy(skT[0][0:DH, a * P:b * P], bank[4 + gi % 2][0:DH, 0:(b - a) * P])
                dve.tensor_copy(skT[1][DH:P, a * P:b * P], bank[4 + gi % 2][DH:P, 0:(b - a) * P]).then_inc(s["s_kcp"], 1)

            def smax(it, k):
                u, i = STEPS[k]
                lo = P if i == 0 else 0
                a, q = 4 + 2 * (k % 2), 8 + 2 * (k % 2)
                n = it * NS * 2 + 2 * k
                dve.wait_ge(s["s_qk"], it * NS + (k + 1))
                if k >= 2:
                    dve.wait_ge(s["s_sexp"], it * NS + (k - 1))
                dve.tensor_reduce(nm[:, 12:14], ps[k % 2][:, 0:512].rearrange("p (v n) -> p v n", v=2)[:, :, lo:256],
                                  AX.X, ALU.max, negate=True).then_inc(s["s_nmc"], 1)
                dve.wait_ge(s["s_nmc"], n + 1)
                g2 = it * 4 + 2 * u
                dve.tensor_tensor(nm[:, a:a + 2], nm[:, 12:14], nsink[:, ds(g2, 2)], ALU.min).then_inc(s["s_nmc"], 1)
                dve.wait_ge(s["s_nmc"], n + 2)
                dve.tensor_tensor(nm[:, q:q + 2], nm[:, a:a + 2], sink[:, ds(g2, 2)], ALU.add).then_inc(s["s_nm"], 1)

            def scopy(it, k):
                if k % 2 == 0:
                    n = 2 * P if STEPS[k][1] == 0 else 4 * P
                    dve.wait_ge(s["s_pT"], it * NS + (k + 1))
                    dve.tensor_copy(sprobT[0][:, 0:n], bank[4][:, 0:n]).then_inc(s["s_cpv"], 1)

            def snorm(it, k):
                u, i = STEPS[k]
                a, q = 4 + 2 * (k % 3), 10 + 2 * (k % 3)
                n = it * NS * 2 + 2 * k
                dve.wait_ge(s["s_sexp"], it * NS + (k + 1))
                dve.tensor_tensor(rc[:, 2:4], rs[:, a:a + 2], rs[:, q:q + 2], ALU.add).then_inc(s["s_rc"], 1)
                dve.wait_ge(s["s_rc"], n + 1)
                dve.reciprocal(rc[:, 4:6], rc[:, 2:4]).then_inc(s["s_rc"], 1)
                dve.wait_ge(s["s_rc"], n + 2)
                dve.wait_ge(s["s_pv"], it * NS + (k + 1))
                o = o_all[:, i, :].rearrange("p (b g d) -> p b g d", g=4, d=DH)[:, 2:4, ds(it * 2 + u, 1), :]
                dve.tensor_tensor(o.rearrange("p b g d -> p b (g d)"),
                                  bank[6][:, (k % 2) * P:(k % 2) * P + P].rearrange("p (v d) -> p v d", v=2),
                                  rc[:, 4:6, None].to_broadcast([P, 2, DH]), ALU.mult).then_inc(s["s_od"], 1)

            with dve.Fori(0, 2) as it:
                smax(it, 0)
                for k in range(NS):
                    if k + 1 < NS:
                        smax(it, k + 1)
                    scopy(it, k)
                    if k >= 1:
                        snorm(it, k - 1)
                    if k in WO_AT:
                        c = it * (C // 2) + WO_AT.index(k)
                        dve.wait_ge(s["wo_hi_set"], c + 1)
                        dve.tensor_tensor(w_out_l[:, ds(c, 1), :].rearrange("p a n -> p (a n)"), fox[:, ds(c * D + w_out_at, D)],
                                          w_out_h[:, ds(c, 1), :].rearrange("p a n -> p (a n)").bitcast(F32),
                                          ALU.subtract).then_inc(s["wo_lo_set"], 1)
                snorm(it, NS - 1)

            dve.wait_ge(s["s_od"], 2 * NS + 1)

            def scale_o(i, u):
                dve.wait_ge(s["o_rms"], i + 1)
                dve.reciprocal(st[:, 8 + 2 * u:10 + 2 * u], st[:, 4 + 2 * u:6 + 2 * u]).then_inc(s["o_rstd"], 1)
                dve.wait_ge(s["o_rstd"], i + 1)
                for v in range(2):
                    cols = slice(512 * v, 512 * v + 512)
                    dve.scalar_tensor_tensor(out=on[u][:, cols], in0=o_all[:, ds(i, 1), cols].rearrange("p a n -> p (a n)"),
                                             scalar=st[:, 8 + 2 * u + v:9 + 2 * u + v], in1=g1[:, cols],
                                             op0=ALU.mult, op1=ALU.mult).then_inc(s["on_done"], 1)

            def add_x(i, j, u):
                dve.wait_ge(xr_in[u], j * 16 + 16)
                dve.wait_ge(s["om_done"], i + 1)
                dve.wait_ge(s["on_done"], i * 2 + 2)
                for v in range(2):
                    cols = slice(512 * v, 512 * v + 512)
                    dve.tensor_tensor(o_all[:, ds(i, 1), cols].rearrange("p a n -> p (a n)"), bank[2 + 2 * u + v], xr[u][:, cols],
                                      ALU.add).then_inc(s["x2_done"], 1)

            def scale_h(i, u):
                dve.wait_ge(s["h_rms"], i + 1)
                dve.reciprocal(st[:, 14:15], st[:, 13:14]).then_inc(s["h_rstd"], 1)
                dve.wait_ge(s["h_rstd"], i + 1)
                dve.scalar_tensor_tensor(out=hh[u], in0=o_all[:, ds(i, 1), :].rearrange("p a n -> p (a n)"),
                                         scalar=st[:, 14:15], in1=g0[:, :], op0=ALU.mult, op1=ALU.mult).then_inc(s["h_done"], 1)

            def low_o(i, u):
                if not (isinstance(i, int) and i < 2):
                    dve.wait_ge(s["om_done"], i - 1)
                for b in range(2):
                    dve.wait_ge(s["oTh_done"], i * 2 + (b + 1))
                    dve.tensor_tensor(oTl[u][:, 4 * b:4 * b + 4, :], bank[b].rearrange("p (c k) -> p c k", c=4),
                                      oTh[u][:, 4 * b:4 * b + 4, :].bitcast(F32), ALU.subtract).then_inc(s["oTl_done"], 1)

            for i in range(3):
                scale_o(i, i % 2)
                low_o(i, i % 2)
            dve.wait_ge(s["g_late_in"], 16)
            with dve.Fori(0, 3) as j:
                for u in range(2):
                    scale_o(j * 2 + (u + 3), 1 - u)
                    add_x(j * 2 + u, j, u)
                    scale_h(j * 2 + u, u)
                    low_o(j * 2 + (u + 3), 1 - u)
            for i in (6, 7, 8):
                add_x(i, i // 2, i % 2)
                scale_h(i, i % 2)

            cnt = [0]

            def link(ins):
                cnt[0] += 1
                ins.then_inc(s["r_step"], 1)
                dve.wait_ge(s["r_step"], cnt[0])

            dve.wait_ge(s["r_done"], NT)
            dve.wait_ge(s["h_out_a"], 16 * 5)
            dve.wait_ge(s["h_out_b"], 16 * 4)
            link(dve.tensor_tensor(logit_t, bank[6][:, 0:NT * (GRP + NE)].rearrange("p (t e) -> p t e", t=NT),
                                   br[:, None, :].to_broadcast([P, NT, GRP + NE]), ALU.add))
            iota = cr[:, 0:NE]
            lg, le = logit_t[:, :, 0:GRP], logit_t[:, :, GRP:GRP + NE]

            def first_max(val, n, m, idx_, eq, oh):
                link(dve.tensor_reduce(m, val, AX.X, ALU.max))
                link(dve.tensor_tensor(eq, val, m[:, :, None].to_broadcast([P, NT, n]), ALU.is_equal))
                link(dve.scalar_tensor_tensor(out=eq, in0=eq, scalar=-64.0, in1=iota[:, None, 0:n].to_broadcast([P, NT, n]),
                                              op0=ALU.mult, op1=ALU.add))
                link(dve.tensor_reduce(idx_, eq, AX.X, ALU.min))
                link(dve.tensor_tensor(oh, eq, idx_[:, :, None].to_broadcast([P, NT, n]), ALU.is_equal))

            first_max(lg, GRP, small["m0"], small["i0"], rt["eqg"], rt["ohg"])
            dve.tensor_tensor(rt["lg"], lg, small["m0"][:, :, None].to_broadcast([P, NT, GRP]), ALU.subtract).then_inc(s["r_exp"], 1)
            link(dve.tensor_scalar(rt["ohg"], rt["ohg"], BIG, -BIG, ALU.mult, ALU.add))
            link(dve.tensor_tensor(rt["lem"].rearrange("p t (g e) -> p t g e", g=GRP), le.rearrange("p t (g e) -> p t g e", g=GRP),
                                   rt["ohg"][:, :, :, None].to_broadcast([P, NT, GRP, EPG]), ALU.add))
            first_max(rt["lem"], NE, small["m1"], small["i1"], rt["eq"], rt["oh1"])
            link(dve.scalar_tensor_tensor(out=rt["lem"], in0=rt["oh1"], scalar=-2 * BIG, in1=rt["lem"], op0=ALU.mult, op1=ALU.add))
            first_max(rt["lem"], NE, small["m2"], small["i2"], rt["eq"], rt["oh2"])
            valid = cr[:, NE:NE + NT]
            link(dve.tensor_tensor(rt["tmp"], rt["oh1"], rt["oh2"], ALU.add))
            link(dve.tensor_tensor(maskb[:, :].rearrange("p (t e) -> p t e", t=NT), rt["tmp"],
                                   valid[:, :, None].to_broadcast([P, NT, NE]), ALU.mult))
            runb_t = runb[:, :].rearrange("p (t e) -> p t e", t=NT)
            maskb_t = maskb[:, :].rearrange("p (t e) -> p t e", t=NT)
            link(dve.memset(runb[:, :], 0.0))
            for i in range(1, NT):
                link(dve.tensor_tensor(runb_t[:, i, :], runb_t[:, i - 1, :], maskb_t[:, i - 1, :], ALU.add))
            dve.sem_inc(s["r_mask"], 1)
            link(dve.tensor_tensor(small["m2"], small["m2"], small["m1"], ALU.subtract))
            dve.wait_ge(s["r_exp"], 2)
            link(dve.tensor_reduce(small["den"], rt["eqg"], AX.X, ALU.add))
            dve.sem_inc(s["r_exp"], 1)
            dve.wait_ge(s["r_exp"], 4)
            link(dve.tensor_scalar(small["pg"], small["e21"], 1.0, None, ALU.add))
            link(dve.tensor_tensor(small["den"], small["den"], small["pg"], ALU.mult))
            link(dve.reciprocal(wgt[:, 0:NT], small["den"]))
            link(dve.tensor_tensor(wgt[:, NT:2 * NT], wgt[:, 0:NT], small["e21"], ALU.mult))
            dve.wait_ge(s["r_mm"], 2)
            link(dve.tensor_copy(rt["rank"].rearrange("p t e -> p (t e)"), bank[0][:, 0:NT * NE]))
            cntp = bank[1][:, 0:NE]
            link(dve.tensor_scalar(nov[:, 0, :], cntp, -1.0, 0.0, ALU.add, ALU.max))
            link(dve.tensor_copy(ovi[:, 0:NE], nov[:, 0, :]))
            link(dve.tensor_scalar(ovi[:, NE:2 * NE], ovi[:, 0:NE], 7, None, ALU.logical_shift_right))
            link(dve.tensor_copy(nov[:, 1, :], ovi[:, NE:2 * NE]))
            cur = 1
            for b in range(5):
                sh = 1 << b
                nxt = 2 + b % 2
                link(dve.tensor_copy(nov[:, nxt, :], nov[:, cur, :]))
                link(dve.tensor_tensor(nov[:, nxt, sh:NE], nov[:, cur, sh:NE], nov[:, cur, 0:NE - sh], ALU.add))
                cur = nxt
            incl = nov[:, cur, :]
            link(dve.tensor_tensor(nov[:, 4, :], incl, nov[:, 1, :], ALU.subtract))
            link(dve.scalar_tensor_tensor(out=nov[:, 5, :], in0=nov[:, 4, :], scalar=float(NE - 1), in1=iota,
                                          op0=ALU.add, op1=ALU.subtract))
            link(dve.tensor_copy(qi, rt["rank"].rearrange("p t e -> p (t e)")))
            link(dve.tensor_scalar(qi, qi, 7, None, ALU.logical_shift_right))
            link(dve.tensor_copy(rt["q"].rearrange("p t e -> p (t e)"), qi))
            link(dve.tensor_scalar(rt["tmp"], rt["rank"], float(NTILES), None, ALU.mult))
            link(dve.scalar_tensor_tensor(out=rt["tmp"], in0=rt["q"], scalar=float(1 - P * NTILES), in1=rt["tmp"],
                                          op0=ALU.mult, op1=ALU.add))
            link(dve.tensor_tensor(rt["pos"], rt["tmp"], iota[:, None, :].to_broadcast([P, NT, NE]), ALU.add))
            link(dve.tensor_scalar(rt["q"], rt["q"], 1.0, None, ALU.min))
            link(dve.tensor_tensor(rt["tmp"], rt["q"], nov[:, 5, None, :].to_broadcast([P, NT, NE]), ALU.mult))
            link(dve.tensor_tensor(rt["pos"], rt["pos"], rt["tmp"], ALU.add))
            link(dve.tensor_scalar(small["m0"], valid, float(-SKIP), float(SKIP), ALU.mult, ALU.add))
            for c, oh in enumerate(("oh1", "oh2")):
                link(dve.tensor_tensor(rt[oh], rt[oh], rt["pos"], ALU.mult))
                link(dve.tensor_reduce(small["p1"], rt[oh], AX.X, ALU.add))
                link(dve.tensor_tensor(dest[:, :].rearrange("p (t c) -> p t c", c=2)[:, :, c], small["p1"], small["m0"], ALU.add))
            dve.sem_inc(s["r_mask"], 1)
            link(dve.tensor_tensor(ovc, incl[:, None, :].to_broadcast([P, NOVER, NE]),
                                   iota[:, 0:NOVER, None].to_broadcast([P, NOVER, NE]), ALU.is_le))
            link(dve.tensor_reduce(ovf, ovc, AX.X, ALU.add))
            link(dve.tensor_scalar(ovf, ovf, float(NE - 1), None, ALU.min))
            link(dve.tensor_copy(over[0:1, 1:NOVER + 1], ovf[0:1, :]))
            link(dve.tensor_copy(over[0:1, 0:1], incl[0:1, NE - 1:NE]))
            dve.sem_inc(s["r_mask"], 1)

            def copy_gT(tt, u):
                dve.wait_ge(s["gT_done"], tt * 2 + 2)
                if not (isinstance(tt, int) and tt < 2):
                    dve.wait_ge(s["gu_done"], tt - 1)
                dve.tensor_copy(hgT[u][:, 4:8, :], bank[1].rearrange("p (c k) -> p c k", c=4)).then_inc(s["gT_cv"], 1)

            def gate(tt, u):
                dve.wait_ge(s["e_done"], tt + 1)
                dve.tensor_scalar(ex["s"][u], ex["e"][u], 1.0, None, ALU.add).then_inc(s["ev_step"], 1)
                dve.wait_ge(s["ev_step"], tt * 3 + 1)
                dve.reciprocal(ex["r"][u], ex["s"][u]).then_inc(s["ev_step"], 1)
                dve.wait_ge(s["ev_step"], tt * 3 + 2)
                dve.tensor_tensor(ex["a"][u], ex["r"][u], bank[2 + u][:, 0:FE], ALU.mult).then_inc(s["ev_step"], 1)
                dve.wait_ge(s["ev_step"], tt * 3 + 3)
                dve.tensor_tensor(ex["hid"][u], ex["a"][u], bank[2 + u][:, FE:2 * FE], ALU.mult).then_inc(s["hid_done"], 1)

            def copy_y(tt, u):
                dve.wait_ge(s["dn_done"], tt + 1)
                if not (isinstance(tt, int) and tt < 2):
                    dve.wait_ge(y_out[u], (tt - u) * 8)
                dve.tensor_copy(yo[u][:, 512:D], bank[5]).then_inc(s["y_cv"], 1)

            copy_gT(0, 0)
            copy_gT(1, 1)
            gate(0, 0)

            def estep(tt, u, last=2):
                if last >= 1:
                    gate(tt + 1, 1 - u)
                if last >= 2:
                    copy_gT(tt + 2, u)
                copy_y(tt, u)

            estep(0, 0)
            estep(1, 1)
            with dve.Fori(1, NE // 2 - 1) as j:
                for u in range(2):
                    estep(j * 2 + u, u)
            estep(NE - 2, 0, 1)
            estep(NE - 1, 1, 0)

            n_over = dve.value_load(over[0:1, 0:1], min_val=0, max_val=NOVER)
            with dve.Fori(0, NOVER) as k:
                with dve.If(k < n_over):
                    dve.wait_ge(s["v_gT"], k * 2 + 2)
                    dve.tensor_copy(hgT[0][:, 4:8, :], bank[1].rearrange("p (c k) -> p c k", c=4)).then_inc(s["v_gTc"], 1)
                    dve.wait_ge(s["v_e"], k + 1)
                    dve.tensor_scalar(ex["s"][0], ex["e"][0], 1.0, None, ALU.add).then_inc(s["v_s"], 1)
                    dve.wait_ge(s["v_s"], k * 3 + 1)
                    dve.reciprocal(ex["r"][0], ex["s"][0]).then_inc(s["v_s"], 1)
                    dve.wait_ge(s["v_s"], k * 3 + 2)
                    dve.tensor_tensor(ex["a"][0], ex["r"][0], bank[2][:, 0:FE], ALU.mult).then_inc(s["v_s"], 1)
                    dve.wait_ge(s["v_s"], k * 3 + 3)
                    dve.tensor_tensor(ex["hid"][0], ex["a"][0], bank[2][:, FE:2 * FE], ALU.mult).then_inc(s["v_hid"], 1)
                    dve.wait_ge(s["v_dn"], k + 2)
                    dve.tensor_copy(yo[0][:, 512:D], bank[5]).then_inc(s["v_y"], 1)

            def add_y(i, j, u, rows):
                dve.wait_ge(y_in[u], j * 32 + 32)
                o = o_all[0:rows, ds(i, 1), :].rearrange("p a n -> p (a n)")
                dve.scalar_tensor_tensor(out=o, in0=ya[u][0:rows, :], scalar=wgt[0:rows, ds(i, 1)], in1=o,
                                         op0=ALU.mult, op1=ALU.add).then_inc(s["f_acc"], 1)
                dve.wait_ge(s["f_acc"], i * 2 + 1)
                dve.scalar_tensor_tensor(out=o, in0=yb[u][0:rows, :], scalar=wgt[0:rows, ds(i + NT, 1)], in1=o,
                                         op0=ALU.mult, op1=ALU.add).then_inc(s["f_acc"], 1)

            def scale_f(i, u, rows):
                dve.wait_ge(s["f_rms"], i + 1)
                dve.reciprocal(st[0:rows, 4 + u:5 + u], st[0:rows, 2 + u:3 + u]).then_inc(s["f_rstd"], 1)
                dve.wait_ge(s["f_rstd"], i + 1)
                dve.scalar_tensor_tensor(out=fin[u][0:rows, :], in0=o_all[0:rows, ds(i, 1), :].rearrange("p a n -> p (a n)"),
                                         scalar=st[0:rows, 4 + u:5 + u], in1=g1[0:rows, :],
                                         op0=ALU.mult, op1=ALU.mult).then_inc(s["f_fin"], 1)

            dve.wait_ge(s["g_late_in"], 32)
            add_y(0, 0, 0, P)
            with dve.Fori(0, NP_T // 2 - 1) as j:
                add_y(j * 2 + 1, j, 1, P)
                scale_f(j * 2, 0, P)
                add_y(j * 2 + 2, j + 1, 0, P)
                scale_f(j * 2 + 1, 1, P)
            add_y(7, 3, 1, P)
            scale_f(6, 0, P)
            add_y(8, 4, 0, DEC)
            scale_f(7, 1, P)
            scale_f(8, 0, DEC)

        @block.tensor
        def _(pe):
            pe.wait_ge(s["const_in"], 16)

            def transpose_x(i, u):
                pe.wait_ge(s["xn_done"], i + 1)
                if not (isinstance(i, int) and i < 1):
                    pe.wait_ge(s["xl_done"], i * 2)
                src = xn[u].rearrange("p (k c) -> p c k", c=C)
                for c in range(C):
                    mm = pe.transpose(bank[c // 4][:, (c % 4) * P:(c % 4) * P + P], src[:, c, :], ident)
                    if c % 4 == 3:
                        mm.then_inc(s["xT_done"], 1)

            def three_passes(out, xs, ws):
                for c in range(C):
                    for k, (a, b) in enumerate([(1, 0), (0, 1), (0, 0)]):
                        mm = pe.matmul(out, xs[a](c), ws[b](c), start=(c + k == 0), stop=(c == C - 1 and k == 2))
                return mm

            def x_parts(i):
                return lambda c: xh[:, i * C + c, :], lambda c: xl[:, i * C + c, :]

            def product(copied, k, i):
                pe.wait_ge(s["evac_s" if k % 2 else "evac_v"], copied)
                u = k // NT % 2
                return three_passes(bank[2 + k % 6][:, 0:WG], x_parts(i),
                                    (lambda c: wg_hi[u][:, c, :], lambda c: wg_lo[u][:, c, :]))

            transpose_x(0, 0)
            transpose_x(1, 1)
            for i in range(NT):
                if 1 <= i < NT - 1:
                    transpose_x(i + 1, (i + 1) % 2)
                pe.wait_ge(s["xl_done"], i * 2 + 2)
                if i == 0:
                    pe.wait_ge(s["wg_lo_set"], 2)
                product(i // 2 + 1, i, i)
                three_passes(bank[2 + i % 6][:, WG:WG + NH], x_parts(i),
                             (lambda c: wf_hi[:, c, :], lambda c: wf_lo[:, c, :])).then_inc(s["proj_done"], 1)
            with pe.Fori(0, (NG - 1) // 2) as j:
                for g in (1, 2):
                    pe.wait_ge(s["wg_lo_set"], j * 2 + (g + 2))
                    for i in range(NT):
                        k = g * NT + i
                        product(j * NT + (k // 2 + 1), k, i).then_inc(s["proj_done"], 1)

            pe.wait_ge(s["lf_v"], 4 + NP_T - 1)
            pe.matmul(bank[0][:, 0:NK * NH], upto, lf[:, :], start=True, stop=False)
            pe.matmul(bank[0][:, 0:NK * NH], ones, lsum[:, :], start=False, stop=True).then_inc(s["c_mm"], 1)

            def stage(h1, h6, c3, gi):
                kind, a, b = SG[gi]
                if gi == 0:
                    pe.wait_ge(s["kv_staged"], h1)
                if gi == 0:
                    if not (isinstance(c3, int) and c3 == 0):
                        pe.wait_ge(s["st_copied_v"], c3)
                elif gi <= 3:
                    pe.wait_ge(s["st_copied_s"], c3 + gi)
                else:
                    pe.wait_ge(s["st_copied_v"], c3 + (gi - 3))
                src = qst if kind == "q" else kst
                for m in range(a, b):
                    mm = pe.transpose(bank[7][0:DH + 1, (m - a) * P:(m - a + 1) * P], src[:, m, :], ident)
                mm.then_inc(s["st_T"], 1)

            for gi in range(6):
                stage(1, 0, 0, gi)

            def fqk(it, k):
                u, i = STEPS[k]
                if i == 0:
                    pe.wait_ge(s["st_copied_s"], it * 6 + 3 * (u + 1))
                    pe.wait_ge(s["st_copied_v"], it * 6 + 3 * (u + 1))
                pe.wait_ge(s["exp_done"], it * NS + (k + 1))
                n = nblk[i] * P
                q = qT[u][:, i * P:(i + 1) * P]
                if i < SAMPLE:
                    spans = [(0, 0, min(n, 512))] + ([(512, 512, n - 512)] if n > 512 else [])
                    dg = i * P
                else:
                    spans = [(0, NT * P, PAST), (PAST, SAMPLE * P, P)]
                    dg = PAST
                for at_, k0, w in spans:
                    pe.matmul(ps[k % 2][:, at_:at_ + w], q, kT[u][:, k0:k0 + w], start=(at_ % 512 == 0), stop=False,
                              skip_group_check=True)
                pe.matmul(ps[k % 2][:, dg:dg + P], identb, causal, start=False, stop=True,
                          skip_group_check=True).then_inc(s["qk_done"], 1)

            def ftrans(it, k):
                u, i = STEPS[k]
                nb = nblk[i]
                pe.wait_ge(s["exp_done"], it * NS + (k + 3))
                if k >= 1:
                    pe.wait_ge(s["cp_a"], it * NS + k)
                for b in range(nb):
                    if b == 4:
                        seen = sum(nblk[STEPS[m][1]] > 4 for m in range(k))
                        pe.wait_ge(s["cp_b"], it * 2 * len(TWO) + (seen + 1))
                    mm = pe.transpose(bank[4 + b // 4][:, (b % 4) * P:(b % 4) * P + P], prob[k % 2][:, b * P:(b + 1) * P], ident)
                    if b == min(nb, 4) - 1:
                        mm.then_inc(s["pT_a"], 1)
                if nb > 4:
                    mm.then_inc(s["pT_b"], 1)

            def fpv(it, k):
                u, i = STEPS[k]
                nb = nblk[i]
                pe.wait_ge(s["cp_a"], it * NS + (k + 1))
                if nb > 4:
                    seen = sum(nblk[STEPS[m][1]] > 4 for m in range(k + 1))
                    pe.wait_ge(s["cp_b"], it * 2 * len(TWO) + (seen + 1))
                pe.wait_ge(s["o_done"], it * NS + (k + 1))
                for b in range(nb):
                    m = keytile(i, b)
                    if m < NT:
                        v = fox_t[:, m, ds(it * 2 * DH + (2 * NH * DH + u * DH), DH)]
                    else:
                        v = cv[:, m - NT, ds(it * 2 * DH + u * DH, DH)]
                    mm = pe.matmul(bank[6][:, (k % 2) * DH:(k % 2) * DH + DH], probT[k % 2][:, b * P:(b + 1) * P], v,
                                   start=(b == 0), stop=(b == nb - 1))
                mm.then_inc(s["pv_done"], 1)

            with pe.Fori(0, NH // 2) as it:
                fqk(it, 0)
                for k in range(NS):
                    u, i = STEPS[k]
                    if k + 1 < NS:
                        fqk(it, k + 1)
                    if i in SG_AT:
                        stage(it * 2 + (u + 2), None, it * 6 + 3 * (u + 1), SG_AT[i])
                    ftrans(it, k)
                    if k >= 1:
                        fpv(it, k - 1)
                fpv(it, NS - 1)

            pe.wait_ge(s["o_done"], 4 * NS + 1)
            for gi, (a, b) in enumerate([(0, 4), (4, 8), (8, 10)]):
                if gi == 2:
                    pe.wait_ge(s["s_kcp"], 1)
                for m in range(a, b):
                    src = swa_t[:, m, NH * DH:NH * DH + 2 * DH] if m < NT else skv[:, 0:2 * DH]
                    mm = pe.transpose(bank[4 + gi % 2][:, (m - a) * P:(m - a + 1) * P], src, ident)
                mm.then_inc(s["s_kT"], 1)

            def s_stage(g1_, c3, gi):
                a, b = SSG[gi]
                if gi == 0:
                    pe.wait_ge(s["s_staged"], g1_)
                if not (isinstance(c3, int) and c3 + gi == 0):
                    pe.wait_ge(s["s_qT_cp"], c3 + gi)
                for m in range(a, b):
                    mm = pe.transpose(bank[7][:, (m - a) * P:(m - a + 1) * P], sqst[:, m, :], ident)
                mm.then_inc(s["s_qT_T"], 1)

            for gi in range(3):
                s_stage(1, 0, gi)
            pe.wait_ge(s["s_kcp"], 3)
            pe.wait_ge(s["s_aug"], 3)

            def sqk(it, k):
                u, i = STEPS[k]
                if i == 0:
                    pe.wait_ge(s["s_qT_cp"], it * 6 + 3 * (u + 1))
                if k >= 2:
                    pe.wait_ge(s["s_exp"], it * NS * 2 + 2 * (k - 1))
                for v in range(2):
                    for b in range(1 if i == 0 else 0, 2):
                        m = skeytile(i, b)
                        pe.matmul(ps[k % 2][:, v * 256 + b * P:v * 256 + (b + 1) * P], sqT[u][:, i * P:(i + 1) * P],
                                  skT[v][:, m * P:(m + 1) * P], start=(v == 0 and b == (1 if i == 0 else 0)), stop=False,
                                  skip_group_check=True)
                lo = P if i == 0 else 0
                bias = alibi[:, ds(it * 4 * 256 + u * 2 * 256, 512)].rearrange("p (v n) -> p v n", v=2)[:, :, lo:256]
                pe.matmul(ps[k % 2][:, 0:512].rearrange("p (v n) -> p v n", v=2)[:, :, lo:256], identb, bias,
                          start=False, stop=True, skip_group_check=True).then_inc(s["s_qk"], 1)

            def strans(it, k):
                u, i = STEPS[k]
                pe.wait_ge(s["s_exp"], it * NS * 2 + 2 * (k + 1))
                if k >= 2:
                    pe.wait_ge(s["s_cps"] if k % 2 else s["s_cpv"], it * (NS // 2) + k // 2)
                n = 0
                for v in range(2):
                    for b in range(1 if i == 0 else 0, 2):
                        mm = pe.transpose(bank[4 + k % 2][:, n * P:(n + 1) * P], sprob[k % 2][:, v, b * P:(b + 1) * P], ident)
                        n += 1
                mm.then_inc(s["s_pT"], 1)

            def spv(it, k):
                u, i = STEPS[k]
                if k % 2 == 0:
                    pe.wait_ge(s["s_cpv"], it * (NS // 2) + (k // 2 + 1))
                else:
                    pe.wait_ge(s["s_cps"], it * (NS // 2) + (k // 2 + 1))
                pe.wait_ge(s["s_od"], it * NS + (k + 1))
                n = 0
                for v in range(2):
                    for b in range(1 if i == 0 else 0, 2):
                        m = skeytile(i, b)
                        val = swa_t[:, m, NH * DH + (2 + v) * DH:NH * DH + (3 + v) * DH] if m < NT else skv[:, (2 + v) * DH:(3 + v) * DH]
                        mm = pe.matmul(bank[6][:, (k % 2) * P + v * DH:(k % 2) * P + (v + 1) * DH],
                                       sprobT[k % 2][:, n * P:(n + 1) * P], val,
                                       start=(b == (1 if i == 0 else 0)), stop=(b == 1))
                        n += 1
                mm.then_inc(s["s_pv"], 1)

            with pe.Fori(0, 2) as it:
                sqk(it, 0)
                for k in range(NS):
                    u, i = STEPS[k]
                    if k + 1 < NS:
                        sqk(it, k + 1)
                    if i in SSG_AT:
                        s_stage(it * 2 + (u + 2), it * 6 + 3 * (u + 1), SSG_AT[i])
                    strans(it, k)
                    if k >= 1:
                        spv(it, k - 1)
                spv(it, NS - 1)

            def transpose_o(i, u):
                pe.wait_ge(s["on_done"], i * 2 + 2)
                if not isinstance(i, int) or i >= 3:
                    pe.wait_ge(s["hT_copied"], i * 2 - 4)
                elif i > 0:
                    pe.wait_ge(s["oTl_done"], i * 2)
                for c in range(C):
                    mm = pe.transpose(bank[c // 4][:, (c % 4) * P:(c % 4) * P + P], on[u][:, c * P:(c + 1) * P], ident)
                    if c % 4 == 3:
                        mm.then_inc(s["oT_done"], 1)

            def out_proj(i, u):
                pe.wait_ge(s["oTl_done"], i * 2 + 2)
                if not (isinstance(i, int) and i < 2):
                    pe.wait_ge(s["x2_done"], i * 2 - 2)
                for n in range(2):
                    mm = three_passes(bank[2 + 2 * u + n], (lambda c: oTh[u][:, c, :], lambda c: oTl[u][:, c, :]),
                                      (lambda c: w_out_h[:, c, 512 * n:512 * n + 512], lambda c: w_out_l[:, c, 512 * n:512 * n + 512]))
                mm.then_inc(s["om_done"], 1)

            def transpose_h(i, u, last):
                pe.wait_ge(s["h_done"], i + 1)
                pe.wait_ge(s["oTl_done"], last * 2 + 2)
                if not (isinstance(i, int) and i < 1):
                    pe.wait_ge(s["hT_copied"], i * 2)
                src = hh[u].rearrange("p (k c) -> p c k", c=C)
                for c in range(C):
                    mm = pe.transpose(bank[c // 4][:, (c % 4) * P:(c % 4) * P + P], src[:, c, :], ident)
                    if c % 4 == 3:
                        mm.then_inc(s["hT_done"], 1)

            def router(i):
                pe.wait_ge(s["hT_copied"], i * 2 + 2)
                for c in range(C):
                    mm = pe.matmul(bank[6][:, ds(i * (GRP + NE), GRP + NE)], hhT[:, c, :], wr_t[:, c, :],
                                   start=(c == 0), stop=(c == C - 1))
                mm.then_inc(s["r_done"], 1)

            def ostep(i, u, more=True):
                if not (isinstance(i, int) and i == NT - 1):
                    out_proj(i + 1, 1 - u)
                if not (isinstance(i, int) and i == 0):
                    router(i - 1)
                transpose_h(i, u, i + 2 if more else NT - 1)
                if more:
                    transpose_o(i + 3, 1 - u)

            pe.wait_ge(s["s_od"], 2 * NS + 1)
            transpose_o(0, 0)
            transpose_o(1, 1)
            pe.wait_ge(s["wo_lo_set"], C)
            out_proj(0, 0)
            transpose_o(2, 0)
            for i in (0, 1):
                ostep(i, i)
            with pe.Fori(1, 3) as j:
                for u in range(2):
                    ostep(j * 2 + u, u)
            for i in (6, 7, 8):
                ostep(i, i % 2, False)
            router(8)

            pe.wait_ge(s["r_mask"], 1)
            pe.matmul(bank[0][:, 0:NT * NE], before, maskb[:, :], start=True, stop=False)
            pe.matmul(bank[0][:, 0:NT * NE], onesb, runb[:, :], start=False, stop=True).then_inc(s["r_mm"], 1)
            pe.matmul(bank[1][:, 0:NE], onesb, runb[:, (NT - 1) * NE:NT * NE], start=True, stop=False)
            pe.matmul(bank[1][:, 0:NE], onesb, maskb[:, (NT - 1) * NE:NT * NE], start=False, stop=True).then_inc(s["r_mm"], 1)

            def transpose_g(u, sig):
                src = hg[u].rearrange("p (k c) -> p c k", c=C)
                for c in range(C):
                    mm = pe.transpose(bank[c // 4][:, (c % 4) * P:(c % 4) * P + P], src[:, c, :], ident)
                    if c % 4 == 3:
                        mm.then_inc(sig, 1)

            def gate_up(u, w, sig):
                wv = w[:, 0:2 * D].rearrange("p (m c f) -> p c m f", m=2, c=C)
                for c in range(C):
                    mm = pe.matmul(bank[2 + u][:, 0:2 * FE].rearrange("p (m f) -> p m f", m=2), hgT[u][:, c, :], wv[:, c, :, :],
                                   start=(c == 0), stop=(c == C - 1))
                mm.then_inc(sig, 1)

            def down(u, w, sig):
                for n in range(2):
                    mm = pe.matmul(bank[4 + n], ex["hidT"][u], w[:, 2 * D + 512 * n:2 * D + 512 * n + 512], start=True, stop=True)
                mm.then_inc(sig, 1)

            def tg(tt, j, k):
                pe.wait_ge(g_in[k], j * 16 + 16)
                if not (isinstance(tt, int) and tt < 1):
                    pe.wait_ge(s["gT_cs"], tt)
                    pe.wait_ge(s["gT_cv"], tt)
                transpose_g(k, s["gT_done"])

            def gu(tt, j, k):
                u = k % 2
                pe.wait_ge(w_in_slot[k], j * 48 + 48)
                pe.wait_ge(s["gT_cs"], tt + 1)
                pe.wait_ge(s["gT_cv"], tt + 1)
                if not (isinstance(tt, int) and tt < 2):
                    pe.wait_ge(s["hid_done"], tt - 1)
                gate_up(u, wslot[k], s["gu_done"])

            def hd(tt, k):
                u = k % 2
                pe.wait_ge(s["hid_done"], tt + 1)
                if not (isinstance(tt, int) and tt < 1):
                    pe.wait_ge(s["hidT_cp"], tt)
                pe.transpose(bank[6][:, 0:P], ex["hid"][u], ident).then_inc(s["hidT_done"], 1)

            def dn(tt, k):
                pe.wait_ge(s["hidT_cp"], tt + 1)
                if not (isinstance(tt, int) and tt < 1):
                    pe.wait_ge(s["y_cs"], tt)
                    pe.wait_ge(s["y_cv"], tt)
                down(k % 2, wslot[k], s["dn_done"])

            def estep(tt, j4, k, last=2):
                if last >= 1:
                    gu(tt + 1, j4 + (k + 1) // NSLOT, (k + 1) % NSLOT)
                hd(tt, k)
                if last >= 2:
                    tg(tt + 2, j4 + (k + 2) // 4, (k + 2) % 4)
                dn(tt, k)

            pe.wait_ge(s["r_mask"], 3)
            tg(0, 0, 0)
            tg(1, 0, 1)
            gu(0, 0, 0)
            for tt in range(4):
                estep(tt, 0, tt)
            with pe.Fori(1, NE // NSLOT - 1) as j:
                for k in range(NSLOT):
                    estep(j * NSLOT + k, j, k)
            for tt in range(NE - NSLOT, NE):
                estep(tt, tt // NSLOT, tt % NSLOT, min(2, NE - 1 - tt))

            pe.sem_inc(s["v_dn"], 1)
            n_over = pe.value_load(over[0:1, 0:1], min_val=0, max_val=NOVER)
            with pe.Fori(0, NOVER) as k:
                with pe.If(k < n_over):
                    pe.wait_ge(s["v_g"], k * 16 + 16)
                    transpose_g(0, s["v_gT"])
                    pe.wait_ge(s["v_gTc"], k * 2 + 2)
                    pe.wait_ge(s["v_w"], k * 48 + 48)
                    gate_up(0, wslot[0], s["v_gu"])
                    pe.wait_ge(s["v_hid"], k + 1)
                    pe.transpose(bank[6][:, 0:P], ex["hid"][0], ident).then_inc(s["v_hT"], 1)
                    pe.wait_ge(s["v_hTc"], k + 1)
                    down(0, wslot[0], s["v_dn"])
            pe.wait_ge(s["experts_done"], 1)


_INS = ['x_prompt', 'x_sample', 'cache_fox_k', 'cache_fox_v', 'cache_fox_logf', 'cache_swa_k', 'cache_swa_v',
        'g_mix_norm', 'w_in', 'b_forget', 'swa_sinks', 'g_fox_out', 'g_swa_out', 'w_out', 'g_ffn_norm',
        'w_router_group', 'b_router_group', 'w_router_expert', 'b_router_expert', 'w_gate', 'w_up', 'w_down', 'g_final']
_OUTS = [('y_prompt', (1, SEQ, D)), ('y_sample', (1, DEC, D)),
         ('fox_k_prompt', (1, 1, SEQ, NH, DH)), ('fox_v_prompt', (1, 1, SEQ, NH, DH)), ('fox_logf_prompt', (1, 1, SEQ, NH)),
         ('swa_k_prompt', (1, 1, WIN, 2, DH)), ('swa_v_prompt', (1, 1, WIN, 2, DH)),
         ('fox_k_sample', (1, 1, DEC, NH, DH)), ('fox_v_sample', (1, 1, DEC, NH, DH)), ('fox_logf_sample', (1, 1, DEC, NH)),
         ('swa_k_sample', (1, 1, DEC, 2, DH)), ('swa_v_sample', (1, 1, DEC, 2, DH))]


def constants():
    r = np.arange(P)
    const_f = np.concatenate([np.eye(P), r[:, None] <= r[None, :], np.ones((P, P))], axis=1).astype(np.float32)
    causal = np.where(r[None, :] <= r[:, None], 0.0, -BIG)
    k = np.arange(2 * P)
    dist = np.abs(r[:, None] + P - k[None, :])
    behind = r[:, None] // 64 + 2 - k[None, :] // 64
    seen = (behind >= 0) & (behind <= 2)
    slope = 2.0 ** -(np.arange(NH) + 1.0)
    bias = np.where(seen[:, None, :], -slope[None, :, None] * dist[:, None, :], -BIG)
    bias = bias.reshape(P, 2, 4, 2 * P).transpose(0, 2, 1, 3).reshape(P, 2 * NH * P)
    const_b = np.concatenate([np.eye(P), causal, r[:, None] < r[None, :], np.ones((P, P)), bias], axis=1).astype(mybir.dt.np(BF16))
    tok = np.arange(NT)[None, :, None] * P + r[:, None, None]
    const_i = np.stack([np.broadcast_to(tok, (P, NT, 2)), tok + TOK * np.arange(2)[None, None, :]], axis=-1)
    const_i = const_i.reshape(P, NT * 4).astype(np.int32)
    exists = (np.arange(NT)[None, :] * P + r[:, None]) < SEQ + DEC
    const_r = np.concatenate([np.broadcast_to(np.arange(NE), (P, NE)), exists], axis=1).astype(np.float32)
    return {"const_f": const_f, "const_b": const_b, "const_i": const_i, "const_r": const_r}


def kernel(**inputs):
    import concourse.bacc as _bacc
    from concourse.bass_utils import run_bass_kernel_spmd as _run

    nc = _bacc.Bacc("TRN2", target_bir_lowering=False, num_devices=1)
    arrays, t = {}, {}
    for name, a in [(n, inputs[n]) for n in _INS] + list(constants().items()):
        a = np.ascontiguousarray(a)
        arrays[f"in_{name}"] = a
        t[name] = nc.dram_tensor(f"in_{name}", a.shape, mybir.dt.from_np(a.dtype), kind="ExternalInput").ap()
    for name, shape in _OUTS:
        t[name] = nc.dram_tensor(f"out_{name}", shape, F32, kind="ExternalOutput").ap()
    build(nc, t)
    r = _run(nc, [arrays], core_ids=[0])
    return tuple(r.results[0][f"out_{name}"] for name, _ in _OUTS)
```

```python
from contextlib import ExitStack

import concourse.bass as bass
import numpy as np
from concourse import mybir

F32 = mybir.dt.float32
F32R = mybir.dt.float32r
BF16 = mybir.dt.bfloat16
I32 = mybir.dt.int32
ALU = mybir.AluOpType
ACT = mybir.ActivationFunctionType
AX = mybir.AxisListType

P = 128
D = 1024
C = D // P
SEQ, DEC, PAST, WIN = 1024, 64, 256, 128
NP_T = SEQ // P
NT = NP_T + 1
SAMPLE = NP_T
NK = NT + PAST // P
DH = 64
NH = 8
QKV = 3 * NH * DH
SWA = NH * DH + 2 * 2 * DH
PROJ = QKV + NH + SWA
GRP, EPG = 4, 8
NE = GRP * EPG
FE = 128
NOVER = 2 * NT * P // P - 2
NTILES = NE + NOVER
TOK = NT * P
SCALE = DH ** -0.5
EPS = 1e-6
BIG = 1.0e30
SKIP = 1 << 20
WSLOT = 3 * D
NSLOT = 8
WG = 256
NG = (PROJ - NH) // WG
FOX_G = QKV // WG


def build(nc, t):
    ctx = ExitStack()
    with ctx:
        def sb(name, shape, dt=F32):
            return ctx.enter_context(nc.sbuf_tensor(name, shape, dt))

        def sem(name):
            return ctx.enter_context(nc.semaphore(name))

        ds = bass.ds

        def sb_at(name, shape):
            at_ = -(-nc.sbuf_base // 32) * 32
            return sb(name, shape), at_

        def rounded(name, base, first, *shape):
            n_ = int(np.prod(shape))
            r = nc.alloc_sbuf_tensor_at(name, [P, n_], F32R, offset=base + 4 * first)
            return r[:, :] if len(shape) == 1 else r[:, :].rearrange("p (a b) -> p a b", b=shape[1])

        def cut(region, at, *shape):
            n = int(np.prod(shape))
            ap = region[:, at:at + n]
            if len(shape) == 2:
                ap = ap.rearrange("p (a b) -> p a b", b=shape[1])
            return ap

        big, big_at = sb_at("big", [P, C * PROJ])
        xh = rounded("xh", big_at, 0, NT * C, P)
        xl = rounded("xl", big_at, NT * D, NT * C, P)
        assert 2 * NT * D <= C * PROJ
        o_all = big[:, 0:NT * D].rearrange("p (t n) -> p t n", t=NT)
        free0 = NT * D

        kT = [cut(big, free0 + u * NK * P, NK * P) for u in range(2)]
        qT = [cut(big, free0 + 2 * NK * P + u * NT * P, NT * P) for u in range(2)]
        at = free0 + 2 * NK * P + 2 * NT * P
        prob = [cut(big, at + u * SEQ, SEQ) for u in range(2)]
        probT = [cut(big, at + (2 + u) * SEQ, SEQ) for u in range(2)]
        skT = [cut(big, free0 + v * (NT + 1) * P, (NT + 1) * P) for v in range(2)]
        at = free0 + 2 * (NT + 1) * P
        sqT = [cut(big, at + u * NT * P, NT * P) for u in range(2)]
        at += 2 * NT * P
        sprob = [cut(big, at + u * 4 * P, 2, 2 * P) for u in range(2)]
        sprobT = [cut(big, at + (2 + u) * 4 * P, 4 * P) for u in range(2)]
        assert at + 8 * P * 2 <= free0 + 7 * D
        xr = [cut(big, free0 + u * D, D) for u in range(2)]
        on = [cut(big, free0 + (7 + u) * D, D) for u in range(2)]
        hh = [cut(big, free0 + (2 + u) * D, D) for u in range(2)]
        hhT = [cut(big, free0 + (4 + u) * D, C, P) for u in range(2)]
        at = free0
        rt = {}
        for name in ("lem", "eq", "oh1", "oh2", "run", "rank", "pos", "tmp", "q"):
            rt[name] = cut(big, at, NT, NE)
            at += NT * NE
        qi = cut(big, at, NT * NE).bitcast(I32)
        at += NT * NE
        for name in ("lg", "ohg", "eqg"):
            rt[name] = cut(big, at, NT, GRP)
            at += NT * GRP
        small = {}
        for name in ("m0", "m1", "m2", "i0", "i1", "i2", "den", "pg", "e21", "w1", "w2", "p1", "p2"):
            small[name] = cut(big, at, NT)
            at += NT
        nov = cut(big, at, 7, NE)
        at += 7 * NE
        ovi = cut(big, at, 2 * NE).bitcast(I32)
        at += 2 * NE
        ovc = cut(big, at, NOVER, NE)
        at += NOVER * NE
        ovf = cut(big, at, NOVER)
        at += NOVER
        ex = {}
        for name in ("e", "s", "r", "a", "hid", "hidT"):
            ex[name] = [cut(big, at + u * FE, FE) for u in range(2)]
            at += 2 * FE
        logit_t = cut(big, at, NT, GRP + NE)
        at += NT * (GRP + NE)
        maskb = cut(big, at, NT * NE // 2).bitcast(BF16)
        at += NT * NE // 2
        runb = cut(big, at, NT * NE // 2).bitcast(BF16)
        at += NT * NE // 2
        idx = cut(big, at, 8).bitcast(I32)
        at += 8
        ids = cut(big, at, 2 * NTILES).bitcast(I32)
        at += 2 * NTILES
        assert at <= C * PROJ - WSLOT
        fin = [cut(big, free0 + 7 * D + u * D, D) for u in range(2)]

        fox, fox_at = sb_at("fox", [P, NT * QKV + WSLOT])
        fox_t = fox[:, 0:NT * QKV].rearrange("p (t n) -> p t n", t=NT)
        w_out_h = rounded("w_out_h", fox_at, 0, C, D)
        swa, swa_at = sb_at("swa", [P, NT * SWA])
        swa_t = swa[:, :].rearrange("p (t n) -> p t n", t=NT)
        w_out_at = NT * QKV + WSLOT - C * D
        w_out_raw = fox[:, w_out_at:w_out_at + C * D]
        w_out_l = rounded("w_out_l", fox_at, w_out_at, C, D)
        wslot = ([cut(swa, k * WSLOT, WSLOT) for k in range(2)] + [cut(fox, k * WSLOT, WSLOT) for k in range(5)]
                 + [cut(big, C * PROJ - WSLOT, WSLOT)])
        assert C * D <= w_out_at and 2 * WSLOT <= NT * SWA and 5 * WSLOT + D <= NT * QKV + WSLOT
        ya = [cut(fox, 2 * WSLOT + u * D, D) for u in range(4)]
        yb = [cut(fox, 2 * WSLOT + (4 + u) * D, D) for u in range(4)]
        work, work_at = sb_at("work", [P, 6 * D])
        x = [cut(work, u * D, D) for u in (0, 1, 4, 5)]
        xn = [cut(work, (2 + u) * D, D) for u in range(2)]
        wg_raw = [cut(work, 4 * D, C, WG), cut(work, 0, C, WG)]
        wg_lo = [rounded("wg_lo0", work_at, 4 * D, C, WG), rounded("wg_lo1", work_at, 0, C, WG)]
        wg_hi = [rounded("wg_hi0", fox_at, NT * QKV, C, WG), rounded("wg_hi1", work_at, 2 * D, C, WG)]
        WF = WG + NH
        w0_raw = cut(swa, 0, C, WF)
        w0_lo, w0_hi = rounded("w0_lo", swa_at, 0, C, WF), rounded("w0_hi", swa_at, C * WF, C, WF)
        at = 0
        ck = cut(work, at, 2, (NH + 1) * DH)
        at += 2 * (NH + 1) * DH
        cv = cut(work, at, 2, NH * DH)
        at += 2 * NH * DH
        kst = cut(work, at, NK, DH + 1)
        at += NK * (DH + 1)
        qst = cut(work, at, NT, DH + 1)
        at += NT * (DH + 1)
        skv = cut(work, at, 2 * 2 * DH)
        at += 2 * 2 * DH
        assert at <= 4 * D
        sqst = cut(work, at, NT, P)
        at += NT * P
        assert at <= 6 * D
        at = NT * QKV + C * WG
        lz = cut(fox, at, 3 * NT * NH)
        at += 3 * NT * NH
        lsum = cut(fox, at, NK * NH)
        lsum_t = cut(fox, at, NK, NH)
        assert at + NK * NH <= NT * QKV + WSLOT
        hgT = [cut(work, (2 + u) * D, C, P) for u in range(2)]
        oTh = [rounded(f"oTh{u}", work_at, u * D, C, P) for u in range(2)]
        oTl = [rounded(f"oTl{u}", work_at, (2 + u) * D, C, P) for u in range(2)]

        cf = sb("cf", [P, 3 * P])
        ident, upto, ones = cf[:, 0:P], cf[:, P:2 * P], cf[:, 2 * P:3 * P]
        cb = sb("cb", [P, 4 * P + 2 * NH * P], BF16)
        identb, causal, before, onesb = (cb[:, n * P:(n + 1) * P] for n in range(4))
        alibi = cb[:, 4 * P:4 * P + 2 * NH * P]
        ci = sb("ci", [P, NT * 4], I32)
        cr = sb("cr", [P, NE + NT])
        g0 = sb("g0", [P, D])
        hg = [cut(work, 0, D), cut(work, D, D), cut(fox, 5 * WSLOT, D), g0[:, :]]
        g1 = sb("g1", [P, D])
        assert 2 * NH * P == 2 * D
        yo = [cut(work, 4 * D, D), cut(work, 5 * D, D), g1[:, :], alibi.bitcast(F32)]
        bf = sb("bf", [P, NH])
        sink = sb("sink", [P, NH])
        nsink = sb("nsink", [P, NH])
        sraw = sb("sraw", [P, NH])
        br = sb("br", [P, GRP + NE])
        wr = sb("wr", [P, C * (GRP + NE)])
        wr_t = wr[:, :].rearrange("p (c e) -> p c e", c=C)
        lf = sb("lf", [P, NK * NH])
        lf_t = lf[:, :].rearrange("p (t h) -> p t h", t=NK)
        negc = sb("negc", [P, NK * (NH + 1)])
        negc_t = negc[:, :].rearrange("p (t h) -> p t h", t=NK)
        st = sb("st", [P, 16])
        eps = sb("eps", [P, 2])
        nm = sb("nm", [P, 16])
        rs = sb("rs", [P, 16])
        rc = sb("rc", [P, 8])
        wgt = sb("wgt", [P, 2 * NT])
        dest = sb("dest", [P, 2 * NT], I32)
        over = sb("over", [1, NOVER + 1], I32)

        ps = [ctx.enter_context(nc.psum_tensor(f"ps{b}", [P, 1024], F32)) for b in range(4)]
        bank = [ps[b // 2][:, 512 * (b % 2):512 * (b % 2) + 512] for b in range(8)]

        h_dram = nc.dram_tensor("h_rows", (TOK, D), F32, kind="Internal").ap()
        y_dram = nc.dram_tensor("y_rows", (2 * TOK, D), F32, kind="Internal").ap()
        id_dram = nc.dram_tensor("id_rows", (P * NTILES, 2), I32, kind="Internal").ap()

        names = """const_in gain_in small_in w0_in cache_in kv_out w_out_in g_late_in eps_set
            square_done rms_done rstd_done xn_done xT_done xh_done xl_done wg_hi_set wg_lo_set proj_done evac_v evac_s
            lf_v lf_s c_mm c_ready wo_hi_set wo_lo_set
            pad_set aug_set kv_staged st_T st_copied_s st_copied_v qk_done nmax_done exp_done pT_a pT_b cp_a cp_b pv_done o_done recip
            s_aug s_staged s_kT s_kcp s_qT_T s_qT_cp s_qk s_nm s_nmc s_exp s_sexp s_pT s_cpv s_cps s_pv s_rc s_od
            o_stat o_rms o_rstd on_done oT_done oTh_done oTl_done om_done x2_done h_stat h_rms h_rstd h_done h_out_a h_out_b hT_done hT_copied r_done
            r_step r_exp r_mask r_mm r_id id_init id_out id_in
            pool_went idx_set dst_set gT_done gT_cs gT_cv gu_done e_done ev_step hid_done hidT_done hidT_cp dn_done y_cs y_cv hg_set
            v_idx v_g v_w v_gT v_gTc v_gu v_e v_s v_hid v_hT v_hTc v_dn v_y v_out experts_done
            f_acc f_stat f_rms f_rstd f_fin f_out_a f_out_b""".split()
        s = {n: sem(n) for n in names}
        wg_in = [sem(f"wg_in{u}") for u in range(2)]
        x_in = [sem(f"x_in{u}") for u in range(4)]
        xr_in = [sem(f"xr_in{u}") for u in range(2)]
        w_in_slot = [sem(f"w_in_slot{k}") for k in range(NSLOT)]
        g_in = [sem(f"g_in{u}") for u in range(4)]
        y_out = [sem(f"y_out{u}") for u in range(4)]
        y_in = [sem(f"y_in{u}") for u in range(4)]

        x_rows = t["x_prompt"].rearrange("a s d -> (a s) d")
        xs_rows = t["x_sample"].rearrange("a s d -> (a s) d")
        w_in_dram = t["w_in"].rearrange("l (p c) n -> p (l c) n", c=C)

        def wg_cols(g):
            at_ = g * WG + (NH if g >= FOX_G else 0)
            return w_in_dram[:, :, at_:at_ + WG]

        def wg_dest(g, i):
            to, c0 = (fox_t, g * WG) if g < FOX_G else (swa_t, (g - FOX_G) * WG)
            return to[:, i, c0:c0 + WG]

        def row(ap, n):
            return ap.rearrange("(a n) -> a n", a=1).broadcast_to([P, n])

        EVAC_V, EVAC_S = 3 + (NG * NT + 1) // 2, 3 + NG * NT // 2
        STEPS = [(u, i) for u in range(2) for i in range(NT)]
        NS = len(STEPS)
        nblk = [i + 1 for i in range(NP_T)] + [1 + PAST // P]
        TWO = [i for i in range(NT) if nblk[i] > 4]
        SG = [("q", 0, 4), ("q", 4, 8), ("q", 8, 9), ("k", 0, 4), ("k", 4, 8), ("k", 8, 11)]
        SG_AT = {2: 0, 3: 1, 4: 2, 5: 3, 6: 4, 7: 5}
        SSG = [(0, 4), (4, 8), (8, 9)]
        SSG_AT = {2: 0, 4: 1, 6: 2}

        WO_AT = (4, 8, 12, 16)

        def keytile(i, b):
            return b if i < SAMPLE else [NT, NT + 1, SAMPLE][b]

        def skeytile(i, b):
            return i - 1 + b if i < SAMPLE else [NT, SAMPLE][b]

        block = ctx.enter_context(nc.Block())

        @block.sync
        def _(sp):
            sp.dma_start(x[0], x_rows[0:P, :]).then_inc(x_in[0], 16)
            sp.dma_start(g0[:, :], row(t["g_mix_norm"].rearrange("l d -> (l d)"), D)).then_inc(s["gain_in"], 16)
            sp.dma_start(cf[:, :], t["const_f"]).then_inc(s["const_in"], 16)
            sp.dma_start(w0_raw[:, :, 0:WG], wg_cols(0)).then_inc(s["w0_in"], 16)
            sp.dma_start(w0_raw[:, :, WG:WF], w_in_dram[:, :, QKV:QKV + NH]).then_inc(s["w0_in"], 16)
            for i in range(1, 4):
                sp.dma_start(x[i], x_rows[i * P:(i + 1) * P, :]).then_inc(x_in[i], 16)
            small_loads = [
                (cb[:, :], t["const_b"]), (ci[:, :], t["const_i"]), (cr[:, :], t["const_r"]),
                (bf[:, :], row(t["b_forget"].rearrange("l d -> (l d)"), NH)),
                (sraw[:, :], row(t["swa_sinks"].rearrange("l d -> (l d)"), NH)),
                (br[:, 0:GRP], row(t["b_router_group"].rearrange("l d -> (l d)"), GRP)),
                (br[:, GRP:GRP + NE], row(t["b_router_expert"].rearrange("l d -> (l d)"), NE)),
                (wr_t[:, :, 0:GRP], t["w_router_group"].rearrange("l (p c) n -> p (l c) n", c=C)),
                (wr_t[:, :, GRP:GRP + NE], t["w_router_expert"].rearrange("l (p c) n -> p (l c) n", c=C)),
                (lf_t[:, NT:NK, :], t["cache_fox_logf"].rearrange("l b (t p) h -> p (l b t) h", p=P)),
                (g1[:, 0:512], row(t["g_fox_out"].rearrange("l d -> (l d)"), 512)),
                (g1[:, 512:D], row(t["g_swa_out"].rearrange("l d -> (l d)"), 512)),
            ]
            for dst, src in small_loads:
                sp.dma_start(dst, src).then_inc(s["small_in"], 16)
            for i in range(4, NT):
                sp.wait_ge(s["xn_done"], i - 3)
                if i < SAMPLE:
                    sp.dma_start(x[i % 4], x_rows[i * P:(i + 1) * P, :]).then_inc(x_in[i % 4], 16)
                else:
                    sp.dma_start(x[i % 4][0:DEC, :], xs_rows).then_inc(x_in[i % 4], 16)
            sp.wait_ge(s["xn_done"], NT)
            for g in range(1, NG):
                if g >= 3:
                    sp.wait_ge(s["proj_done"], NT * (g - 1))
                sp.dma_start(wg_raw[g % 2], wg_cols(g)).then_inc(wg_in[g % 2], 16)
            sp.wait_ge(s["proj_done"], NT * (NG - 1))
            sp.dma_start(ck[:, :, 0:NH * DH], t["cache_fox_k"].rearrange("l b (t p) h d -> p (l b t) (h d)", p=P)).then_inc(s["cache_in"], 16)
            sp.dma_start(cv[:, :, :], t["cache_fox_v"].rearrange("l b (t p) h d -> p (l b t) (h d)", p=P)).then_inc(s["cache_in"], 16)
            sp.dma_start(skv[:, 0:2 * DH], t["cache_swa_k"].rearrange("l b p h d -> p (l b h d)")).then_inc(s["cache_in"], 16)
            sp.dma_start(skv[:, 2 * DH:4 * DH], t["cache_swa_v"].rearrange("l b p h d -> p (l b h d)")).then_inc(s["cache_in"], 16)
            sp.wait_ge(s["evac_v"], EVAC_V)
            sp.wait_ge(s["evac_s"], EVAC_S)
            sp.dma_start(g0[:, :], row(t["g_ffn_norm"].rearrange("l d -> (l d)"), D)).then_inc(s["g_late_in"], 16)
            for n, name in ((1, "fox_k"), (2, "fox_v")):
                cols = slice(n * 512, (n + 1) * 512)
                sp.dma_start(t[name + "_prompt"].rearrange("l b (t p) h d -> p (l b t) (h d)", p=P),
                             fox_t[:, 0:NP_T, cols]).then_inc(s["kv_out"], 16)
                sp.dma_start(t[name + "_sample"].rearrange("l b s h d -> (l b s) (h d)"),
                             fox_t[0:DEC, SAMPLE, cols]).then_inc(s["kv_out"], 16)
            for n, name in ((4, "swa_k"), (5, "swa_v")):
                cols = slice(n * P, (n + 1) * P)
                sp.dma_start(t[name + "_prompt"].rearrange("l b s h d -> (l b s) (h d)"),
                             swa_t[:, NP_T - 1, cols]).then_inc(s["kv_out"], 16)
                sp.dma_start(t[name + "_sample"].rearrange("l b s h d -> (l b s) (h d)"),
                             swa_t[0:DEC, SAMPLE, cols]).then_inc(s["kv_out"], 16)
            sp.wait_ge(s["lf_v"], 3)
            sp.dma_start(t["fox_logf_prompt"].rearrange("l b (t p) h -> p (l b t) h", p=P),
                         lf_t[:, 0:NP_T, :]).then_inc(s["kv_out"], 16)
            sp.dma_start(t["fox_logf_sample"].rearrange("l b s h -> (l b s) h"),
                         lf_t[0:DEC, SAMPLE, :]).then_inc(s["kv_out"], 16)
            sp.wait_ge(s["kv_out"], 16 * 10)
            sp.wait_ge(s["pv_done"], 4 * NS)
            sp.wait_ge(s["kv_staged"], NH + 1)
            sp.dma_start(w_out_raw.rearrange("p (c n) -> p c n", c=C), t["w_out"].rearrange("l (c p) n -> p (l c) n", p=P)).then_inc(s["w_out_in"], 16)

            def gate_up(e, k):
                for n, w in ((0, wg), (1, wu)):
                    sp.dma_start(wslot[k][:, n * D:(n + 1) * D].rearrange("p (c f) -> p c f", c=C),
                                 w[ds(e, 1)].rearrange("e p c f -> p (e c) f")).then_inc(w_in_slot[k], 16)

            def down(e, k):
                sp.dma_start(wslot[k][:, 2 * D:3 * D], wd[ds(e, 1)].rearrange("e f d -> (e f) d")).then_inc(w_in_slot[k], 16)

            def expert(k):
                gate_up(k, k)
                down(k, k)

            wg = t["w_gate"].rearrange("l e (p c) f -> (l e) p c f", c=C)
            wu = t["w_up"].rearrange("l e (p c) f -> (l e) p c f", c=C)
            wd = t["w_down"].rearrange("l e f d -> (l e) f d")
            sp.wait_ge(s["s_pv"], 2 * NS)
            for k in (0, 1):
                expert(k)
            def load_xr(i, u, rows):
                src = x_rows[ds(i * P, P), :] if rows == P else xs_rows
                sp.dma_start(xr[u][0:rows, :], src).then_inc(xr_in[u], 16)

            for u in range(2):
                load_xr(u, u, P)

            def send_h(i, u):
                sp.wait_ge(s["h_done"], i + 1)
                sp.dma_start(h_dram[ds(i * P, P), :], hh[u]).then_inc(s["h_out_b" if u else "h_out_a"], 16)

            with sp.Fori(0, NP_T // 2 - 1) as j:
                for u in range(2):
                    sp.wait_ge(s["x2_done"], (j * 2 + (u + 1)) * 2)
                    load_xr(j * 2 + (u + 2), u, P)
                    send_h(j * 2 + u, u)
            sp.wait_ge(s["x2_done"], (NT - 2) * 2)
            load_xr(NT - 1, 0, DEC)
            for i in range(NT - 3, NT):
                send_h(i, i % 2)
            sp.wait_ge(s["om_done"], NT)
            for k in (2, 3, 4):
                expert(k)
            sp.wait_ge(s["r_id"], 1)
            sp.dma_start(id_dram.rearrange("(p t) w -> p (t w)", p=P), ids[:, :]).then_inc(s["id_init"], 16)
            for k in (5, 6, 7):
                expert(k)
            sp.wait_ge(s["id_out"], 16 * 2 * NT)
            sp.dma_start(ids[:, :], id_dram.rearrange("(p t) w -> p (t w)", p=P)).then_inc(s["id_in"], 16)
            def refill(n, k, more=True):
                if more:
                    sp.wait_ge(s["gu_done"], n + 2)
                    gate_up(n + (1 + NSLOT), (k + 1) % NSLOT)
                sp.wait_ge(s["dn_done"], n + 1)
                down(n + NSLOT, k)

            sp.wait_ge(s["gu_done"], 1)
            gate_up(NSLOT, 0)
            with sp.Fori(0, NE // NSLOT - 2) as j:
                for k in range(NSLOT):
                    refill(j * NSLOT + k, k)
            for n in range(NE - 2 * NSLOT, NE - NSLOT):
                refill(n, n % NSLOT, n + 1 < NE - NSLOT)
            sp.wait_ge(s["dn_done"], NE)
            sp.wait_ge(s["id_in"], 16)
            n_over = sp.value_load(over[0:1, 0:1], min_val=0, max_val=NOVER)
            with sp.If(n_over > 0):
                with sp.Fori(0, NOVER) as k:
                    with sp.If(k < n_over):
                        e = sp.value_load(over[0:1, ds(k + 1, 1)], min_val=0, max_val=NE - 1)
                        sp.wait_ge(s["v_dn"], k + 1)
                        for n, w in ((0, wg), (1, wu)):
                            sp.dma_start(wslot[0][:, n * D:(n + 1) * D].rearrange("p (c f) -> p c f", c=C),
                                         w[ds(e, 1)].rearrange("e p c f -> p (e c) f")).then_inc(s["v_w"], 16)
                        sp.dma_start(wslot[0][:, 2 * D:3 * D], wd[ds(e, 1)].rearrange("e f d -> (e f) d")).then_inc(s["v_w"], 16)
            sp.wait_ge(s["experts_done"], 1)

            def load_y(i, u, rows):
                sp.dma_start(ya[u][0:rows, :], y_dram[ds(i * P, rows), :]).then_inc(y_in[u], 16)
                sp.dma_start(yb[u][0:rows, :], y_dram[ds(i * P + TOK, rows), :]).then_inc(y_in[u], 16)

            def store(i, u):
                sp.wait_ge(s["f_fin"], i + 1)
                sp.dma_start(t["y_prompt"].rearrange("a s d -> (a s) d")[ds(i * P, P), :], fin[u]).then_inc(s["f_out_b" if u else "f_out_a"], 16)

            load_y(0, 0, P)
            load_y(1, 1, P)
            sp.dma_start(g1[:, :], row(t["g_final"], D)).then_inc(s["g_late_in"], 16)
            load_y(2, 2, P)
            load_y(3, 3, P)
            for i in range(NT):
                if i + 4 < NT:
                    sp.wait_ge(s["f_acc"], i * 2 + 2)
                    load_y(i + 4, i % 4, P if i + 4 < SAMPLE else DEC)
                if i < SAMPLE:
                    store(i, i % 2)
            sp.wait_ge(s["f_fin"], NT)
            sp.dma_start(t["y_sample"].rearrange("a s d -> (a s) d"), fin[0][0:DEC, :]).then_inc(s["f_out_a"], 16)
            sp.wait_ge(s["f_out_a"], 16 * 5)
            sp.wait_ge(s["f_out_b"], 16 * 4)

        @block.gpsimd
        def _(pool):
            pool.wait_ge(s["proj_done"], NT * (NG - 1))
            pool.wait_ge(s["cache_in"], 64)
            pool.memset(qst[:, :, DH:DH + 1], 1.0 / SCALE).then_inc(s["pad_set"], 1)
            pool.memset(ck[:, :, NH * DH:], 0.0).then_inc(s["pad_set"], 1)
            pool.wait_ge(s["pad_set"], 2)

            def stage(h, done, first=False):
                if not first:
                    pool.wait_ge(s["st_T"], done)
                pool.tensor_copy(qst[:, :, 0:DH], fox_t[:, :, ds(h * DH, DH)])
                pool.tensor_copy(kst[:, 0:NT, 0:DH], fox_t[:, :, ds(h * DH + NH * DH, DH)])
                pool.tensor_copy(kst[:, NT:NK, 0:DH], ck[:, :, ds(h * DH, DH)])
                if first:
                    pool.wait_ge(s["c_ready"], 1)
                pool.tensor_copy(kst[:, :, DH:DH + 1], negc_t[:, :, ds(h, 1)]).then_inc(s["kv_staged"], 1)

            stage(0, 0, True)
            with pool.Fori(0, NH) as h:
                stage(h + 1, h * 6 + 6)

            def s_stage(g, done, first=False):
                if not first:
                    pool.wait_ge(s["s_qT_T"], done)
                pool.tensor_copy(sqst[:, :, 0:DH], swa_t[:, :, ds(g * DH, DH)])
                pool.tensor_copy(sqst[:, :, DH:P], swa_t[:, :, ds(g * DH + 4 * DH, DH)]).then_inc(s["s_staged"], 1)

            pool.wait_ge(s["evac_v"], EVAC_V)
            pool.wait_ge(s["evac_s"], EVAC_S)
            s_stage(0, 0, True)
            with pool.Fori(0, 4) as g:
                s_stage(g + 1, g * 3 + 3)
            pool.wait_ge(s["om_done"], NT)
            pool.wait_ge(s["h_done"], NT)
            for k in range(4):
                pool.memset(hg[k], 0.0).then_inc(s["hg_set"], 1)
            pool.wait_ge(s["r_done"], NT)
            pool.memset(ids[:, :], SKIP).then_inc(s["r_id"], 1)
            pool.wait_ge(s["id_init"], 16)
            for c in range(2):
                pool.wait_ge(s["r_mask"], c + 2)
                for i in range(NT):
                    n = 2 * i + c
                    pool.indirect_dma_start(
                        out=id_dram, out_offset=bass.IndirectOffsetOnAxis(ap=dest[:, n:n + 1], axis=0),
                        in_=ci[:, 2 * n:2 * n + 2], in_offset=None,
                        bounds_check=P * NTILES - 1, oob_is_err=False).then_inc(s["id_out"], 16)
            pool.wait_ge(s["hg_set"], 4)
            pool.wait_ge(s["id_in"], 16)
            for i in range(2):
                pool.wait_ge(s["h_out_a"], 16 * 5)
                pool.wait_ge(s["h_out_b"], 16 * 4)

            def gather(tt, k):
                pool.tensor_copy(idx[:, k:k + 1], ids[:, ds(tt * 2, 1)]).then_inc(s["idx_set"], 1)
                pool.wait_ge(s["idx_set"], tt + 1)
                pool.sem_inc(s["pool_went"], 1)
                pool.indirect_dma_start(
                    out=hg[k], out_offset=None, in_=h_dram,
                    in_offset=bass.IndirectOffsetOnAxis(ap=idx[:, k:k + 1], axis=0),
                    bounds_check=TOK - 1, oob_is_err=False).then_inc(g_in[k], 16)

            def scatter(tt, k):
                u = k
                if not (isinstance(tt, int) and tt < 4):
                    pool.wait_ge(y_out[u], (tt - u) * 4)
                pool.tensor_copy(idx[:, 4 + u:5 + u], ids[:, ds(tt * 2 + 1, 1)]).then_inc(s["dst_set"], 1)
                pool.wait_ge(s["dst_set"], tt + 1)
                pool.wait_ge(s["y_cs"], tt + 1)
                pool.wait_ge(s["y_cv"], tt + 1)
                pool.sem_inc(s["pool_went"], 1)
                pool.indirect_dma_start(
                    out=y_dram, out_offset=bass.IndirectOffsetOnAxis(ap=idx[:, 4 + u:5 + u], axis=0),
                    in_=yo[u], in_offset=None,
                    bounds_check=2 * TOK - 1, oob_is_err=False).then_inc(y_out[u], 16)

            def rows_step(tt, k, more=True):
                if more:
                    pool.wait_ge(s["gT_done"], tt * 2 + 4)
                    gather(tt + 5, (k + 1) % 4)
                scatter(tt, k)

            for tt in range(4):
                gather(tt, tt)
            pool.wait_ge(s["gT_done"], 2)
            gather(4, 0)
            for tt in range(4):
                rows_step(tt, tt)
            with pool.Fori(1, NE // 4 - 2) as j:
                for k in range(4):
                    rows_step(j * 4 + k, k)
            for tt in range(NE - 8, NE):
                rows_step(tt, tt % 4, tt + 5 < NE)
            for u in range(4):
                pool.wait_ge(y_out[u], 16 * NE // 4)
            n_over = pool.value_load(over[0:1, 0:1], min_val=0, max_val=NOVER)
            with pool.If(n_over > 0):
                with pool.Fori(0, NOVER) as k:
                    with pool.If(k < n_over):
                        pool.tensor_copy(idx[:, 0:2], ids[:, ds(k * 2 + 2 * NE, 2)]).then_inc(s["v_idx"], 1)
                        pool.wait_ge(s["v_idx"], k + 1)
                        pool.sem_inc(s["pool_went"], 1)
                        pool.indirect_dma_start(
                            out=hg[0], out_offset=None, in_=h_dram,
                            in_offset=bass.IndirectOffsetOnAxis(ap=idx[:, 0:1], axis=0),
                            bounds_check=TOK - 1, oob_is_err=False).then_inc(s["v_g"], 16)
                        pool.wait_ge(s["v_y"], k * 2 + 2)
                        pool.sem_inc(s["pool_went"], 1)
                        pool.indirect_dma_start(
                            out=y_dram, out_offset=bass.IndirectOffsetOnAxis(ap=idx[:, 1:2], axis=0),
                            in_=yo[0], in_offset=None,
                            bounds_check=2 * TOK - 1, oob_is_err=False).then_inc(s["v_out"], 16)
                        pool.wait_ge(s["v_out"], k * 16 + 16)
            pool.sem_inc(s["experts_done"], 1)

        @block.scalar
        def _(act):
            act.sem_inc(s["evac_s"], 3)
            act.sem_inc(s["cp_b"], 1)
            act.sem_inc(s["exp_done"], 2)
            act.wait_ge(s["eps_set"], 1)

            def norm(i):
                u = i % 2
                act.wait_ge(x_in[i % 4], i // 4 * 16 + 16)
                if i >= 2:
                    act.wait_ge(s["xT_done"], i * 2 - 2)
                act.activation(xn[u], x[i % 4], ACT.Square, accum_out=st[:, u:u + 1]).then_inc(s["square_done"], 1)
                act.wait_ge(s["square_done"], i + 1)
                act.activation(st[:, 2 + u:3 + u], st[:, u:u + 1], ACT.Sqrt, bias=eps[:, 0:1], scale=1.0 / D).then_inc(s["rms_done"], 1)

            def high_x(i):
                for b in range(2):
                    act.wait_ge(s["xT_done"], i * 2 + (b + 1))
                    act.activation(xh[:, ds(i * C + 4 * b, 4), :], bank[b].rearrange("p (c k) -> p c k", c=4), ACT.Copy).then_inc(s["xh_done"], 1)

            def high_w(u, loads):
                act.wait_ge(wg_in[u], loads * 16)
                act.activation(wg_hi[u], wg_raw[u], ACT.Copy).then_inc(s["wg_hi_set"], 1)

            def evac(n, k, dest):
                act.wait_ge(s["proj_done"], n + 1)
                act.activation(dest, bank[2 + k % 6][:, 0:WG], ACT.Copy).then_inc(s["evac_s"], 1)

            def evac_first(i, k):
                act.wait_ge(s["proj_done"], i + 1)
                act.activation(lf_t[:, ds(i, 1), :].rearrange("p a n -> p (a n)"), bank[2 + k % 6][:, WG:WG + NH], ACT.Copy)
                evac(i, k, fox_t[:, ds(i, 1), 0:WG].rearrange("p a n -> p (a n)"))

            norm(0)
            act.wait_ge(s["w0_in"], 32)
            act.activation(w0_hi, w0_raw, ACT.Copy).then_inc(s["wg_hi_set"], 1)
            high_x(0)
            norm(1)
            for i in range(6):
                norm(i + 2)
                high_x(i + 1)
                if i > 0 and i % 2 == 0:
                    evac_first(i - 1, i - 1)
            norm(8)
            high_x(7)
            evac_first(5, 5)
            high_x(8)
            act.wait_ge(s["xT_done"], 2 * NT)
            high_w(1, 1)
            evac_first(7, 7)

            n = NT * NH
            act.wait_ge(s["lf_v"], 2)
            act.activation(lz[:, n:2 * n], lz[:, 2 * n:3 * n], ACT.Exp, scale=-1.0).then_inc(s["lf_s"], 1)
            act.wait_ge(s["lf_s"], 1)
            act.activation(lz[:, 2 * n:3 * n], lz[:, n:2 * n], ACT.Ln, bias=eps[:, 1:2]).then_inc(s["lf_s"], 1)

            def group(n0, k0, loads, proj, dest, more=True):
                for i in range(NT):
                    if i == 3 and more:
                        act.wait_ge(s["proj_done"], proj)
                        high_w((k0 + 1) % 2, loads)
                    if (k0 + i) % 2:
                        evac(n0 + i, k0 + i, dest(i))

            with act.Fori(0, 2) as j:
                for g in (1, 2):
                    group(j * 2 * NT + g * NT, g * NT, j + (g + 2) // 2, j * 2 * NT + g * NT,
                          lambda i: fox_t[:, i, ds(j * 2 * WG + g * WG, WG)])
            for g in range(5, NG - 1):
                group(g * NT, g * NT, (g + 2) // 2, g * NT, lambda i: wg_dest(g, i))

            def stage_q(h6, u, gi, b=7):
                _, first, end = SG[gi]
                act.wait_ge(s["st_T"], h6 + (gi + 1))
                act.activation(qT[u][0:DH + 1, first * P:end * P], bank[b][0:DH + 1, 0:(end - first) * P], ACT.Copy,
                               scale=SCALE).then_inc(s["st_copied_s"], 1)

            for i in range(NT):
                n = (NG - 1) * NT + i
                if n % 2:
                    evac(n, n, wg_dest(NG - 1, i))
                if i == 6:
                    act.wait_ge(s["aug_set"], 2)
                    stage_q(0, 0, 0, 0)
                    stage_q(0, 0, 1, 1)
            stage_q(0, 0, 2, 0)
            act.wait_ge(s["aug_set"], 4)


            def fexp(it, k):
                u, i = STEPS[k]
                n = nblk[i] * P
                act.wait_ge(s["nmax_done"], it * NS + (k + 1))
                if k >= 1:
                    act.wait_ge(s["pT_a"], it * NS + max(k - 1, 1))
                act.activation(prob[k % 2][:, 0:n], ps[k % 2][:, 0:n], ACT.Exp, bias=nm[:, k % 2:k % 2 + 1],
                               accum_out=rs[:, k % 4:k % 4 + 1]).then_inc(s["exp_done"], 1)

            def copy_b(it, k):
                u, i = STEPS[k]
                n = nblk[i] * P
                if n > 512:
                    seen = sum(nblk[STEPS[m][1]] > 4 for m in range(k + 1))
                    act.wait_ge(s["pT_b"], it * 2 * len(TWO) + seen)
                    act.wait_ge(s["pv_done"], it * NS + (k - 1))
                    act.activation(probT[k % 2][:, 512:n], bank[5][:, 0:n - 512], ACT.Copy).then_inc(s["cp_b"], 1)

            with act.Fori(0, NH // 2) as it:
                fexp(it, 0)
                for k in range(NS):
                    u, i = STEPS[k]
                    if k + 1 < NS:
                        fexp(it, k + 1)
                    if i in SG_AT and SG_AT[i] < 3:
                        stage_q(it * 12 + 6 * (u + 1), 1 - u, SG_AT[i])
                    copy_b(it, k)

            def stage_sq(g3, u, gi, bk=7):
                a, b = SSG[gi]
                act.wait_ge(s["s_qT_T"], g3 + (gi + 1))
                act.activation(sqT[u][:, a * P:b * P], bank[bk][:, 0:(b - a) * P], ACT.Copy, scale=SCALE).then_inc(s["s_qT_cp"], 1)

            for gi in range(3):
                stage_sq(0, 0, gi, gi)

            def sexp(it, k):
                u, i = STEPS[k]
                lo = P if i == 0 else 0
                act.wait_ge(s["s_nm"], it * NS + (k + 1))
                if k >= 1:
                    act.wait_ge(s["s_pT"], it * NS + max(k - 1, 1))
                if k >= 3:
                    act.wait_ge(s["s_od"], it * NS + (k - 1))
                for v in range(2):
                    act.activation(sprob[k % 2][:, v, lo:2 * P], bank[k % 3][:, v * 256 + lo:v * 256 + 256], ACT.Exp,
                                   bias=nm[:, 2 * (k % 3) + v:1 + 2 * (k % 3) + v],
                                   accum_out=rs[:, 4 + 2 * (k % 3) + v:5 + 2 * (k % 3) + v]).then_inc(s["s_exp"], 1)
                act.activation(rs[:, 10 + 2 * (k % 3):12 + 2 * (k % 3)], nm[:, 6 + 2 * (k % 3):8 + 2 * (k % 3)], ACT.Exp).then_inc(s["s_sexp"], 1)

            def scopy(it, k):
                if k % 2:
                    n = 2 * P if STEPS[k][1] == 0 else 4 * P
                    act.wait_ge(s["s_pT"], it * NS + (k + 1))
                    if k > 1:
                        act.wait_ge(s["s_pv"], it * NS + (k - 1))
                    act.activation(sprobT[1][:, 0:n], bank[5][:, 0:n], ACT.Copy).then_inc(s["s_cps"], 1)

            with act.Fori(0, 2) as it:
                sexp(it, 0)
                for k in range(NS):
                    u, i = STEPS[k]
                    if k + 1 < NS:
                        sexp(it, k + 1)
                    if i in SSG_AT:
                        stage_sq(it * 6 + 3 * (u + 1), 1 - u, SSG_AT[i])
                    scopy(it, k)
                    if k in WO_AT:
                        act.wait_ge(s["w_out_in"], 16)
                        c = it * (C // 2) + WO_AT.index(k)
                        act.activation(w_out_h[:, ds(c, 1), :].rearrange("p a n -> p (a n)"), fox[:, ds(c * D + w_out_at, D)],
                                       ACT.Copy).then_inc(s["wo_hi_set"], 1)

            def norm_o(i, u):
                if not (isinstance(i, int) and i < 2):
                    act.wait_ge(s["oT_done"], i * 2 - 2)
                for v in range(2):
                    act.activation(on[u][:, 512 * v:512 * v + 512], o_all[:, ds(i, 1), 512 * v:512 * v + 512].rearrange("p a n -> p (a n)"),
                                   ACT.Square, accum_out=st[:, 2 * u + v:2 * u + v + 1]).then_inc(s["o_stat"], 1)
                act.wait_ge(s["o_stat"], i * 2 + 2)
                act.activation(st[:, 4 + 2 * u:6 + 2 * u], st[:, 2 * u:2 * u + 2], ACT.Sqrt, bias=eps[:, 0:1], scale=2.0 / D).then_inc(s["o_rms"], 1)

            def high_o(i, u):
                if not (isinstance(i, int) and i < 2):
                    act.wait_ge(s["om_done"], i - 1)
                for b in range(2):
                    act.wait_ge(s["oT_done"], i * 2 + (b + 1))
                    act.activation(oTh[u][:, 4 * b:4 * b + 4, :], bank[b].rearrange("p (c k) -> p c k", c=4), ACT.Copy).then_inc(s["oTh_done"], 1)

            def norm_h(i, u):
                act.wait_ge(s["x2_done"], i * 2 + 2)
                if not (isinstance(i, int) and i < 2):
                    act.wait_ge(s["hT_done"], i * 2 - 2)
                    act.wait_ge(s["h_out_b" if u else "h_out_a"], (i - u) * 8)
                act.activation(hh[u], o_all[:, ds(i, 1), :].rearrange("p a n -> p (a n)"), ACT.Square,
                               accum_out=st[:, 12:13]).then_inc(s["h_stat"], 1)
                act.wait_ge(s["h_stat"], i + 1)
                act.activation(st[:, 13:14], st[:, 12:13], ACT.Sqrt, bias=eps[:, 0:1], scale=1.0 / D).then_inc(s["h_rms"], 1)

            def copy_hT(i, u):
                if not (isinstance(i, int) and i < 2):
                    act.wait_ge(s["r_done"], i - 1)
                for b in range(2):
                    act.wait_ge(s["hT_done"], i * 2 + (b + 1))
                    act.activation(hhT[u][:, 4 * b:4 * b + 4, :], bank[b].rearrange("p (c k) -> p c k", c=4), ACT.Copy).then_inc(s["hT_copied"], 1)

            for i in range(3):
                act.wait_ge(s["s_od"], NS + NT + 2 + i if i < 2 else 2 * NS + 1)
                norm_o(i, i % 2)
                high_o(i, i % 2)

            def ostep(i, u, more=True):
                if more:
                    norm_o(i + 3, 1 - u)
                norm_h(i, u)
                copy_hT(i, u)
                if more:
                    high_o(i + 3, 1 - u)

            for i in (0, 1):
                ostep(i, i)
            with act.Fori(1, 3) as j:
                for u in range(2):
                    ostep(j * 2 + u, u)
            for i in (6, 7, 8):
                ostep(i, i % 2, False)

            act.wait_ge(s["r_exp"], 1)
            act.activation(rt["eqg"], rt["lg"], ACT.Exp).then_inc(s["r_exp"], 1)
            act.wait_ge(s["r_exp"], 3)
            act.activation(small["e21"], small["m2"], ACT.Exp).then_inc(s["r_exp"], 1)

            def copy_gT(tt, u):
                act.wait_ge(s["gT_done"], tt * 2 + 1)
                if not (isinstance(tt, int) and tt < 2):
                    act.wait_ge(s["gu_done"], tt - 1)
                act.activation(hgT[u][:, 0:4, :], bank[0].rearrange("p (c k) -> p c k", c=4), ACT.Copy).then_inc(s["gT_cs"], 1)

            def gate_exp(tt, u):
                act.wait_ge(s["gu_done"], tt + 1)
                if not (isinstance(tt, int) and tt < 2):
                    act.wait_ge(s["ev_step"], tt * 3 - 5)
                act.activation(ex["e"][u], bank[2 + u][:, 0:FE], ACT.Exp, scale=-1.0).then_inc(s["e_done"], 1)

            def copy_hid(tt, u):
                act.wait_ge(s["hidT_done"], tt + 1)
                if not (isinstance(tt, int) and tt < 2):
                    act.wait_ge(s["dn_done"], tt - 1)
                act.activation(ex["hidT"][u], bank[6][:, 0:P], ACT.Copy).then_inc(s["hidT_cp"], 1)

            def copy_y(tt, u):
                act.wait_ge(s["dn_done"], tt + 1)
                if not (isinstance(tt, int) and tt < 4):
                    act.wait_ge(y_out[u], (tt - u) * 4)
                act.activation(yo[u][:, 0:512], bank[4], ACT.Copy).then_inc(s["y_cs"], 1)

            def estep(tt, k, last=2):
                if last >= 1:
                    gate_exp(tt + 1, (k + 1) % 2)
                copy_hid(tt, k % 2)
                if last >= 2:
                    copy_gT(tt + 2, k % 2)
                copy_y(tt, k)

            copy_gT(0, 0)
            copy_gT(1, 1)
            gate_exp(0, 0)
            for tt in range(4):
                estep(tt, tt)
            with act.Fori(1, NE // 4 - 1) as j:
                for k in range(4):
                    estep(j * 4 + k, k)
            for tt in range(NE - 4, NE):
                estep(tt, tt % 4, min(2, NE - 1 - tt))

            n_over = act.value_load(over[0:1, 0:1], min_val=0, max_val=NOVER)
            with act.If(n_over > 0):
                with act.Fori(0, NOVER) as k:
                    with act.If(k < n_over):
                        act.wait_ge(s["v_gT"], k * 2 + 1)
                        act.activation(hgT[0][:, 0:4, :], bank[0].rearrange("p (c k) -> p c k", c=4), ACT.Copy).then_inc(s["v_gTc"], 1)
                        act.wait_ge(s["v_gu"], k + 1)
                        act.activation(ex["e"][0], bank[2][:, 0:FE], ACT.Exp, scale=-1.0).then_inc(s["v_e"], 1)
                        act.wait_ge(s["v_hT"], k + 1)
                        act.activation(ex["hidT"][0], bank[6][:, 0:P], ACT.Copy).then_inc(s["v_hTc"], 1)
                        act.wait_ge(s["v_dn"], k + 2)
                        act.activation(yo[0][:, 0:512], bank[4], ACT.Copy).then_inc(s["v_y"], 1)
            act.wait_ge(s["experts_done"], 1)

            def norm_f(i, u, rows):
                act.wait_ge(s["f_acc"], i * 2 + 2)
                if not (isinstance(i, int) and i < 2):
                    act.wait_ge(s["f_out_b" if u else "f_out_a"], (i - u) * 8)
                act.activation(fin[u][0:rows, :], o_all[0:rows, ds(i, 1), :].rearrange("p a n -> p (a n)"), ACT.Square,
                               accum_out=st[0:rows, u:u + 1]).then_inc(s["f_stat"], 1)
                act.wait_ge(s["f_stat"], i + 1)
                act.activation(st[0:rows, 2 + u:3 + u], st[0:rows, u:u + 1], ACT.Sqrt, bias=eps[0:rows, 0:1], scale=1.0 / D).then_inc(s["f_rms"], 1)

            norm_f(0, 0, P)
            norm_f(1, 1, P)
            with act.Fori(1, NP_T // 2) as j:
                for u in range(2):
                    norm_f(j * 2 + u, u, P)
            norm_f(8, 0, DEC)

        @block.vector
        def _(dve):
            dve.memset(eps[:, 0:1], EPS)
            dve.memset(negc[:, :], 0.0)
            dve.memset(eps[:, 1:2], 1.0).then_inc(s["eps_set"], 1)
            dve.sem_inc(s["evac_v"], 3)
            dve.sem_inc(s["o_done"], 1)
            dve.sem_inc(s["s_od"], 1)

            def scale_x(i, u):
                dve.wait_ge(s["rms_done"], i + 1)
                dve.reciprocal(st[:, 4 + u:5 + u], st[:, 2 + u:3 + u]).then_inc(s["rstd_done"], 1)
                dve.wait_ge(s["rstd_done"], i + 1)
                dve.scalar_tensor_tensor(out=xn[u], in0=x[i % 4], scalar=st[:, 4 + u:5 + u], in1=g0[:, :],
                                         op0=ALU.mult, op1=ALU.mult).then_inc(s["xn_done"], 1)

            def low_x(i):
                for b in range(2):
                    dve.wait_ge(s["xh_done"], i * 2 + (b + 1))
                    dve.tensor_tensor(xl[:, ds(i * C + 4 * b, 4), :], bank[b].rearrange("p (c k) -> p c k", c=4),
                                      xh[:, ds(i * C + 4 * b, 4), :].bitcast(F32), ALU.subtract).then_inc(s["xl_done"], 1)

            def low_w(u, highs):
                dve.wait_ge(s["wg_hi_set"], highs)
                dve.tensor_tensor(wg_lo[u], wg_raw[u], wg_hi[u].bitcast(F32), ALU.subtract).then_inc(s["wg_lo_set"], 1)

            def evac(n, k, dest):
                dve.wait_ge(s["proj_done"], n + 1)
                dve.tensor_copy(dest, bank[2 + k % 6][:, 0:WG]).then_inc(s["evac_v"], 1)

            def evac_first(i, k):
                dve.wait_ge(s["proj_done"], i + 1)
                dve.tensor_copy(lf_t[:, ds(i, 1), :].rearrange("p a n -> p (a n)"), bank[2 + k % 6][:, WG:WG + NH])
                evac(i, k, fox_t[:, ds(i, 1), 0:WG].rearrange("p a n -> p (a n)"))

            dve.wait_ge(s["gain_in"], 16)
            scale_x(0, 0)
            dve.wait_ge(s["wg_hi_set"], 1)
            dve.tensor_tensor(w0_lo, w0_raw, w0_hi.bitcast(F32), ALU.subtract).then_inc(s["wg_lo_set"], 1)
            low_x(0)
            scale_x(1, 1)
            for i in range(6):
                scale_x(i + 2, i % 2)
                low_x(i + 1)
                if i % 2:
                    evac_first(i - 1, i - 1)
            scale_x(8, 0)
            low_x(7)
            low_x(8)
            low_w(1, 2)
            evac_first(6, 6)
            evac_first(8, 8)

            n = NT * NH
            dve.wait_ge(s["small_in"], 16 * 12)
            dve.wait_ge(s["evac_v"], 3 + (NT + 1) // 2)
            dve.wait_ge(s["evac_s"], 3 + NT // 2)
            z, mn = lz[:, 0:n], lz[:, n:2 * n]
            dve.tensor_tensor(z.rearrange("p (t h) -> p t h", h=NH), lf_t[:, 0:NT, :],
                              bf[:, None, :].to_broadcast([P, NT, NH]), ALU.add).then_inc(s["lf_v"], 1)
            dve.wait_ge(s["lf_v"], 1)
            dve.scalar_tensor_tensor(out=lz[:, 2 * n:3 * n], in0=z, scalar=-1.0, in1=z, op0=ALU.mult, op1=ALU.max).then_inc(s["lf_v"], 1)
            dve.wait_ge(s["lf_s"], 2)
            dve.scalar_tensor_tensor(out=lf[:, 0:n], in0=z, scalar=0.0, in1=lz[:, 2 * n:3 * n],
                                     op0=ALU.min, op1=ALU.subtract).then_inc(s["lf_v"], 1)
            dve.wait_ge(s["lf_v"], 3)
            dve.memset(lsum[:, :], 0.0).then_inc(s["lf_v"], 1)
            dve.wait_ge(s["lf_v"], 4)
            dve.tensor_copy(lsum_t[:, NT + 1, :], lf_t[:, NT, :])
            dve.tensor_tensor(lsum_t[:, SAMPLE, :], lf_t[:, NT, :], lf_t[:, NT + 1, :], ALU.add)
            for i in range(1, NP_T):
                dve.tensor_tensor(lsum_t[:, i, :], lsum_t[:, i - 1, :], lf_t[:, i - 1, :], ALU.add).then_inc(s["lf_v"], 1)
                dve.wait_ge(s["lf_v"], 4 + i)

            def group(n0, k0, highs, dest, more=True):
                for i in range(NT):
                    if i == 4 and more:
                        low_w((k0 + 1) % 2, highs)
                    if (k0 + i) % 2 == 0:
                        evac(n0 + i, k0 + i, dest(i))

            with dve.Fori(0, 2) as j:
                for g in (1, 2):
                    group(j * 2 * NT + g * NT, g * NT, j * 2 + (g + 2),
                          lambda i: fox_t[:, i, ds(j * 2 * WG + g * WG, WG)])
            for g in range(5, NG - 1):
                group(g * NT, g * NT, g + 2, lambda i: wg_dest(g, i))
            dve.wait_ge(s["c_mm"], 1)
            dve.tensor_scalar(negc_t[:, :, 0:NH], bank[0][:, 0:NK * NH].rearrange("p (t h) -> p t h", h=NH),
                              -1.0, None, ALU.mult).then_inc(s["c_ready"], 1)

            def clear_pad(u):
                dve.memset(qT[u][DH:P, :], 0.0).then_inc(s["aug_set"], 1)
                dve.memset(kT[u][DH:P, :], 0.0).then_inc(s["aug_set"], 1)

            for i in range(NT):
                n = (NG - 1) * NT + i
                if n % 2 == 0:
                    evac(n, n, wg_dest(NG - 1, i))
                if i in (4, 6):
                    dve.wait_ge(s["proj_done"], (NG - 1) * NT + 5)
                    clear_pad((i - 4) // 2)
            dve.wait_ge(s["aug_set"], 4)

            def stage_k(h6, u, gi, b=7):
                _, first, end = SG[gi]
                dve.wait_ge(s["st_T"], h6 + (gi + 1))
                dve.tensor_copy(kT[u][0:DH + 1, first * P:end * P], bank[b][0:DH + 1, 0:(end - first) * P]).then_inc(s["st_copied_v"], 1)

            for gi in range(3, 6):
                stage_k(0, 0, gi, gi % 2)

            def fmax(it, k):
                n = nblk[STEPS[k][1]] * P
                dve.wait_ge(s["qk_done"], it * NS + (k + 1))
                dve.tensor_reduce(nm[:, k % 2:k % 2 + 1], ps[k % 2][:, 0:n], AX.X, ALU.max, negate=True).then_inc(s["nmax_done"], 1)

            def copy_a(it, k):
                n = min(nblk[STEPS[k][1]] * P, 512)
                dve.wait_ge(s["pT_a"], it * NS + (k + 1))
                dve.tensor_copy(probT[k % 2][:, 0:n], bank[4][:, 0:n]).then_inc(s["cp_a"], 1)

            def fnorm(it, k):
                u, i = STEPS[k]
                dve.reciprocal(rc[:, k % 2:k % 2 + 1], rs[:, k % 4:k % 4 + 1]).then_inc(s["recip"], 1)
                dve.wait_ge(s["recip"], it * NS + (k + 1))
                dve.wait_ge(s["pv_done"], it * NS + (k + 1))
                dve.tensor_scalar(o_all[:, i, ds(it * 2 * DH + u * DH, DH)], bank[6][:, (k % 2) * DH:(k % 2) * DH + DH],
                                  rc[:, k % 2:k % 2 + 1], None, ALU.mult).then_inc(s["o_done"], 1)

            with dve.Fori(0, NH // 2) as it:
                fmax(it, 0)
                for k in range(NS):
                    u, i = STEPS[k]
                    if k + 1 < NS:
                        fmax(it, k + 1)
                    if i in SG_AT and SG_AT[i] >= 3:
                        stage_k(it * 12 + 6 * (u + 1), 1 - u, SG_AT[i])
                    copy_a(it, k)
                    if k >= 1:
                        fnorm(it, k - 1)
                fnorm(it, NS - 1)

            pairs = sraw[:, :].rearrange("p (v g) -> p g v", v=2)
            dve.tensor_copy(sink[:, :].rearrange("p (g v) -> p g v", v=2), pairs)
            dve.tensor_scalar(nsink[:, :].rearrange("p (g v) -> p g v", v=2), pairs, -1.0, None, ALU.mult).then_inc(s["s_aug"], 1)
            dve.wait_ge(s["s_aug"], 1)
            dve.memset(skT[0][DH:P, :], 0.0).then_inc(s["s_aug"], 1)
            dve.memset(skT[1][0:DH, :], 0.0).then_inc(s["s_aug"], 1)
            for gi, (a, b) in enumerate([(0, 4), (4, 8), (8, 10)]):
                dve.wait_ge(s["s_kT"], gi + 1)
                dve.tensor_copy(skT[0][0:DH, a * P:b * P], bank[3 + gi][0:DH, 0:(b - a) * P])
                dve.tensor_copy(skT[1][DH:P, a * P:b * P], bank[3 + gi][DH:P, 0:(b - a) * P]).then_inc(s["s_kcp"], 1)

            def smax(it, k):
                u, i = STEPS[k]
                lo = P if i == 0 else 0
                a, q = 2 * (k % 3), 6 + 2 * (k % 3)
                n = it * NS * 2 + 2 * k
                dve.wait_ge(s["s_qk"], it * NS + (k + 1))
                if k >= 3:
                    dve.wait_ge(s["s_sexp"], it * NS + (k - 2))
                dve.tensor_reduce(nm[:, 12:14], bank[k % 3].rearrange("p (v n) -> p v n", v=2)[:, :, lo:256],
                                  AX.X, ALU.max, negate=True).then_inc(s["s_nmc"], 1)
                dve.wait_ge(s["s_nmc"], n + 1)
                g2 = it * 4 + 2 * u
                dve.tensor_tensor(nm[:, a:a + 2], nm[:, 12:14], nsink[:, ds(g2, 2)], ALU.min).then_inc(s["s_nmc"], 1)
                dve.wait_ge(s["s_nmc"], n + 2)
                dve.tensor_tensor(nm[:, q:q + 2], nm[:, a:a + 2], sink[:, ds(g2, 2)], ALU.add).then_inc(s["s_nm"], 1)

            def scopy(it, k):
                if k % 2 == 0:
                    n = 2 * P if STEPS[k][1] == 0 else 4 * P
                    dve.wait_ge(s["s_pT"], it * NS + (k + 1))
                    dve.tensor_copy(sprobT[0][:, 0:n], bank[4][:, 0:n]).then_inc(s["s_cpv"], 1)

            def snorm(it, k):
                u, i = STEPS[k]
                a, q = 4 + 2 * (k % 3), 10 + 2 * (k % 3)
                n = it * NS * 2 + 2 * k
                dve.wait_ge(s["s_sexp"], it * NS + (k + 1))
                dve.tensor_tensor(rc[:, 2:4], rs[:, a:a + 2], rs[:, q:q + 2], ALU.add).then_inc(s["s_rc"], 1)
                dve.wait_ge(s["s_rc"], n + 1)
                dve.reciprocal(rc[:, 4:6], rc[:, 2:4]).then_inc(s["s_rc"], 1)
                dve.wait_ge(s["s_rc"], n + 2)
                dve.wait_ge(s["s_pv"], it * NS + (k + 1))
                o = o_all[:, i, :].rearrange("p (b g d) -> p b g d", g=4, d=DH)[:, 2:4, ds(it * 2 + u, 1), :]
                dve.tensor_tensor(o.rearrange("p b g d -> p b (g d)"),
                                  bank[6][:, (k % 2) * P:(k % 2) * P + P].rearrange("p (v d) -> p v d", v=2),
                                  rc[:, 4:6, None].to_broadcast([P, 2, DH]), ALU.mult).then_inc(s["s_od"], 1)

            with dve.Fori(0, 2) as it:
                smax(it, 0)
                smax(it, 1)
                for k in range(NS):
                    if k + 2 < NS:
                        smax(it, k + 2)
                    scopy(it, k)
                    if k >= 1:
                        snorm(it, k - 1)
                    if k in WO_AT:
                        c = it * (C // 2) + WO_AT.index(k)
                        dve.wait_ge(s["wo_hi_set"], c + 1)
                        dve.tensor_tensor(w_out_l[:, ds(c, 1), :].rearrange("p a n -> p (a n)"), fox[:, ds(c * D + w_out_at, D)],
                                          w_out_h[:, ds(c, 1), :].rearrange("p a n -> p (a n)").bitcast(F32),
                                          ALU.subtract).then_inc(s["wo_lo_set"], 1)
                snorm(it, NS - 1)

            dve.wait_ge(s["s_od"], 2 * NS + 1)

            def scale_o(i, u):
                dve.wait_ge(s["o_rms"], i + 1)
                dve.reciprocal(st[:, 8 + 2 * u:10 + 2 * u], st[:, 4 + 2 * u:6 + 2 * u]).then_inc(s["o_rstd"], 1)
                dve.wait_ge(s["o_rstd"], i + 1)
                for v in range(2):
                    cols = slice(512 * v, 512 * v + 512)
                    dve.scalar_tensor_tensor(out=on[u][:, cols], in0=o_all[:, ds(i, 1), cols].rearrange("p a n -> p (a n)"),
                                             scalar=st[:, 8 + 2 * u + v:9 + 2 * u + v], in1=g1[:, cols],
                                             op0=ALU.mult, op1=ALU.mult).then_inc(s["on_done"], 1)

            def add_x(i, j, u):
                dve.wait_ge(xr_in[u], j * 16 + 16)
                dve.wait_ge(s["om_done"], i + 1)
                dve.wait_ge(s["on_done"], i * 2 + 2)
                for v in range(2):
                    cols = slice(512 * v, 512 * v + 512)
                    dve.tensor_tensor(o_all[:, ds(i, 1), cols].rearrange("p a n -> p (a n)"), bank[2 + 2 * u + v], xr[u][:, cols],
                                      ALU.add).then_inc(s["x2_done"], 1)

            def scale_h(i, u):
                dve.wait_ge(s["h_rms"], i + 1)
                dve.reciprocal(st[:, 14:15], st[:, 13:14]).then_inc(s["h_rstd"], 1)
                dve.wait_ge(s["h_rstd"], i + 1)
                dve.scalar_tensor_tensor(out=hh[u], in0=o_all[:, ds(i, 1), :].rearrange("p a n -> p (a n)"),
                                         scalar=st[:, 14:15], in1=g0[:, :], op0=ALU.mult, op1=ALU.mult).then_inc(s["h_done"], 1)

            def low_o(i, u):
                if not (isinstance(i, int) and i < 2):
                    dve.wait_ge(s["om_done"], i - 1)
                for b in range(2):
                    dve.wait_ge(s["oTh_done"], i * 2 + (b + 1))
                    dve.tensor_tensor(oTl[u][:, 4 * b:4 * b + 4, :], bank[b].rearrange("p (c k) -> p c k", c=4),
                                      oTh[u][:, 4 * b:4 * b + 4, :].bitcast(F32), ALU.subtract).then_inc(s["oTl_done"], 1)

            for i in range(3):
                scale_o(i, i % 2)
                low_o(i, i % 2)
            dve.wait_ge(s["g_late_in"], 16)
            with dve.Fori(0, 3) as j:
                for u in range(2):
                    scale_o(j * 2 + (u + 3), 1 - u)
                    add_x(j * 2 + u, j, u)
                    scale_h(j * 2 + u, u)
                    low_o(j * 2 + (u + 3), 1 - u)
            for i in (6, 7, 8):
                add_x(i, i // 2, i % 2)
                scale_h(i, i % 2)

            cnt = [0]

            def link(ins):
                cnt[0] += 1
                ins.then_inc(s["r_step"], 1)
                dve.wait_ge(s["r_step"], cnt[0])

            dve.wait_ge(s["r_done"], NT)
            dve.wait_ge(s["h_out_a"], 16 * 5)
            dve.wait_ge(s["h_out_b"], 16 * 4)
            link(dve.tensor_tensor(logit_t, bank[6][:, 0:NT * (GRP + NE)].rearrange("p (t e) -> p t e", t=NT),
                                   br[:, None, :].to_broadcast([P, NT, GRP + NE]), ALU.add))
            iota = cr[:, 0:NE]
            lg, le = logit_t[:, :, 0:GRP], logit_t[:, :, GRP:GRP + NE]

            def first_max(val, n, m, idx_, eq, oh):
                link(dve.tensor_reduce(m, val, AX.X, ALU.max))
                link(dve.tensor_tensor(eq, val, m[:, :, None].to_broadcast([P, NT, n]), ALU.is_equal))
                link(dve.scalar_tensor_tensor(out=eq, in0=eq, scalar=-64.0, in1=iota[:, None, 0:n].to_broadcast([P, NT, n]),
                                              op0=ALU.mult, op1=ALU.add))
                link(dve.tensor_reduce(idx_, eq, AX.X, ALU.min))
                link(dve.tensor_tensor(oh, eq, idx_[:, :, None].to_broadcast([P, NT, n]), ALU.is_equal))

            first_max(lg, GRP, small["m0"], small["i0"], rt["eqg"], rt["ohg"])
            dve.tensor_tensor(rt["lg"], lg, small["m0"][:, :, None].to_broadcast([P, NT, GRP]), ALU.subtract).then_inc(s["r_exp"], 1)
            link(dve.tensor_scalar(rt["ohg"], rt["ohg"], BIG, -BIG, ALU.mult, ALU.add))
            link(dve.tensor_tensor(rt["lem"].rearrange("p t (g e) -> p t g e", g=GRP), le.rearrange("p t (g e) -> p t g e", g=GRP),
                                   rt["ohg"][:, :, :, None].to_broadcast([P, NT, GRP, EPG]), ALU.add))
            first_max(rt["lem"], NE, small["m1"], small["i1"], rt["eq"], rt["oh1"])
            link(dve.scalar_tensor_tensor(out=rt["lem"], in0=rt["oh1"], scalar=-2 * BIG, in1=rt["lem"], op0=ALU.mult, op1=ALU.add))
            first_max(rt["lem"], NE, small["m2"], small["i2"], rt["eq"], rt["oh2"])
            valid = cr[:, NE:NE + NT]
            link(dve.tensor_tensor(rt["tmp"], rt["oh1"], rt["oh2"], ALU.add))
            link(dve.tensor_tensor(maskb[:, :].rearrange("p (t e) -> p t e", t=NT), rt["tmp"],
                                   valid[:, :, None].to_broadcast([P, NT, NE]), ALU.mult))
            runb_t = runb[:, :].rearrange("p (t e) -> p t e", t=NT)
            maskb_t = maskb[:, :].rearrange("p (t e) -> p t e", t=NT)
            link(dve.memset(runb[:, :], 0.0))
            for i in range(1, NT):
                link(dve.tensor_tensor(runb_t[:, i, :], runb_t[:, i - 1, :], maskb_t[:, i - 1, :], ALU.add))
            dve.sem_inc(s["r_mask"], 1)
            link(dve.tensor_tensor(small["m2"], small["m2"], small["m1"], ALU.subtract))
            dve.wait_ge(s["r_exp"], 2)
            link(dve.tensor_reduce(small["den"], rt["eqg"], AX.X, ALU.add))
            dve.sem_inc(s["r_exp"], 1)
            link(dve.tensor_scalar(small["m0"], valid, float(-SKIP), float(SKIP), ALU.mult, ALU.add))
            dve.wait_ge(s["r_mm"], 2)
            link(dve.tensor_copy(rt["rank"].rearrange("p t e -> p (t e)"), bank[0][:, 0:NT * NE]))
            cntp = bank[1][:, 0:NE]
            link(dve.tensor_scalar(nov[:, 0, :], cntp, -1.0, 0.0, ALU.add, ALU.max))
            link(dve.tensor_copy(ovi[:, 0:NE], nov[:, 0, :]))
            link(dve.tensor_scalar(ovi[:, NE:2 * NE], ovi[:, 0:NE], 7, None, ALU.logical_shift_right))
            link(dve.tensor_copy(nov[:, 1, :], ovi[:, NE:2 * NE]))
            cur = 1
            for b in range(5):
                sh = 1 << b
                nxt = 2 + b % 2
                link(dve.tensor_copy(nov[:, nxt, :], nov[:, cur, :]))
                link(dve.tensor_tensor(nov[:, nxt, sh:NE], nov[:, cur, sh:NE], nov[:, cur, 0:NE - sh], ALU.add))
                cur = nxt
            incl = nov[:, cur, :]
            link(dve.tensor_tensor(nov[:, 4, :], incl, nov[:, 1, :], ALU.subtract))
            link(dve.scalar_tensor_tensor(out=nov[:, 5, :], in0=nov[:, 4, :], scalar=float(NE - 1), in1=iota,
                                          op0=ALU.add, op1=ALU.subtract))
            link(dve.tensor_copy(qi, rt["rank"].rearrange("p t e -> p (t e)")))
            link(dve.tensor_scalar(qi, qi, 7, None, ALU.logical_shift_right))
            link(dve.tensor_copy(rt["q"].rearrange("p t e -> p (t e)"), qi))
            link(dve.tensor_scalar(rt["tmp"], rt["rank"], float(NTILES), None, ALU.mult))
            link(dve.scalar_tensor_tensor(out=rt["tmp"], in0=rt["q"], scalar=float(1 - P * NTILES), in1=rt["tmp"],
                                          op0=ALU.mult, op1=ALU.add))
            link(dve.tensor_tensor(rt["pos"], rt["tmp"], iota[:, None, :].to_broadcast([P, NT, NE]), ALU.add))
            link(dve.tensor_scalar(rt["q"], rt["q"], 1.0, None, ALU.min))
            link(dve.tensor_tensor(rt["tmp"], rt["q"], nov[:, 5, None, :].to_broadcast([P, NT, NE]), ALU.mult))
            link(dve.tensor_tensor(rt["pos"], rt["pos"], rt["tmp"], ALU.add))
            for c, oh in enumerate(("oh1", "oh2")):
                link(dve.tensor_tensor(rt[oh], rt[oh], rt["pos"], ALU.mult))
                link(dve.tensor_reduce(small["p1"], rt[oh], AX.X, ALU.add))
                link(dve.tensor_tensor(dest[:, :].rearrange("p (t c) -> p t c", c=2)[:, :, c], small["p1"], small["m0"], ALU.add))
                dve.sem_inc(s["r_mask"], 1)
            dve.wait_ge(s["r_exp"], 4)
            link(dve.tensor_scalar(small["pg"], small["e21"], 1.0, None, ALU.add))
            link(dve.tensor_tensor(small["den"], small["den"], small["pg"], ALU.mult))
            link(dve.reciprocal(wgt[:, 0:NT], small["den"]))
            link(dve.tensor_tensor(wgt[:, NT:2 * NT], wgt[:, 0:NT], small["e21"], ALU.mult))
            link(dve.tensor_tensor(ovc, incl[:, None, :].to_broadcast([P, NOVER, NE]),
                                   iota[:, 0:NOVER, None].to_broadcast([P, NOVER, NE]), ALU.is_le))
            link(dve.tensor_reduce(ovf, ovc, AX.X, ALU.add))
            link(dve.tensor_scalar(ovf, ovf, float(NE - 1), None, ALU.min))
            link(dve.tensor_copy(over[0:1, 1:NOVER + 1], ovf[0:1, :]))
            link(dve.tensor_copy(over[0:1, 0:1], incl[0:1, NE - 1:NE]))
            dve.sem_inc(s["r_mask"], 1)

            def copy_gT(tt, u):
                dve.wait_ge(s["gT_done"], tt * 2 + 2)
                if not (isinstance(tt, int) and tt < 2):
                    dve.wait_ge(s["gu_done"], tt - 1)
                dve.tensor_copy(hgT[u][:, 4:8, :], bank[1].rearrange("p (c k) -> p c k", c=4)).then_inc(s["gT_cv"], 1)

            def gate(tt, u):
                dve.wait_ge(s["e_done"], tt + 1)
                dve.tensor_scalar(ex["s"][u], ex["e"][u], 1.0, None, ALU.add).then_inc(s["ev_step"], 1)
                dve.wait_ge(s["ev_step"], tt * 3 + 1)
                dve.reciprocal(ex["r"][u], ex["s"][u]).then_inc(s["ev_step"], 1)
                dve.wait_ge(s["ev_step"], tt * 3 + 2)
                dve.tensor_tensor(ex["a"][u], ex["r"][u], bank[2 + u][:, 0:FE], ALU.mult).then_inc(s["ev_step"], 1)
                dve.wait_ge(s["ev_step"], tt * 3 + 3)
                dve.tensor_tensor(ex["hid"][u], ex["a"][u], bank[2 + u][:, FE:2 * FE], ALU.mult).then_inc(s["hid_done"], 1)

            def copy_y(tt, u):
                dve.wait_ge(s["dn_done"], tt + 1)
                if not (isinstance(tt, int) and tt < 4):
                    dve.wait_ge(y_out[u], (tt - u) * 4)
                dve.tensor_copy(yo[u][:, 512:D], bank[5]).then_inc(s["y_cv"], 1)

            copy_gT(0, 0)
            copy_gT(1, 1)
            gate(0, 0)

            def estep(tt, k, last=2):
                if last >= 2:
                    copy_gT(tt + 2, k % 2)
                if last >= 1:
                    gate(tt + 1, (k + 1) % 2)
                copy_y(tt, k)

            for tt in range(4):
                estep(tt, tt)
            with dve.Fori(1, NE // 4 - 1) as j:
                for k in range(4):
                    estep(j * 4 + k, k)
            for tt in range(NE - 4, NE):
                estep(tt, tt % 4, min(2, NE - 1 - tt))

            n_over = dve.value_load(over[0:1, 0:1], min_val=0, max_val=NOVER)
            with dve.If(n_over > 0):
                with dve.Fori(0, NOVER) as k:
                    with dve.If(k < n_over):
                        dve.wait_ge(s["v_gT"], k * 2 + 2)
                        dve.tensor_copy(hgT[0][:, 4:8, :], bank[1].rearrange("p (c k) -> p c k", c=4)).then_inc(s["v_gTc"], 1)
                        dve.wait_ge(s["v_e"], k + 1)
                        dve.tensor_scalar(ex["s"][0], ex["e"][0], 1.0, None, ALU.add).then_inc(s["v_s"], 1)
                        dve.wait_ge(s["v_s"], k * 3 + 1)
                        dve.reciprocal(ex["r"][0], ex["s"][0]).then_inc(s["v_s"], 1)
                        dve.wait_ge(s["v_s"], k * 3 + 2)
                        dve.tensor_tensor(ex["a"][0], ex["r"][0], bank[2][:, 0:FE], ALU.mult).then_inc(s["v_s"], 1)
                        dve.wait_ge(s["v_s"], k * 3 + 3)
                        dve.tensor_tensor(ex["hid"][0], ex["a"][0], bank[2][:, FE:2 * FE], ALU.mult).then_inc(s["v_hid"], 1)
                        dve.wait_ge(s["v_dn"], k + 2)
                        dve.tensor_copy(yo[0][:, 512:D], bank[5]).then_inc(s["v_y"], 1)

            def add_y(i, j, u, rows):
                dve.wait_ge(y_in[u], j * 32 + 32)
                o = o_all[0:rows, ds(i, 1), :].rearrange("p a n -> p (a n)")
                dve.scalar_tensor_tensor(out=o, in0=ya[u][0:rows, :], scalar=wgt[0:rows, ds(i, 1)], in1=o,
                                         op0=ALU.mult, op1=ALU.add).then_inc(s["f_acc"], 1)
                dve.wait_ge(s["f_acc"], i * 2 + 1)
                dve.scalar_tensor_tensor(out=o, in0=yb[u][0:rows, :], scalar=wgt[0:rows, ds(i + NT, 1)], in1=o,
                                         op0=ALU.mult, op1=ALU.add).then_inc(s["f_acc"], 1)

            def scale_f(i, u, rows):
                dve.wait_ge(s["f_rms"], i + 1)
                dve.reciprocal(st[0:rows, 4 + u:5 + u], st[0:rows, 2 + u:3 + u]).then_inc(s["f_rstd"], 1)
                dve.wait_ge(s["f_rstd"], i + 1)
                dve.scalar_tensor_tensor(out=fin[u][0:rows, :], in0=o_all[0:rows, ds(i, 1), :].rearrange("p a n -> p (a n)"),
                                         scalar=st[0:rows, 4 + u:5 + u], in1=g1[0:rows, :],
                                         op0=ALU.mult, op1=ALU.mult).then_inc(s["f_fin"], 1)

            add_y(0, 0, 0, P)
            for i in range(NT):
                if i + 1 < NT:
                    add_y(i + 1, (i + 1) // 4, (i + 1) % 4, P if i + 1 < SAMPLE else DEC)
                if i == 0:
                    dve.wait_ge(s["g_late_in"], 32)
                scale_f(i, i % 2, P if i < SAMPLE else DEC)

        @block.tensor
        def _(pe):
            pe.wait_ge(s["const_in"], 16)

            def transpose_x(i, u):
                pe.wait_ge(s["xn_done"], i + 1)
                if not (isinstance(i, int) and i < 1):
                    pe.wait_ge(s["xl_done"], i * 2)
                src = xn[u].rearrange("p (k c) -> p c k", c=C)
                for c in range(C):
                    mm = pe.transpose(bank[c // 4][:, (c % 4) * P:(c % 4) * P + P], src[:, c, :], ident)
                    if c % 4 == 3:
                        mm.then_inc(s["xT_done"], 1)

            def three_passes(out, xs, ws, halfway=None):
                for c in range(C):
                    if c == C // 2 and halfway:
                        halfway()
                    for k, (a, b) in enumerate([(1, 0), (0, 1), (0, 0)]):
                        mm = pe.matmul(out, xs[a](c), ws[b](c), start=(c + k == 0), stop=(c == C - 1 and k == 2))
                return mm

            def x_parts(i):
                return lambda c: xh[:, i * C + c, :], lambda c: xl[:, i * C + c, :]

            def product(copied, k, i):
                pe.wait_ge(s["evac_s" if k % 2 else "evac_v"], copied)
                u = k // NT % 2
                return three_passes(bank[2 + k % 6][:, 0:WG], x_parts(i),
                                    (lambda c: wg_hi[u][:, c, :], lambda c: wg_lo[u][:, c, :]))

            transpose_x(0, 0)
            for i in range(NT):
                if 1 <= i < NT - 1:
                    transpose_x(i + 1, (i + 1) % 2)
                pe.wait_ge(s["xl_done"], i * 2 + 2)
                if i == 0:
                    pe.wait_ge(s["wg_lo_set"], 1)
                pe.wait_ge(s["evac_s" if i % 2 else "evac_v"], i // 2 + 1)
                three_passes(bank[2 + i % 6][:, 0:WF], x_parts(i), (lambda c: w0_hi[:, c, :], lambda c: w0_lo[:, c, :]),
                             (lambda: transpose_x(1, 1)) if i == 0 else None).then_inc(s["proj_done"], 1)
            with pe.Fori(0, (NG - 1) // 2 - 1) as j:
                for g in (1, 2):
                    pe.wait_ge(s["wg_lo_set"], j * 2 + (g + 1))
                    for i in range(NT):
                        k = g * NT + i
                        product(j * NT + (k // 2 + 1), k, i).then_inc(s["proj_done"], 1)
            pe.wait_ge(s["wg_lo_set"], NG - 1)
            for i in range(NT):
                k = (NG - 2) * NT + i
                product(k // 2 + 1, k, i).then_inc(s["proj_done"], 1)

            pe.wait_ge(s["lf_v"], 4 + NP_T - 1)
            pe.matmul(bank[0][:, 0:NK * NH], upto, lf[:, :], start=True, stop=False)
            pe.matmul(bank[0][:, 0:NK * NH], ones, lsum[:, :], start=False, stop=True).then_inc(s["c_mm"], 1)

            def first_stage(gi):
                if gi == 0:
                    pe.wait_ge(s["kv_staged"], 1)
                    pe.wait_ge(s["c_ready"], 1)
                elif gi >= 2:
                    pe.wait_ge(s["st_copied_s"] if gi < 5 else s["st_copied_v"], gi - 1 if gi < 5 else 1)
                kind, a, b = SG[gi]
                src = qst if kind == "q" else kst
                for m in range(a, b):
                    mm = pe.transpose(bank[gi % 2][0:DH + 1, (m - a) * P:(m - a + 1) * P], src[:, m, :], ident)
                mm.then_inc(s["st_T"], 1)

            pe.wait_ge(s["wg_lo_set"], NG)
            for i in range(NT):
                k = (NG - 1) * NT + i
                product(k // 2 + 1, k, i).then_inc(s["proj_done"], 1)
                if i >= 6:
                    first_stage(2 * i - 12)
                    first_stage(2 * i - 11)

            def stage(h1, h6, c3, gi):
                kind, a, b = SG[gi]
                if gi == 0:
                    pe.wait_ge(s["kv_staged"], h1)
                if gi == 0:
                    if not (isinstance(c3, int) and c3 == 0):
                        pe.wait_ge(s["st_copied_v"], c3)
                elif gi <= 3:
                    pe.wait_ge(s["st_copied_s"], c3 + gi)
                else:
                    pe.wait_ge(s["st_copied_v"], c3 + (gi - 3))
                src = qst if kind == "q" else kst
                for m in range(a, b):
                    mm = pe.transpose(bank[7][0:DH + 1, (m - a) * P:(m - a + 1) * P], src[:, m, :], ident)
                mm.then_inc(s["st_T"], 1)

            def fqk(it, k):
                u, i = STEPS[k]
                if i == 0:
                    pe.wait_ge(s["st_copied_s"], it * 6 + 3 * (u + 1))
                    pe.wait_ge(s["st_copied_v"], it * 6 + 3 * (u + 1))
                pe.wait_ge(s["exp_done"], it * NS + (k + 1))
                n = nblk[i] * P
                q = qT[u][:, i * P:(i + 1) * P]
                if i < SAMPLE:
                    spans = [(0, 0, min(n, 512))] + ([(512, 512, n - 512)] if n > 512 else [])
                    dg = i * P
                else:
                    spans = [(0, NT * P, PAST), (PAST, SAMPLE * P, P)]
                    dg = PAST
                for at_, k0, w in spans:
                    pe.matmul(ps[k % 2][:, at_:at_ + w], q, kT[u][:, k0:k0 + w], start=(at_ % 512 == 0), stop=False,
                              skip_group_check=True)
                pe.matmul(ps[k % 2][:, dg:dg + P], identb, causal, start=False, stop=True,
                          skip_group_check=True).then_inc(s["qk_done"], 1)

            def ftrans(it, k):
                u, i = STEPS[k]
                nb = nblk[i]
                pe.wait_ge(s["exp_done"], it * NS + (k + 3))
                if k >= 1:
                    pe.wait_ge(s["cp_a"], it * NS + k)
                for b in range(nb):
                    if b == 4:
                        seen = sum(nblk[STEPS[m][1]] > 4 for m in range(k))
                        pe.wait_ge(s["cp_b"], it * 2 * len(TWO) + (seen + 1))
                    mm = pe.transpose(bank[4 + b // 4][:, (b % 4) * P:(b % 4) * P + P], prob[k % 2][:, b * P:(b + 1) * P], ident)
                    if b == min(nb, 4) - 1:
                        mm.then_inc(s["pT_a"], 1)
                if nb > 4:
                    mm.then_inc(s["pT_b"], 1)

            def fpv(it, k):
                u, i = STEPS[k]
                nb = nblk[i]
                pe.wait_ge(s["cp_a"], it * NS + (k + 1))
                if nb > 4:
                    seen = sum(nblk[STEPS[m][1]] > 4 for m in range(k + 1))
                    pe.wait_ge(s["cp_b"], it * 2 * len(TWO) + (seen + 1))
                pe.wait_ge(s["o_done"], it * NS + (k + 1))
                for b in range(nb):
                    m = keytile(i, b)
                    if m < NT:
                        v = fox_t[:, m, ds(it * 2 * DH + (2 * NH * DH + u * DH), DH)]
                    else:
                        v = cv[:, m - NT, ds(it * 2 * DH + u * DH, DH)]
                    mm = pe.matmul(bank[6][:, (k % 2) * DH:(k % 2) * DH + DH], probT[k % 2][:, b * P:(b + 1) * P], v,
                                   start=(b == 0), stop=(b == nb - 1))
                mm.then_inc(s["pv_done"], 1)

            with pe.Fori(0, NH // 2) as it:
                fqk(it, 0)
                for k in range(NS):
                    u, i = STEPS[k]
                    if k + 1 < NS:
                        fqk(it, k + 1)
                    if i in SG_AT:
                        stage(it * 2 + (u + 2), None, it * 6 + 3 * (u + 1), SG_AT[i])
                    ftrans(it, k)
                    if k >= 1:
                        fpv(it, k - 1)
                fpv(it, NS - 1)

            pe.wait_ge(s["o_done"], 4 * NS + 1)
            pe.wait_ge(s["evac_v"], EVAC_V)
            pe.wait_ge(s["evac_s"], EVAC_S)
            for gi, (a, b) in enumerate([(0, 4), (4, 8), (8, 10)]):
                for m in range(a, b):
                    src = swa_t[:, m, NH * DH:NH * DH + 2 * DH] if m < NT else skv[:, 0:2 * DH]
                    mm = pe.transpose(bank[3 + gi][:, (m - a) * P:(m - a + 1) * P], src, ident)
                mm.then_inc(s["s_kT"], 1)

            def s_stage(g1_, c3, gi, bk=7):
                a, b = SSG[gi]
                if gi == 0:
                    pe.wait_ge(s["s_staged"], g1_)
                if bk == 7:
                    pe.wait_ge(s["s_qT_cp"], c3 + gi)
                for m in range(a, b):
                    mm = pe.transpose(bank[bk][:, (m - a) * P:(m - a + 1) * P], sqst[:, m, :], ident)
                mm.then_inc(s["s_qT_T"], 1)

            for gi in range(3):
                s_stage(1, 0, gi, gi)
            pe.wait_ge(s["s_kcp"], 3)
            pe.wait_ge(s["s_aug"], 3)

            def sqk(it, k):
                u, i = STEPS[k]
                if i == 0:
                    pe.wait_ge(s["s_qT_cp"], it * 6 + 3 * (u + 1))
                if k >= 3:
                    pe.wait_ge(s["s_exp"], it * NS * 2 + 2 * (k - 2))
                for v in range(2):
                    for b in range(1 if i == 0 else 0, 2):
                        m = skeytile(i, b)
                        pe.matmul(bank[k % 3][:, v * 256 + b * P:v * 256 + (b + 1) * P], sqT[u][:, i * P:(i + 1) * P],
                                  skT[v][:, m * P:(m + 1) * P], start=(v == 0 and b == (1 if i == 0 else 0)), stop=False,
                                  skip_group_check=True)
                lo = P if i == 0 else 0
                bias = alibi[:, ds(it * 4 * 256 + u * 2 * 256, 512)].rearrange("p (v n) -> p v n", v=2)[:, :, lo:256]
                pe.matmul(bank[k % 3].rearrange("p (v n) -> p v n", v=2)[:, :, lo:256], identb, bias,
                          start=False, stop=True, skip_group_check=True).then_inc(s["s_qk"], 1)

            def strans(it, k):
                u, i = STEPS[k]
                pe.wait_ge(s["s_exp"], it * NS * 2 + 2 * (k + 1))
                if k >= 2:
                    pe.wait_ge(s["s_cps"] if k % 2 else s["s_cpv"], it * (NS // 2) + k // 2)
                n = 0
                for v in range(2):
                    for b in range(1 if i == 0 else 0, 2):
                        mm = pe.transpose(bank[4 + k % 2][:, n * P:(n + 1) * P], sprob[k % 2][:, v, b * P:(b + 1) * P], ident)
                        n += 1
                mm.then_inc(s["s_pT"], 1)

            def spv(it, k):
                u, i = STEPS[k]
                if k % 2 == 0:
                    pe.wait_ge(s["s_cpv"], it * (NS // 2) + (k // 2 + 1))
                else:
                    pe.wait_ge(s["s_cps"], it * (NS // 2) + (k // 2 + 1))
                pe.wait_ge(s["s_od"], it * NS + (k + 1))
                n = 0
                for v in range(2):
                    for b in range(1 if i == 0 else 0, 2):
                        m = skeytile(i, b)
                        val = swa_t[:, m, NH * DH + (2 + v) * DH:NH * DH + (3 + v) * DH] if m < NT else skv[:, (2 + v) * DH:(3 + v) * DH]
                        mm = pe.matmul(bank[6][:, (k % 2) * P + v * DH:(k % 2) * P + (v + 1) * DH],
                                       sprobT[k % 2][:, n * P:(n + 1) * P], val,
                                       start=(b == (1 if i == 0 else 0)), stop=(b == 1))
                        n += 1
                mm.then_inc(s["s_pv"], 1)

            with pe.Fori(0, 2) as it:
                sqk(it, 0)
                sqk(it, 1)
                for k in range(NS):
                    u, i = STEPS[k]
                    if k + 2 < NS:
                        sqk(it, k + 2)
                    if i in SSG_AT:
                        s_stage(it * 2 + (u + 2), it * 6 + 3 * (u + 1), SSG_AT[i])
                    strans(it, k)
                    if k >= 1:
                        spv(it, k - 1)
                spv(it, NS - 1)

            def transpose_o(i, u):
                pe.wait_ge(s["on_done"], i * 2 + 2)
                if not isinstance(i, int) or i >= 3:
                    pe.wait_ge(s["hT_copied"], i * 2 - 4)
                elif i > 0:
                    pe.wait_ge(s["oTl_done"], i * 2)
                for c in range(C):
                    mm = pe.transpose(bank[c // 4][:, (c % 4) * P:(c % 4) * P + P], on[u][:, c * P:(c + 1) * P], ident)
                    if c % 4 == 3:
                        mm.then_inc(s["oT_done"], 1)

            def out_proj(i, u, between=None):
                pe.wait_ge(s["oTl_done"], i * 2 + 2)
                if not (isinstance(i, int) and i < 2):
                    pe.wait_ge(s["x2_done"], i * 2 - 2)
                for n in range(2):
                    mm = three_passes(bank[2 + 2 * u + n], (lambda c: oTh[u][:, c, :], lambda c: oTl[u][:, c, :]),
                                      (lambda c: w_out_h[:, c, 512 * n:512 * n + 512], lambda c: w_out_l[:, c, 512 * n:512 * n + 512]))
                    if n == 0 and between:
                        between()
                mm.then_inc(s["om_done"], 1)

            def transpose_h(i, u, last):
                pe.wait_ge(s["h_done"], i + 1)
                pe.wait_ge(s["oTl_done"], last * 2 + 2)
                if not (isinstance(i, int) and i < 1):
                    pe.wait_ge(s["hT_copied"], i * 2)
                src = hh[u].rearrange("p (k c) -> p c k", c=C)
                for c in range(C):
                    mm = pe.transpose(bank[c // 4][:, (c % 4) * P:(c % 4) * P + P], src[:, c, :], ident)
                    if c % 4 == 3:
                        mm.then_inc(s["hT_done"], 1)

            def router(i, u):
                pe.wait_ge(s["hT_copied"], i * 2 + 2)
                for c in range(C):
                    mm = pe.matmul(bank[6][:, ds(i * (GRP + NE), GRP + NE)], hhT[u][:, c, :], wr_t[:, c, :],
                                   start=(c == 0), stop=(c == C - 1))
                mm.then_inc(s["r_done"], 1)

            def ostep(i, u, more=True):
                if not (isinstance(i, int) and i == NT - 1):
                    out_proj(i + 1, 1 - u)
                transpose_h(i, u, i + 2 if more else NT - 1)
                if not (isinstance(i, int) and i == 0):
                    router(i - 1, 1 - u)
                if more:
                    transpose_o(i + 3, 1 - u)

            pe.wait_ge(s["s_od"], 2 * NS + 1)
            transpose_o(0, 0)
            pe.wait_ge(s["wo_lo_set"], C)
            out_proj(0, 0, lambda: transpose_o(1, 1))
            transpose_o(2, 0)
            for i in (0, 1):
                ostep(i, i)
            with pe.Fori(1, 3) as j:
                for u in range(2):
                    ostep(j * 2 + u, u)
            for i in (6, 7, 8):
                ostep(i, i % 2, False)
            router(8, 0)

            pe.wait_ge(s["r_mask"], 1)
            pe.matmul(bank[0][:, 0:NT * NE], before, maskb[:, :], start=True, stop=False)
            pe.matmul(bank[0][:, 0:NT * NE], onesb, runb[:, :], start=False, stop=True).then_inc(s["r_mm"], 1)
            pe.matmul(bank[1][:, 0:NE], onesb, runb[:, (NT - 1) * NE:NT * NE], start=True, stop=False)
            pe.matmul(bank[1][:, 0:NE], onesb, maskb[:, (NT - 1) * NE:NT * NE], start=False, stop=True).then_inc(s["r_mm"], 1)

            def transpose_g(u, sig):
                src = hg[u].rearrange("p (k c) -> p c k", c=C)
                for c in range(C):
                    mm = pe.transpose(bank[c // 4][:, (c % 4) * P:(c % 4) * P + P], src[:, c, :], ident)
                    if c % 4 == 3:
                        mm.then_inc(sig, 1)

            def gate_up(u, w, sig):
                wv = w[:, 0:2 * D].rearrange("p (m c f) -> p c m f", m=2, c=C)
                for c in range(C):
                    mm = pe.matmul(bank[2 + u][:, 0:2 * FE].rearrange("p (m f) -> p m f", m=2), hgT[u][:, c, :], wv[:, c, :, :],
                                   start=(c == 0), stop=(c == C - 1))
                mm.then_inc(sig, 1)

            def down(u, w, sig):
                for n in range(2):
                    mm = pe.matmul(bank[4 + n], ex["hidT"][u], w[:, 2 * D + 512 * n:2 * D + 512 * n + 512], start=True, stop=True)
                mm.then_inc(sig, 1)

            def tg(tt, j, k):
                pe.wait_ge(g_in[k], j * 16 + 16)
                if not (isinstance(tt, int) and tt < 1):
                    pe.wait_ge(s["gT_cs"], tt)
                    pe.wait_ge(s["gT_cv"], tt)
                transpose_g(k, s["gT_done"])

            def gu(tt, j, k):
                u = k % 2
                pe.wait_ge(w_in_slot[k], j * 48 + 48)
                pe.wait_ge(s["gT_cs"], tt + 1)
                pe.wait_ge(s["gT_cv"], tt + 1)
                if not (isinstance(tt, int) and tt < 2):
                    pe.wait_ge(s["hid_done"], tt - 1)
                gate_up(u, wslot[k], s["gu_done"])

            def hd(tt, k):
                u = k % 2
                pe.wait_ge(s["hid_done"], tt + 1)
                if not (isinstance(tt, int) and tt < 1):
                    pe.wait_ge(s["hidT_cp"], tt)
                pe.transpose(bank[6][:, 0:P], ex["hid"][u], ident).then_inc(s["hidT_done"], 1)

            def dn(tt, k):
                pe.wait_ge(s["hidT_cp"], tt + 1)
                if not (isinstance(tt, int) and tt < 1):
                    pe.wait_ge(s["y_cs"], tt)
                    pe.wait_ge(s["y_cv"], tt)
                down(k % 2, wslot[k], s["dn_done"])

            def estep(tt, j, k, last=2):
                if last >= 1:
                    gu(tt + 1, j + (k + 1) // NSLOT, (k + 1) % NSLOT)
                hd(tt, k)
                if last >= 2:
                    tg(tt + 2, j * 2 + (k + 2) // 4, (k + 2) % 4)
                dn(tt, k)

            pe.wait_ge(s["r_mask"], 4)
            tg(0, 0, 0)
            tg(1, 0, 1)
            gu(0, 0, 0)
            for tt in range(NSLOT):
                estep(tt, 0, tt)
            with pe.Fori(1, NE // NSLOT - 1) as j:
                for k in range(NSLOT):
                    estep(j * NSLOT + k, j, k)
            for tt in range(NE - NSLOT, NE):
                estep(tt, tt // NSLOT, tt % NSLOT, min(2, NE - 1 - tt))

            pe.sem_inc(s["v_dn"], 1)
            n_over = pe.value_load(over[0:1, 0:1], min_val=0, max_val=NOVER)
            with pe.If(n_over > 0):
                with pe.Fori(0, NOVER) as k:
                    with pe.If(k < n_over):
                        pe.wait_ge(s["v_g"], k * 16 + 16)
                        transpose_g(0, s["v_gT"])
                        pe.wait_ge(s["v_gTc"], k * 2 + 2)
                        pe.wait_ge(s["v_w"], k * 48 + 48)
                        gate_up(0, wslot[0], s["v_gu"])
                        pe.wait_ge(s["v_hid"], k + 1)
                        pe.transpose(bank[6][:, 0:P], ex["hid"][0], ident).then_inc(s["v_hT"], 1)
                        pe.wait_ge(s["v_hTc"], k + 1)
                        down(0, wslot[0], s["v_dn"])
            pe.wait_ge(s["experts_done"], 1)


_INS = ['x_prompt', 'x_sample', 'cache_fox_k', 'cache_fox_v', 'cache_fox_logf', 'cache_swa_k', 'cache_swa_v',
        'g_mix_norm', 'w_in', 'b_forget', 'swa_sinks', 'g_fox_out', 'g_swa_out', 'w_out', 'g_ffn_norm',
        'w_router_group', 'b_router_group', 'w_router_expert', 'b_router_expert', 'w_gate', 'w_up', 'w_down', 'g_final']
_OUTS = [('y_prompt', (1, SEQ, D)), ('y_sample', (1, DEC, D)),
         ('fox_k_prompt', (1, 1, SEQ, NH, DH)), ('fox_v_prompt', (1, 1, SEQ, NH, DH)), ('fox_logf_prompt', (1, 1, SEQ, NH)),
         ('swa_k_prompt', (1, 1, WIN, 2, DH)), ('swa_v_prompt', (1, 1, WIN, 2, DH)),
         ('fox_k_sample', (1, 1, DEC, NH, DH)), ('fox_v_sample', (1, 1, DEC, NH, DH)), ('fox_logf_sample', (1, 1, DEC, NH)),
         ('swa_k_sample', (1, 1, DEC, 2, DH)), ('swa_v_sample', (1, 1, DEC, 2, DH))]


def constants():
    r = np.arange(P)
    const_f = np.concatenate([np.eye(P), r[:, None] <= r[None, :], np.ones((P, P))], axis=1).astype(np.float32)
    causal = np.where(r[None, :] <= r[:, None], 0.0, -BIG)
    k = np.arange(2 * P)
    dist = np.abs(r[:, None] + P - k[None, :])
    behind = r[:, None] // 64 + 2 - k[None, :] // 64
    seen = (behind >= 0) & (behind <= 2)
    slope = 2.0 ** -(np.arange(NH) + 1.0)
    bias = np.where(seen[:, None, :], -slope[None, :, None] * dist[:, None, :], -BIG)
    bias = bias.reshape(P, 2, 4, 2 * P).transpose(0, 2, 1, 3).reshape(P, 2 * NH * P)
    const_b = np.concatenate([np.eye(P), causal, r[:, None] < r[None, :], np.ones((P, P)), bias], axis=1).astype(mybir.dt.np(BF16))
    tok = np.arange(NT)[None, :, None] * P + r[:, None, None]
    const_i = np.stack([np.broadcast_to(tok, (P, NT, 2)), tok + TOK * np.arange(2)[None, None, :]], axis=-1)
    const_i = const_i.reshape(P, NT * 4).astype(np.int32)
    exists = (np.arange(NT)[None, :] * P + r[:, None]) < SEQ + DEC
    const_r = np.concatenate([np.broadcast_to(np.arange(NE), (P, NE)), exists], axis=1).astype(np.float32)
    return {"const_f": const_f, "const_b": const_b, "const_i": const_i, "const_r": const_r}


def kernel(**inputs):
    import concourse.bacc as _bacc
    from concourse.bass_utils import run_bass_kernel_spmd as _run

    nc = _bacc.Bacc("TRN2", target_bir_lowering=False, num_devices=1)
    arrays, t = {}, {}
    for name, a in [(n, inputs[n]) for n in _INS] + list(constants().items()):
        a = np.ascontiguousarray(a)
        arrays[f"in_{name}"] = a
        t[name] = nc.dram_tensor(f"in_{name}", a.shape, mybir.dt.from_np(a.dtype), kind="ExternalInput").ap()
    for name, shape in _OUTS:
        t[name] = nc.dram_tensor(f"out_{name}", shape, F32, kind="ExternalOutput").ap()
    build(nc, t)
    r = _run(nc, [arrays], core_ids=[0])
    return tuple(r.results[0][f"out_{name}"] for name, _ in _OUTS)
```
